# Optimizing a Trainium2 kernel written in Bass

```python
import math
import jax
import jax.numpy as jnp
from jax import lax
import numpy as np

D_MODEL = 1024
BATCH = 1
SEQ = 512
DEPTH = 1

CHUNK = 64
EPS = 1e-6
NEG_INF = -1e30

A_HEADS = 8
A_HEAD_DIM = 64
A_WIDTH = A_HEADS * A_HEAD_DIM
A_LEFT_CHUNKS = 8
A_BAND = A_LEFT_CHUNKS + 1
REL_CLIP = 128

B_HEADS = 8
B_HEAD_DIM = 128
B_WIDTH = B_HEADS * B_HEAD_DIM
CONV_WIDTH = 4
DT_MIN = 0.001
DT_MAX = 0.1

N_BRANCHES = 2

IN_SPLITS = (A_WIDTH, A_WIDTH, A_WIDTH, 3 * B_WIDTH, B_HEADS, B_HEADS, B_WIDTH, N_BRANCHES * D_MODEL)
IN_WIDTH = sum(IN_SPLITS)
IN_OFFSETS = tuple(int(o) for o in np.cumsum(IN_SPLITS)[:-1])

PEER_HEADS = 8
PEER_QDIM = 256
PEER_HALF = PEER_QDIM // 2
PEER_NKEYS = 128
PEER_N_EXPERTS = PEER_NKEYS * PEER_NKEYS
PEER_TOPK = 16
PEER_BLOCK = 128

kernel_name = 'hybrid_chunkattn_gdn_peer_block'

def rms_norm(x, w):
    xf = x.astype(jnp.float32)
    y = xf * lax.rsqrt(jnp.mean(xf * xf, axis=-1, keepdims=True) + EPS)
    return (y * w.astype(jnp.float32)).astype(x.dtype)

def l2_normalize(t):
    return t * lax.rsqrt(jnp.sum(t * t, axis=-1, keepdims=True) + EPS)

def chunk_band_attention(q, k, v, q_norm_w, k_norm_w, rel_bias):
    b, s, _ = q.shape
    n = s // CHUNK
    shp = (b, n, CHUNK, A_HEADS, A_HEAD_DIM)
    q = rms_norm(q.reshape(shp), q_norm_w)
    k = rms_norm(k.reshape(shp), k_norm_w)
    v = v.reshape(shp)
    pad = ((0, 0), (A_LEFT_CHUNKS, 0), (0, 0), (0, 0), (0, 0))
    band = jnp.arange(n)[:, None] + jnp.arange(A_BAND)[None, :]
    kb = jnp.pad(k, pad)[:, band].reshape(b, n, A_BAND * CHUNK, A_HEADS, A_HEAD_DIM)
    vb = jnp.pad(v, pad)[:, band].reshape(b, n, A_BAND * CHUNK, A_HEADS, A_HEAD_DIM)
    scores = jnp.einsum('bnihd,bnjhd->bnhij', q, kb).astype(jnp.float32) * (A_HEAD_DIM ** -0.5)
    qpos = A_LEFT_CHUNKS * CHUNK + jnp.arange(CHUNK)
    kpos = jnp.arange(A_BAND * CHUNK)
    rel = jnp.clip(qpos[:, None] - kpos[None, :], -REL_CLIP, REL_CLIP) + REL_CLIP
    bias = rel_bias.astype(jnp.float32)[:, rel]
    valid = jnp.repeat(band >= A_LEFT_CHUNKS, CHUNK, axis=1)
    scores = jnp.where(valid[None, :, None, None, :], scores + bias[None, None], NEG_INF)
    probs = jax.nn.softmax(scores, axis=-1).astype(v.dtype)
    out = jnp.einsum('bnhij,bnjhd->bnihd', probs, vb)
    return out.reshape(b, s, A_WIDTH)

def causal_short_conv(x, w):
    s = x.shape[1]
    xp = jnp.pad(x, ((0, 0), (CONV_WIDTH - 1, 0), (0, 0)))
    return sum(xp[:, i:i + s] * w[i] for i in range(CONV_WIDTH))

def chunk_gated_delta_rule(q, k, v, g, beta):
    c = q.shape[3]
    tri_incl = jnp.tril(jnp.ones((c, c), dtype=bool))
    tri_strict = jnp.tril(jnp.ones((c, c), dtype=bool), -1)
    eye = jnp.eye(c, dtype=jnp.float32)
    g_cum = jnp.cumsum(g, axis=-1)
    decay = jnp.exp(jnp.where(tri_incl, g_cum[..., :, None] - g_cum[..., None, :], -jnp.inf))
    k_beta = k * beta[..., None]
    v_beta = v * beta[..., None]
    a_mat = jnp.where(tri_strict, jnp.einsum('bhnid,bhnjd->bhnij', k_beta, k) * decay, 0.0)
    t_mat = lax.linalg.triangular_solve(eye + a_mat, jnp.broadcast_to(eye, a_mat.shape),
                                        left_side=True, lower=True)
    u = jnp.einsum('bhnij,bhnje->bhnie', t_mat, v_beta)
    w = jnp.einsum('bhnij,bhnjd->bhnid', t_mat, k_beta * jnp.exp(g_cum)[..., None])
    attn_intra = jnp.where(tri_incl, jnp.einsum('bhnid,bhnjd->bhnij', q, k) * decay, 0.0)
    g_last = g_cum[..., -1]
    k_dec = k * jnp.exp(g_last[..., None] - g_cum)[..., None]
    q_dec = q * jnp.exp(g_cum)[..., None]

    def step(state, inp):
        qd, kd, w_c, u_c, attn_c, gl = inp
        v_new = u_c - jnp.einsum('bhcd,bhde->bhce', w_c, state)
        o = jnp.einsum('bhcd,bhde->bhce', qd, state) + jnp.einsum('bhij,bhje->bhie', attn_c, v_new)
        state = state * jnp.exp(gl)[..., None, None] + jnp.einsum('bhcd,bhce->bhde', kd, v_new)
        return state, o

    xs = tuple(jnp.moveaxis(t, 2, 0) for t in (q_dec, k_dec, w, u, attn_intra, g_last))
    b, h = q.shape[0], q.shape[1]
    s0 = jnp.zeros((b, h, q.shape[-1], v.shape[-1]), jnp.float32)
    _, o = lax.scan(step, s0, xs)
    return jnp.moveaxis(o, 0, 2)

def gated_deltanet(qkv_raw, a_raw, beta_raw, gate_raw, conv_w, a_log, dt_bias, norm_w):
    b, s, _ = qkv_raw.shape
    n = s // CHUNK
    f32 = jnp.float32
    qkv = jax.nn.silu(causal_short_conv(qkv_raw, conv_w)).astype(f32)
    q, k, v = jnp.split(qkv, 3, axis=-1)

    def to_chunks(t):
        return t.reshape(b, n, CHUNK, B_HEADS, B_HEAD_DIM).transpose(0, 3, 1, 2, 4)

    def heads_to_chunks(t):
        return t.reshape(b, n, CHUNK, B_HEADS).transpose(0, 3, 1, 2)

    q = l2_normalize(to_chunks(q)) * (B_HEAD_DIM ** -0.5)
    k = l2_normalize(to_chunks(k))
    v = to_chunks(v)
    beta = heads_to_chunks(jax.nn.sigmoid(beta_raw.astype(f32)))
    g = heads_to_chunks(-jnp.exp(a_log.astype(f32)) * jax.nn.softplus(a_raw.astype(f32) + dt_bias.astype(f32)))
    o = chunk_gated_delta_rule(q, k, v, g, beta)
    o = o.transpose(0, 2, 3, 1, 4).reshape(b, s, B_HEADS, B_HEAD_DIM)
    o = rms_norm(o, norm_w) * jax.nn.silu(gate_raw.astype(f32).reshape(b, s, B_HEADS, B_HEAD_DIM))
    return o.reshape(b, s, B_WIDTH).astype(qkv_raw.dtype)

def peer_ffn(h, w_query, keys_1, keys_2, expert_down, expert_up):
    b, s, d = h.shape
    hb = h.reshape((b * s) // PEER_BLOCK, PEER_BLOCK, d)

    def block(xt):
        q = (xt @ w_query).reshape(PEER_BLOCK, PEER_HEADS, PEER_QDIM)
        s1 = jnp.einsum('phd,hkd->phk', q[..., :PEER_HALF], keys_1).astype(jnp.float32)
        s2 = jnp.einsum('phd,hkd->phk', q[..., PEER_HALF:], keys_2).astype(jnp.float32)
        v1, i1 = lax.top_k(s1, PEER_TOPK)
        v2, i2 = lax.top_k(s2, PEER_TOPK)
        cand = (v1[..., :, None] + v2[..., None, :]).reshape(PEER_BLOCK, PEER_HEADS, PEER_TOPK * PEER_TOPK)
        cand_idx = (i1[..., :, None] * PEER_NKEYS + i2[..., None, :]).reshape(PEER_BLOCK, PEER_HEADS, PEER_TOPK * PEER_TOPK)
        top_s, pos = lax.top_k(cand, PEER_TOPK)
        expert_idx = jnp.take_along_axis(cand_idx, pos, axis=-1)
        gate = jax.nn.softmax(top_s, axis=-1)
        u = expert_down[expert_idx]
        act = jax.nn.gelu(jnp.einsum('pd,phkd->phk', xt, u).astype(jnp.float32), approximate=False)
        vv = expert_up[expert_idx]
        return jnp.einsum('phk,phkd->pd', (gate * act).astype(xt.dtype), vv)

    return lax.map(block, hb).reshape(b, s, d)

def hybrid_layer(x, norm_mix_w, w_in, a_q_norm_w, a_k_norm_w, a_rel_bias, b_conv_w, b_a_log,
                 b_dt_bias, b_norm_w, b_merge, w_proj_a, w_proj_b, w_out, norm_ffn_w,
                 peer_w_query, peer_keys_1, peer_keys_2, peer_down, peer_up):
    b, s, _ = x.shape
    h = rms_norm(x, norm_mix_w)
    z = h @ w_in
    qa, ka, va, qkv_b, a_b, beta_b, gate_b, merge_raw = jnp.split(z, IN_OFFSETS, axis=-1)
    o_a = chunk_band_attention(qa, ka, va, a_q_norm_w, a_k_norm_w, a_rel_bias)
    o_b = gated_deltanet(qkv_b, a_b, beta_b, gate_b, b_conv_w, b_a_log, b_dt_bias, b_norm_w)
    gates = jax.nn.sigmoid(merge_raw.astype(jnp.float32) + b_merge.astype(jnp.float32))
    gates = gates.reshape(b, s, N_BRANCHES, D_MODEL).astype(x.dtype)
    mixed = gates[..., 0, :] * (o_a @ w_proj_a) + gates[..., 1, :] * (o_b @ w_proj_b)
    x = x + mixed @ w_out
    x = x + peer_ffn(rms_norm(x, norm_ffn_w), peer_w_query, peer_keys_1, peer_keys_2, peer_down, peer_up)
    return x

def setup_inputs(seed: int = 0) -> dict:
    key = jax.random.key(seed)
    ks = jax.random.split(key, 20)
    f32 = jnp.float32
    L = DEPTH

    def nrm(k, shape, scale):
        return jax.random.normal(k, shape, f32) * scale

    def gain(k, n):
        return 1.0 + 0.02 * jax.random.normal(k, (L, n), f32)

    dt = jnp.exp(jax.random.uniform(ks[7], (L, B_HEADS), f32, math.log(DT_MIN), math.log(DT_MAX)))
    return {
        'x': nrm(ks[0], (BATCH, SEQ, D_MODEL), 1.0),
        'norm_mix_w': gain(ks[1], D_MODEL),
        'w_in': nrm(ks[2], (L, D_MODEL, IN_WIDTH), D_MODEL ** -0.5),
        'a_q_norm_w': gain(ks[3], A_HEAD_DIM),
        'a_k_norm_w': gain(ks[4], A_HEAD_DIM),
        'a_rel_bias': nrm(ks[5], (L, A_HEADS, 2 * REL_CLIP + 1), 0.5),
        'b_conv_w': nrm(ks[6], (L, CONV_WIDTH, 3 * B_WIDTH), CONV_WIDTH ** -0.5),
        'b_a_log': jnp.log(jax.random.uniform(ks[8], (L, B_HEADS), f32, 1.0, 16.0)),
        'b_dt_bias': dt + jnp.log(-jnp.expm1(-dt)),
        'b_norm_w': gain(ks[9], B_HEAD_DIM),
        'b_merge': nrm(ks[10], (L, N_BRANCHES * D_MODEL), 0.02),
        'w_proj_a': nrm(ks[11], (L, A_WIDTH, D_MODEL), A_WIDTH ** -0.5),
        'w_proj_b': nrm(ks[12], (L, B_WIDTH, D_MODEL), B_WIDTH ** -0.5),
        'w_out': nrm(ks[13], (L, D_MODEL, D_MODEL), D_MODEL ** -0.5),
        'norm_ffn_w': gain(ks[14], D_MODEL),
        'peer_w_query': nrm(ks[15], (L, D_MODEL, PEER_HEADS * PEER_QDIM), D_MODEL ** -0.5),
        'peer_keys_1': nrm(ks[16], (L, PEER_HEADS, PEER_NKEYS, PEER_HALF), PEER_HALF ** -0.5),
        'peer_keys_2': nrm(ks[17], (L, PEER_HEADS, PEER_NKEYS, PEER_HALF), PEER_HALF ** -0.5),
        'peer_down': nrm(ks[18], (L, PEER_N_EXPERTS, D_MODEL), D_MODEL ** -0.5),
        'peer_up': nrm(ks[19], (L, PEER_N_EXPERTS, D_MODEL), PEER_HEADS ** -0.5),
    }

def reference(x, norm_mix_w, w_in, a_q_norm_w, a_k_norm_w, a_rel_bias, b_conv_w, b_a_log,
              b_dt_bias, b_norm_w, b_merge, w_proj_a, w_proj_b, w_out, norm_ffn_w,
              peer_w_query, peer_keys_1, peer_keys_2, peer_down, peer_up):
    for l in range(DEPTH):
        x = hybrid_layer(x, norm_mix_w[l], w_in[l], a_q_norm_w[l], a_k_norm_w[l], a_rel_bias[l],
                         b_conv_w[l], b_a_log[l], b_dt_bias[l], b_norm_w[l], b_merge[l],
                         w_proj_a[l], w_proj_b[l], w_out[l], norm_ffn_w[l], peer_w_query[l],
                         peer_keys_1[l], peer_keys_2[l], peer_down[l], peer_up[l])
    return x


_drawn_inputs = setup_inputs


def setup_inputs(seed=0):
    import zlib

    import numpy as np

    out = dict(_drawn_inputs(seed))
    spreads = {}
    factors = {'a_q_norm_w': 8.0,
     'a_k_norm_w': 8.0,
     'b_norm_w': 3.365,
     'b_merge': 6.035,
     'a_rel_bias': 2.746,
     'norm_ffn_w': 3.394}
    for name, (base, spread) in spreads.items():
        noise = np.random.default_rng([zlib.crc32(name.encode()), seed]).standard_normal(out[name].shape)
        drawn = base * np.exp(spread * noise) if base else spread * noise
        out[name] = jnp.asarray(drawn.astype(out[name].dtype))
    for name, factor in factors.items():
        out[name] = (out[name] * factor).astype(out[name].dtype)
    return out
```

```python
from contextlib import ExitStack

import concourse.bass as bass
from concourse import mybir

P = 128
D = 1024
TOK = 512
KD = D // P
NT = TOK // P
CH = 64
NCH = TOK // CH
EPS = 1e-6
HEADS = 8
HD = 128
LEVELS = 6
CONV = 4
NEG = -1e30

F32 = mybir.dt.float32
F32R = mybir.dt.float32r
U32 = mybir.dt.uint32
ALU = mybir.AluOpType
ACT = mybir.ActivationFunctionType
AX = mybir.AxisListType


class Steps:

    def __init__(self, sem, names):
        self.sem = sem
        self.per = len(names)
        self.place = {name: n + 1 for n, name in enumerate(names)}
        assert len(self.place) == self.per

    def open(self, engine):
        engine.sem_inc(self.sem, self.per)

    def after(self, name, turn=0):
        return (turn + 1) * self.per + self.place[name]


class Items:

    def __init__(self, sem, ahead):
        self.sem, self.ahead = sem, ahead

    def open(self, engine):
        engine.sem_inc(self.sem, self.ahead)

    def after(self, n):
        return n + 1 + self.ahead


def three_passes(pe, out, w_hi, w_lo, x_hi, x_lo, first, last):
    pe.matmul(out, w_hi, x_lo, start=first, stop=False)
    pe.matmul(out, w_lo, x_hi, start=False, stop=False)
    return pe.matmul(out, w_hi, x_hi, start=False, stop=last)


class Weights:

    def __init__(self, ctx, nc, tag, dram, pieces, used, names):
        self.dram, self.pieces, self.used, self.names = dram, pieces, used, names
        self.starts = [sum(pieces[:m]) for m in range(len(pieces))]
        self.n = len(pieces)
        shape = [P, sum(pieces), P]
        self.raw = ctx.enter_context(nc.sbuf_tensor(f"{tag}_w_raw", shape, F32))
        self.hi = ctx.enter_context(nc.sbuf_tensor(f"{tag}_w_hi", shape, F32R))
        self.lo = ctx.enter_context(nc.sbuf_tensor(f"{tag}_w_lo", shape, F32R))
        sem = lambda name: ctx.enter_context(nc.semaphore(f"{tag}_{name}"))
        self.raw_in = [sem(f"w_raw_in{m}") for m in range(self.n)]
        self.hi_made = Steps(sem("w_hi_made"), range(self.n))
        self.lo_made = Steps(sem("w_lo_made"), range(self.n))

    def part(self, tensor, m):
        return tensor[:, self.starts[m]:self.starts[m] + self.pieces[m], :]

    def load(self, sp, i):
        for m in range(self.n):
            sp.wait_ge(self.lo_made.sem, self.lo_made.after(m, i - 1))
            src = self.dram[bass.ds(i, 1), :, self.starts[m]:self.starts[m] + self.pieces[m], :]
            sp.dma_start(self.part(self.raw, m), src.rearrange("a p k c -> (a p) k c")).then_inc(self.raw_in[m], 16)

    def high(self, act, i):
        for m in range(self.n):
            act.wait_ge(self.raw_in[m], 16 * (i + 1))
            act.wait_ge(self.used.sem, self.used.after(self.names[m], i - 1))
            act.copy(self.part(self.hi, m), self.part(self.raw, m)).then_inc(self.hi_made.sem, 1)

    def low(self, pool, i):
        for m in range(self.n):
            pool.wait_ge(self.hi_made.sem, self.hi_made.after(m, i))
            pool.tensor_tensor(self.part(self.lo, m), self.part(self.raw, m), self.part(self.hi, m).bitcast(F32),
                               ALU.subtract).then_inc(self.lo_made.sem, 1)

    def product(self, pe, i, m, out, x_hi, x_lo):
        pe.wait_ge(self.lo_made.sem, self.lo_made.after(m, i))
        for k in range(self.pieces[m]):
            at = self.starts[m] + k
            ins = three_passes(pe, out, self.hi[:, at, :], self.lo[:, at, :], x_hi[:, k, :], x_lo[:, k, :],
                               k == 0, k == self.pieces[m] - 1)
        return ins


def norm_and_split(nc, tag, x, gain_dram, ones, h_full, h_hi, h_lo, load=None):
    with ExitStack() as ctx:
        def sb(name, shape, dt=F32):
            return ctx.enter_context(nc.sbuf_tensor(f"{tag}_{name}", shape, dt))

        def sem(name):
            return ctx.enter_context(nc.semaphore(f"{tag}_{name}"))

        sq = sb("sq", [P, KD, TOK])
        var = sb("var", [P, TOK])
        gain = sb("gain", [P, KD])
        sums = ctx.enter_context(nc.psum_tensor(f"{tag}_sums", [P, TOK], F32))
        loaded = sem("loaded")
        n_loads = 1 + len(load or [])
        squared = sem("squared")
        summed = sem("summed")
        biased = sem("biased")
        rooted = sem("rooted")
        inverted = sem("inverted")
        scaled = sem("scaled")
        high = sem("high")
        low = sem("low")
        block = ctx.enter_context(nc.Block())

        @block.sync
        def _(sp):
            for dst, src in load or []:
                sp.dma_start(dst, src).then_inc(loaded, 16)
            sp.dma_start(gain[:], gain_dram).then_inc(loaded, 16)

        @block.scalar
        def _(act):
            act.wait_ge(loaded, 16 * n_loads)
            for k in range(KD):
                act.activation(sq[:, k, :], x[:, k, :], ACT.Square).then_inc(squared, 1)
            act.wait_ge(biased, 1)
            act.activation(var[:], var[:], ACT.Sqrt).then_inc(rooted, 1)
            for k in range(KD):
                act.wait_ge(scaled, k + 1)
                act.copy(h_hi[:, k, :], h_full[:, k, :]).then_inc(high, 1)

        @block.tensor
        def _(pe):
            for k in range(KD):
                pe.wait_ge(squared, k + 1)
                ins = pe.matmul(sums[:], ones[:], sq[:, k, :], start=(k == 0), stop=(k == KD - 1))
            ins.then_inc(summed, 1)

        @block.vector
        def _(dve):
            dve.wait_ge(loaded, 16 * n_loads)
            dve.wait_ge(summed, 1)
            dve.tensor_scalar(var[:], sums[:], 1.0 / D, EPS, ALU.mult, ALU.add).then_inc(biased, 1)
            dve.wait_ge(rooted, 1)
            dve.reciprocal(var[:], var[:]).then_inc(inverted, 1)
            dve.wait_ge(inverted, 1)
            for k in range(KD):
                dve.scalar_tensor_tensor(out=h_full[:, k, :], in0=x[:, k, :], scalar=gain[:, k:k + 1],
                                         in1=var[:], op0=ALU.mult, op1=ALU.mult).then_inc(scaled, 1)
            for k in range(KD):
                dve.wait_ge(high, k + 1)
                dve.tensor_tensor(h_lo[:, k, :], h_full[:, k, :], h_hi[:, k, :].bitcast(F32),
                                  ALU.subtract).then_inc(low, 1)


def decay_rows(nc, h_full, w_ab, dt_bias, a_log, ident8, resets, rows_dram, cols):
    with ExitStack() as ctx:
        def sb(name, shape, dt=F32):
            return ctx.enter_context(nc.sbuf_tensor(f"dr_{name}", shape, dt))

        def sem(name):
            return ctx.enter_context(nc.semaphore(f"dr_{name}"))

        wab = sb("wab", [P, KD, 2 * HEADS])
        bias = sb("bias", [HEADS, 1])
        alog = sb("alog", [HEADS, 1])
        rate = sb("rate", [HEADS, 1])
        mask = sb("mask", [HEADS, TOK])
        rows = sb("rows", [HEADS, 5, TOK])
        tmp = sb("tmp", [HEADS, 6, TOK])
        ps = ctx.enter_context(nc.psum_tensor("dr_ps", [P, 3, TOK], F32))
        loaded = sem("loaded")
        stored = sem("stored")
        dve_done = Steps(sem("dve_done"), ["x", "neg_abs", "e_plus_1", "neg_rate", "part", "rest", "inv", "corr",
                                           "log1p", "pos", "softplus", "g", "gc", "last_minus",
                                           "beta_exp", "cols"])
        act_done = Steps(sem("act_done"), ["beta", "rate", "e", "ln", "egc", "elast"])
        pe_done = Steps(sem("pe_done"), ["a", "b", "turned"])
        block = ctx.enter_context(nc.Block())
        x, ax, e, u, l, g = (tmp[:, i, :] for i in range(6))
        r, d = rows[:, 3, :], rows[:, 4, :]
        gc, beta, egc, begc, elast = (rows[:, i, :] for i in range(5))

        @block.sync
        def _(sp):
            sp.dma_start(wab[:], w_ab).then_inc(loaded, 16)
            sp.dma_start(bias[:], dt_bias).then_inc(loaded, 16)
            sp.dma_start(alog[:], a_log).then_inc(loaded, 16)
            sp.dma_start(mask[:], resets).then_inc(loaded, 16)
            sp.wait_ge(act_done.sem, act_done.after("egc"))
            sp.wait_ge(dve_done.sem, dve_done.after("gc"))
            sp.dma_start(rows_dram, rows[:, 0:3, :]).then_inc(stored, 16)
            sp.wait_ge(stored, 16)

        @block.tensor
        def _(pe):
            pe_done.open(pe)
            pe.wait_ge(loaded, 64)
            for half in range(2):
                for k in range(KD):
                    ins = pe.matmul(ps[0:HEADS, half, :], wab[:, k, HEADS * half:HEADS * half + HEADS],
                                    h_full[:, k, :], start=(k == 0), stop=(k == KD - 1))
                ins.then_inc(pe_done.sem, 1)
            pe.wait_ge(dve_done.sem, dve_done.after("beta_exp"))
            pe.wait_ge(act_done.sem, act_done.after("elast"))
            for n, row in enumerate((beta, gc, begc, elast)):
                for c in range(NCH):
                    at = (n * NCH + c) * HEADS
                    ins = pe.transpose(ps[0:CH, 2, at:at + HEADS], row[:, c * CH:c * CH + CH],
                                       ident8[0:HEADS, 0:HEADS])
            ins.then_inc(pe_done.sem, 1)

        @block.scalar
        def _(act):
            act_done.open(act)
            act.wait_ge(pe_done.sem, pe_done.after("b"))
            act.activation(beta, ps[0:HEADS, 1, :], ACT.Sigmoid).then_inc(act_done.sem, 1)
            act.wait_ge(loaded, 64)
            act.activation(rate[:], alog[:], ACT.Exp).then_inc(act_done.sem, 1)
            act.wait_ge(dve_done.sem, dve_done.after("neg_abs"))
            act.activation(e, ax, ACT.Exp).then_inc(act_done.sem, 1)
            act.wait_ge(dve_done.sem, dve_done.after("e_plus_1"))
            act.activation(l, u, ACT.Ln).then_inc(act_done.sem, 1)
            act.wait_ge(dve_done.sem, dve_done.after("gc"))
            act.activation(egc, gc, ACT.Exp).then_inc(act_done.sem, 1)
            act.wait_ge(dve_done.sem, dve_done.after("last_minus"))
            act.activation(elast, ax, ACT.Exp).then_inc(act_done.sem, 1)

        @block.vector
        def _(dve):
            def own(name):
                dve.wait_ge(dve_done.sem, dve_done.after(name))

            dve_done.open(dve)
            dve.wait_ge(loaded, 64)
            dve.wait_ge(pe_done.sem, pe_done.after("a"))
            dve.tensor_scalar(x, ps[0:HEADS, 0, :], bias[:, 0:1], None, ALU.add).then_inc(dve_done.sem, 1)
            own("x")
            dve.scalar_tensor_tensor(out=ax, in0=x, scalar=-1.0, in1=x, op0=ALU.mult,
                                     op1=ALU.min).then_inc(dve_done.sem, 1)
            dve.wait_ge(act_done.sem, act_done.after("e"))
            dve.tensor_scalar(u, e, 1.0, None, ALU.add).then_inc(dve_done.sem, 1)
            dve.tensor_scalar(rate[:], rate[:], -1.0, None, ALU.mult).then_inc(dve_done.sem, 1)
            own("e_plus_1")
            dve.tensor_scalar(d, u, -1.0, None, ALU.add).then_inc(dve_done.sem, 1)
            own("part")
            dve.tensor_tensor(d, e, d, ALU.subtract).then_inc(dve_done.sem, 1)
            dve.reciprocal(r, u).then_inc(dve_done.sem, 1)
            own("inv")
            dve.tensor_tensor(d, d, r, ALU.mult).then_inc(dve_done.sem, 1)
            own("corr")
            dve.wait_ge(act_done.sem, act_done.after("ln"))
            dve.tensor_tensor(l, l, d, ALU.add).then_inc(dve_done.sem, 1)
            dve.tensor_scalar(x, x, 0.0, None, ALU.max).then_inc(dve_done.sem, 1)
            own("pos")
            dve.tensor_tensor(g, x, l, ALU.add).then_inc(dve_done.sem, 1)
            own("softplus")
            dve.tensor_scalar(g, g, rate[:, 0:1], None, ALU.mult).then_inc(dve_done.sem, 1)
            own("g")
            dve.tensor_tensor_scan(gc, mask[:], g, 0.0, ALU.mult, ALU.add).then_inc(dve_done.sem, 1)
            own("gc")
            chunks = gc.rearrange("p (c i) -> p c i", i=CH)
            dve.tensor_tensor(ax.rearrange("p (c i) -> p c i", i=CH),
                              chunks[:, :, CH - 1:CH].to_broadcast([HEADS, NCH, CH]), chunks,
                              ALU.subtract).then_inc(dve_done.sem, 1)
            dve.wait_ge(act_done.sem, act_done.after("egc"))
            dve.tensor_tensor(begc, beta, egc, ALU.mult).then_inc(dve_done.sem, 1)
            dve.wait_ge(pe_done.sem, pe_done.after("turned"))
            dve.tensor_copy(cols[:].rearrange("p a c h -> p (a c h)"),
                            ps[0:CH, 2, 0:4 * NCH * HEADS]).then_inc(dve_done.sem, 1)


def mixer_b(nc, h_hi, h_lo, w_b, conv_dram, norm_dram, rows_dram, cols, ident, ones, masks_dram, o_b):
    with ExitStack() as ctx:
        def sb(name, shape, dt=F32):
            return ctx.enter_context(nc.sbuf_tensor(f"mb_{name}", shape, dt))

        def sem(name):
            return ctx.enter_context(nc.semaphore(f"mb_{name}"))

        conv = sb("conv", [P, HEADS, 3, CONV])
        norm = sb("norm", [P, 1])
        masks = sb("masks", [CH, LEVELS + 1, CH])
        rows = sb("rows", [P, 3, TOK])
        y = sb("y", [P, 3, TOK])
        act_y = sb("act_y", [P, 3, TOK])
        gate = sb("gate", [P, TOK])
        sq = sb("sq", [P, 2, TOK])
        var = sb("var", [P, 2, TOK])
        qT = sb("qT", [P, TOK])
        kT = sb("kT", [P, TOK])
        kbT = sb("kbT", [P, TOK])
        qdT = sb("qdT", [P, TOK])
        decay = sb("decay", [CH, NCH, CH])
        AT = sb("AT", [CH, NCH, CH])
        attnT = sb("attnT", [CH, NCH, CH])
        prod = sb("prod", [CH, NCH, CH])
        T = sb("T", [CH, NCH, CH])
        TT = sb("TT", [CH, NCH, CH])
        vb = sb("vb", [CH, NCH, HD])
        kbe = sb("kbe", [CH, NCH, HD])
        kd = sb("kd", [CH, NCH, HD])
        nwT = sb("nwT", [P, NCH, CH])
        egl = sb("egl", [P, NCH])
        vn = sb("vn", [CH, 2, HD])
        S = sb("S", [P, 2, HD])
        osq = sb("osq", [P, TOK])
        ovar = sb("ovar", [P, TOK])
        o1 = sb("o1", [P, TOK])
        ps = ctx.enter_context(nc.psum_tensor("mb_ps", [P, 8, TOK], F32))

        consts = sem("consts")
        passed = sem("passed")
        rows_in = sem("rows_in")
        pe_done = Steps(sem("pe_done"),
                        ["project_q", "project_k", "project_v", "project_g", "norm_sums", "turn_v",
                         "turn_k", "gram"]
                        + [f"{s}{l}" for l in range(LEVELS) for s in ("AxT", "TxP")]
                        + ["wT"]
                        + [f"{s}{c}" for c in range(NCH) for s in ("v_new", "state", "out")
                           if (s, c) != ("state", NCH - 1)]
                        + ["out_sums"])
        w = Weights(ctx, nc, "mb", w_b, [KD] * 4, pe_done, ["project_" + t for t in "qkvg"])
        act_done = Steps(sem("act_done"), ["silu_q", "silu_k", "silu_v", "gate", "square_q", "square_k",
                                           "root_qk", "decay", "square_o", "root_o"])
        dve_done = Steps(sem("dve_done"),
                         [f"conv{s}_{t}" for s in range(CONV) for t in "qkv"]
                         + ["diff", "diff_masked", "bias_q", "bias_k", "inv_qk", "q", "k", "kb", "qd", "egl",
                            "vb", "kbe", "kd", "attn", "A"]
                         + [f"{s}{l}" for l in range(LEVELS) for s in ("P", "T", "TT")
                            if (s, l) != ("T", LEVELS - 1)]
                         + ["nw"]
                         + [f"{s}{c}" for c in range(NCH) for s in ("vn", "S")
                            if (s, c) != ("S", NCH - 1)]
                         + ["bias_o", "inv_o", "o_normed", "o"])
        block = ctx.enter_context(nc.Block())
        ps_c = ps[:, :, :].rearrange("p b (c i) -> p b c i", i=CH)
        BETA, GC, BEGC, ELAST = range(4)

        @block.sync
        def _(sp):
            sp.dma_start(conv[:], conv_dram).then_inc(consts, 16)
            sp.dma_start(norm[:], norm_dram).then_inc(consts, 16)
            sp.dma_start(masks[:], masks_dram).then_inc(consts, 16)
            with sp.Fori(0, HEADS) as h:
                sp.wait_ge(dve_done.sem, dve_done.after("egl", h - 1))
                sp.dma_start(rows[:], rows_dram[bass.ds(h, 1), :, :].rearrange("a r t -> (a r t)")
                             .partition_broadcast(P).rearrange("p (r t) -> p r t", r=3)).then_inc(rows_in, 16)
                w.load(sp, h)

        @block.gpsimd
        def _(pool):
            w.lo_made.open(pool)
            with pool.Fori(0, HEADS) as h:
                w.low(pool, h)

        @block.scalar
        def _(act):
            w.hi_made.open(act)
            act_done.open(act)
            act.wait_ge(consts, 48)
            with act.Fori(0, HEADS) as h:
                w.high(act, h)
                for n, t in enumerate("qkv"):
                    act.wait_ge(dve_done.sem, dve_done.after(f"conv{CONV - 1}_{t}", h))
                    act.activation(act_y[:, n, :], y[:, n, :], ACT.Silu).then_inc(act_done.sem, 1)
                act.wait_ge(pe_done.sem, pe_done.after("project_g", h))
                act.activation(gate[:], ps[:, 3, :], ACT.Silu).then_inc(act_done.sem, 1)
                for n, t in enumerate("qk"):
                    act.wait_ge(act_done.sem, act_done.after(f"silu_{t}", h))
                    act.activation(sq[:, n, :], act_y[:, n, :], ACT.Square).then_inc(act_done.sem, 1)
                act.wait_ge(dve_done.sem, dve_done.after("bias_k", h))
                act.activation(var[:], var[:], ACT.Sqrt).then_inc(act_done.sem, 1)
                act.wait_ge(dve_done.sem, dve_done.after("diff_masked", h))
                act.activation(decay[:], decay[:], ACT.Exp).then_inc(act_done.sem, 1)
                act.wait_ge(pe_done.sem, pe_done.after(f"out{NCH - 1}", h))
                act.activation(osq[:], ps[:, 4, :], ACT.Square).then_inc(act_done.sem, 1)
                act.wait_ge(dve_done.sem, dve_done.after("bias_o", h))
                act.activation(ovar[:], ovar[:], ACT.Sqrt).then_inc(act_done.sem, 1)

        @block.tensor
        def _(pe):
            pe_done.open(pe)
            with pe.Fori(0, HEADS) as h:
                def dve(name):
                    pe.wait_ge(dve_done.sem, dve_done.after(name, h))
                    pe.sem_inc(passed, 1)

                for m in range(4):
                    w.product(pe, h, m, ps[:, m, :], h_hi, h_lo).then_inc(pe_done.sem, 1)
                pe.wait_ge(act_done.sem, act_done.after("square_k", h))
                pe.matmul(ps[:, 4, :], ones[:], sq[:, 0, :], start=True, stop=True)
                pe.matmul(ps[:, 5, :], ones[:], sq[:, 1, :], start=True, stop=True).then_inc(pe_done.sem, 1)
                pe.sem_inc(passed, 1)
                for c in range(NCH):
                    ins = pe.transpose(ps[0:CH, 2 + c // 4, c % 4 * HD:c % 4 * HD + HD],
                                       act_y[:, 2, c * CH:c * CH + CH], ident[:])
                ins.then_inc(pe_done.sem, 1)
                dve("k")
                for c in range(NCH):
                    ins = pe.transpose(ps[0:CH, c // 4, c % 4 * HD:c % 4 * HD + HD],
                                       kT[:, c * CH:c * CH + CH], ident[:])
                ins.then_inc(pe_done.sem, 1)
                dve("kb")
                for c in range(NCH):
                    at = slice(c * CH, c * CH + CH)
                    pe.matmul(ps_c[0:CH, 6, c, :], kT[:, at], kbT[:, at], start=True, stop=True)
                    ins = pe.matmul(ps_c[0:CH, 7, c, :], kT[:, at], qT[:, at], start=True, stop=True)
                ins.then_inc(pe_done.sem, 1)
                for l in range(LEVELS):
                    dve("A" if l == 0 else f"TT{l - 1}")
                    for c in range(NCH):
                        ins = pe.matmul(ps_c[0:CH, 4, c, :], AT[:, c, :], ident[0:CH, 0:CH] if l == 0 else T[:, c, :],
                                        start=True, stop=True)
                    ins.then_inc(pe_done.sem, 1)
                    dve(f"P{l}")
                    for c in range(NCH):
                        tt = ident[0:CH, 0:CH] if l == 0 else TT[:, c, :]
                        if l < LEVELS - 1:
                            pe.matmul(ps_c[0:CH, 5, c, :], tt, prod[:, c, :], start=True, stop=True)
                        ins = pe.matmul(ps_c[0:CH, 6, c, :], prod[:, c, :], tt, start=True, stop=True)
                    ins.then_inc(pe_done.sem, 1)
                dve(f"TT{LEVELS - 1}")
                for c in range(NCH):
                    ins = pe.matmul(ps_c[:, 7, c, :], kbe[:, c, :], TT[:, c, :], start=True, stop=True)
                ins.then_inc(pe_done.sem, 1)
                dve("nw")
                for c in range(NCH):
                    at = slice(c * CH, c * CH + CH)
                    state = S[:, c % 2, :]
                    ins = pe.matmul(ps[0:CH, c % 2, 0:HD], TT[:, c, :], vb[:, c, :], start=True, stop=(c == 0))
                    if c == 0:
                        ins.then_inc(pe_done.sem, 1)
                    else:
                        dve(f"S{c - 1}")
                        pe.matmul(ps[0:CH, c % 2, 0:HD], nwT[:, c, :], state, start=False,
                                  stop=True).then_inc(pe_done.sem, 1)
                        pe.matmul(ps[:, 4, at], state, qdT[:, at], start=True, stop=False)
                    dve(f"vn{c}")
                    if c < NCH - 1:
                        pe.matmul(ps[:, 2 + c % 2, 0:HD], kd[:, c, :], vn[:, c % 2, :], start=True,
                                  stop=True).then_inc(pe_done.sem, 1)
                    pe.matmul(ps[:, 4, at], vn[:, c % 2, :], attnT[:, c, :], start=(c == 0),
                              stop=True).then_inc(pe_done.sem, 1)
                pe.wait_ge(act_done.sem, act_done.after("square_o", h))
                pe.matmul(ps[:, 5, :], ones[:], osq[:], start=True, stop=True).then_inc(pe_done.sem, 1)

        @block.vector
        def _(dve):
            dve_done.open(dve)
            dve.wait_ge(consts, 48)
            with dve.Fori(0, HEADS) as h:
                done = dve_done.sem

                def own(name):
                    dve.wait_ge(done, dve_done.after(name, h))

                def pe(name):
                    dve.wait_ge(pe_done.sem, pe_done.after(name, h))

                def act(name):
                    dve.wait_ge(act_done.sem, act_done.after(name, h))

                def taps(n, s):
                    return conv[:, bass.ds(h, 1), n, CONV - 1 - s:CONV - s].rearrange("p a b -> p (a b)")

                for s in range(CONV):
                    for n, t in enumerate("qkv"):
                        if s == 0:
                            pe(f"project_{t}")
                            dve.tensor_scalar(y[:, n, :], ps[:, n, :], taps(n, 0), None,
                                              ALU.mult).then_inc(done, 1)
                        else:
                            own(f"conv{s - 1}_{t}")
                            dve.scalar_tensor_tensor(out=y[:, n, s:], in0=ps[:, n, :TOK - s], scalar=taps(n, s),
                                                     in1=y[:, n, s:], op0=ALU.mult,
                                                     op1=ALU.add).then_inc(done, 1)
                dve.wait_ge(rows_in, 16 * h + 16)
                head_col = lambda kind, width: cols[:, kind, :, bass.ds(h, 1)].to_broadcast([CH, NCH, width])
                dve.tensor_tensor(decay[:], rows[0:CH, 0, :].rearrange("p (c i) -> p c i", i=CH),
                                  head_col(GC, CH), ALU.subtract).then_inc(done, 1)
                own("diff")
                dve.tensor_tensor(decay[:], decay[:], masks[:, LEVELS:LEVELS + 1, :].to_broadcast([CH, NCH, CH]),
                                  ALU.add).then_inc(done, 1)
                pe("norm_sums")
                dve.tensor_scalar(var[:, 0, :], ps[:, 4, :], EPS, float(HD), ALU.add, ALU.mult).then_inc(done, 1)
                dve.tensor_scalar(var[:, 1, :], ps[:, 5, :], EPS, None, ALU.add).then_inc(done, 1)
                act("root_qk")
                dve.reciprocal(var[:], var[:]).then_inc(done, 1)
                own("inv_qk")
                dve.tensor_tensor(qT[:], act_y[:, 0, :], var[:, 0, :], ALU.mult).then_inc(done, 1)
                dve.tensor_tensor(kT[:], act_y[:, 1, :], var[:, 1, :], ALU.mult).then_inc(done, 1)
                own("k")
                dve.tensor_tensor(kbT[:], kT[:], rows[:, 1, :], ALU.mult).then_inc(done, 1)
                dve.tensor_tensor(qdT[:], qT[:], rows[:, 2, :], ALU.mult).then_inc(done, 1)
                dve.tensor_copy(egl[:], rows[:, 2, CH - 1:TOK:CH]).then_inc(done, 1)
                pe("turn_v")
                four = lambda b: ps[0:CH, b:b + 2, :].rearrange("p b (c e) -> p (b c) e", e=HD)
                dve.tensor_tensor(vb[:], four(2), head_col(BETA, HD), ALU.mult).then_inc(done, 1)
                pe("turn_k")
                dve.tensor_tensor(kbe[:], four(0), head_col(BEGC, HD), ALU.mult).then_inc(done, 1)
                dve.tensor_tensor(kd[:], four(0), head_col(ELAST, HD), ALU.mult).then_inc(done, 1)
                pe("gram")
                act("decay")
                dve.tensor_tensor(attnT[:], ps_c[0:CH, 7, :, :], decay[:], ALU.mult).then_inc(done, 1)
                dve.tensor_tensor(AT[:], ps_c[0:CH, 6, :, :], decay[:], ALU.mult).then_inc(done, 1)
                for l in range(LEVELS):
                    pe(f"AxT{l}")
                    dve.tensor_tensor(prod[:], ps_c[0:CH, 4, :, :], masks[:, l:l + 1, :].to_broadcast([CH, NCH, CH]),
                                      ALU.mult).then_inc(done, 1)
                    pe(f"TxP{l}")
                    one = ident[0:CH, 0:CH].unsqueeze(1).to_broadcast([CH, NCH, CH])
                    if l < LEVELS - 1:
                        dve.tensor_tensor(T[:], one if l == 0 else T[:], ps_c[0:CH, 5, :, :],
                                          ALU.subtract).then_inc(done, 1)
                    dve.tensor_tensor(TT[:], one if l == 0 else TT[:], ps_c[0:CH, 6, :, :],
                                      ALU.subtract).then_inc(done, 1)
                pe("wT")
                dve.tensor_scalar(nwT[:], ps_c[:, 7, :, :], -1.0, None, ALU.mult).then_inc(done, 1)
                for c in range(NCH):
                    pe(f"v_new{c}")
                    dve.tensor_copy(vn[:, c % 2, :], ps[0:CH, c % 2, 0:HD]).then_inc(done, 1)
                    if c == 0:
                        pe("state0")
                        dve.tensor_copy(S[:, 1, :], ps[:, 2, 0:HD]).then_inc(done, 1)
                    elif c < NCH - 1:
                        pe(f"state{c}")
                        dve.scalar_tensor_tensor(out=S[:, (c + 1) % 2, :], in0=S[:, c % 2, :],
                                                 scalar=egl[:, c:c + 1], in1=ps[:, 2 + c % 2, 0:HD],
                                                 op0=ALU.mult, op1=ALU.add).then_inc(done, 1)
                pe("out_sums")
                dve.tensor_scalar(ovar[:], ps[:, 5, :], 1.0 / HD, EPS, ALU.mult, ALU.add).then_inc(done, 1)
                act("root_o")
                dve.reciprocal(ovar[:], ovar[:]).then_inc(done, 1)
                own("inv_o")
                dve.tensor_tensor(o1[:], ps[:, 4, :], ovar[:], ALU.mult).then_inc(done, 1)
                own("o_normed")
                dve.scalar_tensor_tensor(out=o_b[:, bass.ds(h, 1), :].rearrange("p a t -> p (a t)"), in0=o1[:], scalar=norm[:, 0:1], in1=gate[:], op0=ALU.mult,
                                         op1=ALU.mult).then_inc(done, 1)


def mixer_a(nc, h_hi, h_lo, w_a, bias_dram, gains_dram, ident, halves, o_a):
    HW = 64
    with ExitStack() as ctx:
        def sb(name, shape, dt=F32):
            return ctx.enter_context(nc.sbuf_tensor(f"ma_{name}", shape, dt))

        def sem(name):
            return ctx.enter_context(nc.semaphore(f"ma_{name}"))

        gains = sb("gains", [P, 2])
        bias = sb("bias", [P, 2, TOK])
        sq = sb("sq", [P, 2, TOK])
        var = sb("var", [P, 2, TOK])
        q = sb("q", [P, TOK])
        kk = sb("k", [P, TOK])
        vT = sb("vT", [P, TOK])
        v = sb("v", [P, NT, P])
        sc = sb("sc", [P, 2, NT, TOK])
        top = sb("top", [P, 2, NT])
        total = sb("total", [P, 2, NT])
        pT = sb("pT", [P, 2, NT, TOK])
        ps = ctx.enter_context(nc.psum_tensor("ma_ps", [P, 8, TOK], F32))
        consts = sem("consts")
        passed = sem("passed")
        bias_in = sem("bias_in")
        bias_masked = sem("bias_masked")
        T = range(NT)
        pe_done = Steps(sem("pe_done"), ["q", "k", "v", "sums", "turn_v"]
                        + [f"{n}" for a in (0, 1) for n in [f"score{a}{t}" for t in T] + [f"turn{a}{b}" for b in T]
                           + [f"pv{a}"]])
        w = Weights(ctx, nc, "ma", w_a, [KD, KD, KD], pe_done, ["q", "k", "v"])
        act_done = Steps(sem("act_done"), ["sq_q", "sq_k", "v", "root"]
                         + [n for a in (0, 1) for n in [f"exp{a}{t}" for t in T] + [f"pT{a}{b}" for b in T]])
        dve_done = Steps(sem("dve_done"), ["var", "inv", "q", "k", "v"]
                         + [n for a in (0, 1) for n in [f"{s}{a}{t}" for t in T for s in ("sc", "top")]
                            + [f"{s}{a}{t}" for t in T for s in ("inv", "p")] + [f"o{a}"]])
        block = ctx.enter_context(nc.Block())
        TURNS = HEADS // 2
        half = lambda a: slice(HW * a, HW * a + HW)
        width = lambda t: P * (t + 1)

        @block.sync
        def _(sp):
            sp.dma_start(gains[:], gains_dram).then_inc(consts, 16)
            with sp.Fori(0, TURNS) as j:
                sp.wait_ge(dve_done.sem, dve_done.after(f"sc1{NT - 1}", j - 1))
                sp.dma_start(bias[:], bias_dram[bass.ds(j, 1), :, :, :].rearrange("a p h t -> (a p) h t")).then_inc(bias_in, 16)
                w.load(sp, j)

        @block.gpsimd
        def _(pool):
            w.lo_made.open(pool)
            with pool.Fori(0, TURNS) as j:
                pool.wait_ge(bias_in, 16 * (j + 1))
                pool.sem_inc(passed, 1)
                pool.memset(bias[0:CH, :, TOK - CH:TOK], NEG).then_inc(bias_masked, 1)
                w.low(pool, j)

        @block.scalar
        def _(act):
            w.hi_made.open(act)
            act_done.open(act)
            with act.Fori(0, TURNS) as j:
                w.high(act, j)
                for n, t in enumerate("qk"):
                    act.wait_ge(pe_done.sem, pe_done.after(t, j))
                    act.activation(sq[:, n, :], ps[:, n, :], ACT.Square).then_inc(act_done.sem, 1)
                act.wait_ge(pe_done.sem, pe_done.after("v", j))
                act.copy(vT[:], ps[:, 2, :]).then_inc(act_done.sem, 1)
                act.wait_ge(dve_done.sem, dve_done.after("var", j))
                act.activation(var[:], var[:], ACT.Sqrt).then_inc(act_done.sem, 1)
                for a in (0, 1):
                    for t in T:
                        act.wait_ge(dve_done.sem, dve_done.after(f"top{a}{t}", j))
                        act.activation(sc[:, a, t, 0:width(t)], sc[:, a, t, 0:width(t)], ACT.Exp,
                                       bias=top[:, a, t:t + 1],
                                       accum_out=total[:, a, t:t + 1]).then_inc(act_done.sem, 1)
                    for b in T:
                        act.wait_ge(pe_done.sem, pe_done.after(f"turn{a}{b}", j))
                        act.copy(pT[:, a, b, P * b:TOK], ps[:, b % 2, P * b:TOK]).then_inc(act_done.sem, 1)

        @block.tensor
        def _(pe):
            pe_done.open(pe)
            pe.wait_ge(consts, 16)
            with pe.Fori(0, TURNS) as j:
                def dve(name):
                    pe.wait_ge(dve_done.sem, dve_done.after(name, j))
                    pe.sem_inc(passed, 1)

                def act(name):
                    pe.wait_ge(act_done.sem, act_done.after(name, j))
                    pe.sem_inc(passed, 1)

                for m in range(3):
                    if m == 2:
                        pe.wait_ge(dve_done.sem, dve_done.after("o1", j - 1))
                    w.product(pe, j, m, ps[:, m, :], h_hi, h_lo).then_inc(pe_done.sem, 1)
                act("sq_k")
                pe.matmul(ps[:, 3, :], halves[:], sq[:, 0, :], start=True, stop=True)
                pe.matmul(ps[:, 4, :], halves[:], sq[:, 1, :], start=True, stop=True).then_inc(pe_done.sem, 1)
                act("v")
                for t in T:
                    ins = pe.transpose(ps[:, 5, P * t:P * t + P], vT[:, P * t:P * t + P], ident[:])
                ins.then_inc(pe_done.sem, 1)
                dve("v")
                for a in (0, 1):
                    for t in T:
                        if a == 1:
                            dve(f"sc0{t}")
                        pe.matmul(ps[:, 4 + t, 0:width(t)], q[half(a), P * t:P * t + P], kk[half(a), 0:width(t)],
                                  start=True, stop=True).then_inc(pe_done.sem, 1)
                    for b in T:
                        if b >= 2:
                            act(f"pT{a}{b - 2}")
                        for t in range(b, NT):
                            if b == 0:
                                dve(f"p{a}{t}")
                            ins = pe.transpose(ps[:, b % 2, P * t:P * t + P], sc[:, a, t, P * b:P * b + P], ident[:])
                        ins.then_inc(pe_done.sem, 1)
                    for b in T:
                        act(f"pT{a}{b}")
                        ins = pe.matmul(ps[:, 2 + a, P * b:TOK], v[:, b, :], pT[:, a, b, P * b:TOK], start=(b == 0),
                                        stop=(b == NT - 1))
                    ins.then_inc(pe_done.sem, 1)

        @block.vector
        def _(dve):
            dve_done.open(dve)
            dve.wait_ge(consts, 16)
            with dve.Fori(0, TURNS) as j:
                done = dve_done.sem

                def own(name):
                    dve.wait_ge(done, dve_done.after(name, j))

                def pe(name):
                    dve.wait_ge(pe_done.sem, pe_done.after(name, j))

                pe("sums")
                dve.tensor_scalar(var[:], ps[:, 3:5, :], 1.0 / HW, EPS, ALU.mult, ALU.add).then_inc(done, 1)
                dve.wait_ge(act_done.sem, act_done.after("root", j))
                dve.reciprocal(var[:], var[:]).then_inc(done, 1)
                own("inv")
                dve.scalar_tensor_tensor(out=q[:], in0=ps[:, 0, :], scalar=gains[:, 0:1], in1=var[:, 0, :],
                                         op0=ALU.mult, op1=ALU.mult).then_inc(done, 1)
                dve.scalar_tensor_tensor(out=kk[:], in0=ps[:, 1, :], scalar=gains[:, 1:2], in1=var[:, 1, :],
                                         op0=ALU.mult, op1=ALU.mult).then_inc(done, 1)
                pe("turn_v")
                dve.tensor_copy(v[:].rearrange("p t c -> p (t c)"), ps[:, 5, :]).then_inc(done, 1)
                dve.wait_ge(bias_masked, j + 1)
                for a in (0, 1):
                    for t in T:
                        s_t = sc[:, a, t, 0:width(t)]
                        pe(f"score{a}{t}")
                        dve.scalar_tensor_tensor(out=s_t, in0=ps[:, 4 + t, 0:width(t)], scalar=HW ** -0.5,
                                                 in1=bias[:, a, TOK - width(t):TOK], op0=ALU.mult,
                                                 op1=ALU.add).then_inc(done, 1)
                        own(f"sc{a}{t}")
                        dve.tensor_reduce(top[:, a, t:t + 1], s_t, AX.X, ALU.max, negate=True).then_inc(done, 1)
                    for t in T:
                        s_t = sc[:, a, t, 0:width(t)]
                        dve.wait_ge(act_done.sem, act_done.after(f"exp{a}{t}", j))
                        dve.reciprocal(total[:, a, t:t + 1], total[:, a, t:t + 1]).then_inc(done, 1)
                        own(f"inv{a}{t}")
                        dve.tensor_scalar(s_t, s_t, total[:, a, t:t + 1], None, ALU.mult).then_inc(done, 1)
                    pe(f"pv{a}")
                    dve.tensor_copy(o_a[half(a), bass.ds(j, 1), :].rearrange("p a t -> p (a t)"),
                                    ps[half(a), 2 + a, :]).then_inc(done, 1)


def merge(nc, tag, w_dram, pieces, h_hi, h_lo, o_a, ob, b_merge_dram, mixed_hi, mixed_lo):
    with ExitStack() as ctx:
        def sb(name, shape, dt=F32):
            return ctx.enter_context(nc.sbuf_tensor(f"{tag}_{name}", shape, dt))

        def sem(name):
            return ctx.enter_context(nc.semaphore(f"{tag}_{name}"))

        NA = A_W // P
        oa_parts = sb("oa_parts", [P, 2, NA, TOK], F32R)
        ob_parts = sb("ob_parts", [P, 2, KD, TOK], F32R)
        b_merge = sb("b_merge", [P, 2, KD])
        gates = sb("gates", [P, 2, TOK])
        full = sb("full", [P, TOK])
        ps = ctx.enter_context(nc.psum_tensor(f"{tag}_ps", [P, 4, TOK], F32))
        loaded = sem("loaded")
        x_hi = sem("x_hi")
        x_lo = sem("x_lo")
        pe_done = Steps(sem("pe_done"), ["gate_a", "gate_b", "proj_a", "proj_b"])
        w = Weights(ctx, nc, tag, w_dram, pieces, pe_done, ["gate_a", "gate_b", "proj_a", "proj_b"])
        act_done = Steps(sem("act_done"), ["gate_a", "gate_b", "high"])
        dve_done = Steps(sem("dve_done"), ["part_a", "part_b", "sum", "low"])
        block = ctx.enter_context(nc.Block())

        @block.sync
        def _(sp):
            sp.dma_start(b_merge[:], b_merge_dram).then_inc(loaded, 16)
            with sp.Fori(0, KD) as n:
                w.load(sp, n)

        @block.gpsimd
        def _(pool):
            w.lo_made.open(pool)
            with pool.Fori(0, KD) as n:
                w.low(pool, n)

        @block.scalar
        def _(act):
            w.hi_made.open(act)
            act_done.open(act)
            act.wait_ge(loaded, 16)
            act.copy(oa_parts[:, 0, :, :], o_a[:]).then_inc(x_hi, 1)
            act.copy(ob_parts[:, 0, :, :], ob[:]).then_inc(x_hi, 1)
            with act.Fori(0, KD) as n:
                w.high(act, n)
                for g, name in enumerate(("gate_a", "gate_b")):
                    act.wait_ge(pe_done.sem, pe_done.after(name, n))
                    act.activation(gates[:, g, :], ps[:, g, :], ACT.Sigmoid,
                                   bias=b_merge[:, g, bass.ds(n, 1)]).then_inc(act_done.sem, 1)
                act.wait_ge(dve_done.sem, dve_done.after("sum", n))
                act.copy(mixed_hi[:, bass.ds(n, 1), :].rearrange("p a t -> p (a t)"), full[:]).then_inc(act_done.sem, 1)

        @block.tensor
        def _(pe):
            pe.wait_ge(x_lo, 2)
            pe_done.open(pe)
            with pe.Fori(0, KD) as n:
                pe.wait_ge(dve_done.sem, dve_done.after("part_b", n - 1))
                w.product(pe, n, 0, ps[:, 0, :], h_hi, h_lo).then_inc(pe_done.sem, 1)
                w.product(pe, n, 1, ps[:, 1, :], h_hi, h_lo).then_inc(pe_done.sem, 1)
                w.product(pe, n, 2, ps[:, 2, :], oa_parts[:, 0, :, :], oa_parts[:, 1, :, :]).then_inc(pe_done.sem, 1)
                w.product(pe, n, 3, ps[:, 3, :], ob_parts[:, 0, :, :], ob_parts[:, 1, :, :]).then_inc(pe_done.sem, 1)

        @block.vector
        def _(dve):
            dve_done.open(dve)
            dve.wait_ge(x_hi, 2)
            dve.tensor_tensor(oa_parts[:, 1, :, :], o_a[:], oa_parts[:, 0, :, :].bitcast(F32), ALU.subtract).then_inc(x_lo, 1)
            dve.tensor_tensor(ob_parts[:, 1, :, :], ob[:], ob_parts[:, 0, :, :].bitcast(F32), ALU.subtract).then_inc(x_lo, 1)
            with dve.Fori(0, KD) as n:
                for g, name in enumerate(("gate_a", "gate_b")):
                    dve.wait_ge(pe_done.sem, pe_done.after("proj" + name[4:], n))
                    dve.wait_ge(act_done.sem, act_done.after(name, n))
                    dve.tensor_tensor(gates[:, g, :], gates[:, g, :], ps[:, 2 + g, :], ALU.mult).then_inc(dve_done.sem, 1)
                dve.wait_ge(dve_done.sem, dve_done.after("part_b", n))
                dve.tensor_tensor(full[:], gates[:, 0, :], gates[:, 1, :], ALU.add).then_inc(dve_done.sem, 1)
                dve.wait_ge(act_done.sem, act_done.after("high", n))
                at = bass.ds(n, 1)
                dve.tensor_tensor(mixed_lo[:, at, :].rearrange("p a t -> p (a t)"), full[:],
                                  mixed_hi[:, at, :].bitcast(F32).rearrange("p a t -> p (a t)"),
                                  ALU.subtract).then_inc(dve_done.sem, 1)


def project_out(nc, w_dram, mixed_hi, mixed_lo, xT):
    with ExitStack() as ctx:
        sem = lambda name: ctx.enter_context(nc.semaphore(f"po_{name}"))
        ps = ctx.enter_context(nc.psum_tensor("po_ps", [P, 2, TOK], F32))
        made = Steps(sem("made"), range(2))
        added = Steps(sem("added"), range(2))
        w = Weights(ctx, nc, "po", w_dram, [KD, KD], made, range(2))
        block = ctx.enter_context(nc.Block())
        TURNS = KD // 2

        @block.sync
        def _(sp):
            with sp.Fori(0, TURNS) as n:
                w.load(sp, n)

        @block.gpsimd
        def _(pool):
            w.lo_made.open(pool)
            with pool.Fori(0, TURNS) as n:
                w.low(pool, n)

        @block.scalar
        def _(act):
            w.hi_made.open(act)
            with act.Fori(0, TURNS) as n:
                w.high(act, n)

        @block.tensor
        def _(pe):
            made.open(pe)
            with pe.Fori(0, TURNS) as n:
                for m in range(2):
                    pe.wait_ge(added.sem, added.after(m, n - 1))
                    w.product(pe, n, m, ps[:, m, :], mixed_hi, mixed_lo).then_inc(made.sem, 1)

        @block.vector
        def _(dve):
            added.open(dve)
            with dve.Fori(0, TURNS) as n:
                for m in range(2):
                    x = xT[:, bass.ds(2 * n + m, 1), :].rearrange("p a t -> p (a t)")
                    dve.wait_ge(made.sem, made.after(m, n))
                    dve.tensor_tensor(x, x, ps[:, m, :], ALU.add).then_inc(added.sem, 1)


KEYS = 128
TOP = 16


def choose_experts(nc, w_dram, keys_dram, iota_dram, h_hi, h_lo, sel):
    with ExitStack() as ctx:
        def sb(name, shape, dt=F32):
            return ctx.enter_context(nc.sbuf_tensor(f"ce_{name}", shape, dt))

        def sem(name):
            return ctx.enter_context(nc.semaphore(f"ce_{name}"))

        keys = sb("keys", [P, 2, KEYS])
        iota = sb("iota", [P, TOP])
        q = sb("q", [P, 2, TOK])
        s = sb("s", [P, 2, NT, KEYS])
        rest = sb("rest", [P, 2, NT, KEYS])
        best = sb("best", [P, 2, NT, TOP])
        place = sb("place", [P, 2, NT, TOP], U32)
        place_f = sb("place_f", [P, 2, NT, TOP])
        cand = sb("cand", [P, NT, TOP * TOP])
        cand_rest = sb("cand_rest", [P, NT, TOP * TOP])
        top = sb("top", [P, NT, TOP])
        pos = sb("pos", [P, NT, TOP], U32)
        pos_part = sb("pos_part", [P, 2, NT, TOP], U32)
        pos_f = sb("pos_f", [P, 2, NT, TOP])
        hot = sb("hot", [P, 2, NT * TOP, TOP])
        e = sb("e", [P, NT, TOP])
        total = sb("total", [P, NT])
        ps = ctx.enter_context(nc.psum_tensor("ce_ps", [P, 4, TOK], F32))
        consts = sem("consts")
        keys_in = sem("keys_in")
        passed = sem("passed")
        pe_done = Steps(sem("pe_done"), ["q0", "q1", "s0", "s1"])
        w = Weights(ctx, nc, "ce", w_dram, [KD, KD], pe_done, ["q0", "q1"])
        act_done = Steps(sem("act_done"), ["q0", "q1", "s0", "s1", "exp"])
        dve_done = Steps(sem("dve_done"), ["max1", "at1", "drop", "max2", "at2", "place_f", "cand", "cmax1", "cat1",
                                           "cdrop", "cmax2", "cat2", "row", "col", "pos_f", "hot0", "hot1", "pick0",
                                           "pick1", "index0", "index1", "minus", "total", "inv", "gate"])
        block = ctx.enter_context(nc.Block())

        @block.sync
        def _(sp):
            sp.dma_start(iota[:], iota_dram).then_inc(consts, 16)
            with sp.Fori(0, HEADS) as h:
                w.load(sp, h)
                sp.wait_ge(pe_done.sem, pe_done.after("s1", h - 1))
                sp.dma_start(keys[:], keys_dram[bass.ds(h, 1), :, :, :].rearrange("a p s k -> (a p) s k")).then_inc(keys_in, 16)

        @block.gpsimd
        def _(pool):
            w.lo_made.open(pool)
            with pool.Fori(0, HEADS) as h:
                w.low(pool, h)

        @block.scalar
        def _(act):
            w.hi_made.open(act)
            act_done.open(act)
            with act.Fori(0, HEADS) as h:
                w.high(act, h)
                for m in (0, 1):
                    act.wait_ge(pe_done.sem, pe_done.after(f"q{m}", h))
                    act.copy(q[:, m, :], ps[:, m, :]).then_inc(act_done.sem, 1)
                act.wait_ge(dve_done.sem, dve_done.after("drop", h - 1))
                for m in (0, 1):
                    act.wait_ge(pe_done.sem, pe_done.after(f"s{m}", h))
                    act.copy(s[:, m, :, :].rearrange("p t k -> p (t k)"), ps[:, 2 + m, :]).then_inc(act_done.sem, 1)
                act.wait_ge(dve_done.sem, dve_done.after("minus", h))
                act.activation(e[:], e[:], ACT.Exp).then_inc(act_done.sem, 1)

        @block.tensor
        def _(pe):
            pe_done.open(pe)
            with pe.Fori(0, HEADS) as h:
                for m in (0, 1):
                    w.product(pe, h, m, ps[:, m, :], h_hi, h_lo).then_inc(pe_done.sem, 1)
                pe.wait_ge(keys_in, 16 * (h + 1))
                for m in (0, 1):
                    pe.wait_ge(act_done.sem, act_done.after(f"q{m}", h))
                    for t in range(NT):
                        ins = pe.matmul(ps[:, 2 + m, P * t:P * t + P], q[:, m, P * t:P * t + P], keys[:, m, :],
                                        start=True, stop=True)
                    ins.then_inc(pe_done.sem, 1)

        @block.vector
        def _(dve):
            dve_done.open(dve)
            dve.wait_ge(consts, 16)
            with dve.Fori(0, HEADS) as h:
                done = dve_done.sem
                first, second = slice(0, 8), slice(8, 16)
                pairs = [(m, t) for m in (0, 1) for t in range(NT)]

                def own(name):
                    dve.wait_ge(done, dve_done.after(name, h))
                    dve.sem_inc(passed, 1)

                dve.wait_ge(act_done.sem, act_done.after("s1", h))
                dve.sem_inc(passed, 1)
                for m, t in pairs:
                    ins = dve.max(best[:, m, t, first], s[:, m, t, :])
                ins.then_inc(done, 1)
                own("max1")
                for m, t in pairs:
                    ins = dve.max_index(place[:, m, t, first], best[:, m, t, first], s[:, m, t, :])
                ins.then_inc(done, 1)
                for m, t in pairs:
                    ins = dve.match_replace(rest[:, m, t, :], best[:, m, t, first], s[:, m, t, :], -3.0e38)
                ins.then_inc(done, 1)
                own("drop")
                for m, t in pairs:
                    ins = dve.max(best[:, m, t, second], rest[:, m, t, :])
                ins.then_inc(done, 1)
                own("max2")
                for m, t in pairs:
                    ins = dve.max_index(place[:, m, t, second], best[:, m, t, second], rest[:, m, t, :])
                ins.then_inc(done, 1)
                own("at2")
                dve.tensor_copy(place_f[:], place[:]).then_inc(done, 1)
                dve.tensor_tensor(cand[:].rearrange("p t (a b) -> p t a b", a=TOP),
                                  best[:, 0, :, :].unsqueeze(3).to_broadcast([P, NT, TOP, TOP]),
                                  best[:, 1, :, :].unsqueeze(2).to_broadcast([P, NT, TOP, TOP]),
                                  ALU.add).then_inc(done, 1)
                own("cand")
                for t in range(NT):
                    ins = dve.max(top[:, t, first], cand[:, t, :])
                ins.then_inc(done, 1)
                own("cmax1")
                for t in range(NT):
                    ins = dve.max_index(pos[:, t, first], top[:, t, first], cand[:, t, :])
                ins.then_inc(done, 1)
                for t in range(NT):
                    ins = dve.match_replace(cand_rest[:, t, :], top[:, t, first], cand[:, t, :], -3.0e38)
                ins.then_inc(done, 1)
                own("cdrop")
                for t in range(NT):
                    ins = dve.max(top[:, t, second], cand_rest[:, t, :])
                ins.then_inc(done, 1)
                own("cmax2")
                for t in range(NT):
                    ins = dve.max_index(pos[:, t, second], top[:, t, second], cand_rest[:, t, :])
                ins.then_inc(done, 1)
                own("cat2")
                dve.tensor_scalar(pos_part[:, 0, :, :], pos[:], 4, None, ALU.logical_shift_right).then_inc(done, 1)
                dve.tensor_scalar(pos_part[:, 1, :, :], pos[:], TOP - 1, None, ALU.bitwise_and).then_inc(done, 1)
                own("col")
                dve.tensor_copy(pos_f[:], pos_part[:]).then_inc(done, 1)
                own("pos_f")
                for m in (0, 1):
                    dve.tensor_tensor(hot[:, m, :, :],
                                      pos_f[:, m, :, :].rearrange("p t k -> p (t k)").unsqueeze(2).to_broadcast([P, NT * TOP, TOP]),
                                      iota[:].unsqueeze(1).to_broadcast([P, NT * TOP, TOP]),
                                      ALU.is_equal).then_inc(done, 1)
                for m in (0, 1):
                    four = hot[:, m, :, :].rearrange("p (t k) r -> p t k r", t=NT)
                    own(f"hot{m}")
                    dve.tensor_tensor(four, four, place_f[:, m, :, :].unsqueeze(2).to_broadcast([P, NT, TOP, TOP]),
                                      ALU.mult).then_inc(done, 1)
                for m in (0, 1):
                    own(f"pick{m}")
                    dve.tensor_reduce(sel[:, 1 + m, :, bass.ds(h, 1), :].rearrange("p t a k -> p t (a k)"),
                                      hot[:, m, :, :].rearrange("p (t k) r -> p t k r", t=NT), AX.X,
                                      ALU.add).then_inc(done, 1)
                dve.tensor_tensor(e[:], top[:], top[:, :, 0:1].to_broadcast([P, NT, TOP]), ALU.subtract).then_inc(done, 1)
                dve.wait_ge(act_done.sem, act_done.after("exp", h))
                dve.tensor_reduce(total[:], e[:], AX.X, ALU.add).then_inc(done, 1)
                own("total")
                dve.reciprocal(total[:], total[:]).then_inc(done, 1)
                own("inv")
                dve.tensor_tensor(sel[:, 0, :, bass.ds(h, 1), :].rearrange("p t a k -> p t (a k)"), e[:],
                                  total[:].unsqueeze(2).to_broadcast([P, NT, TOP]), ALU.mult).then_inc(done, 1)


def spread_gates(nc, sel, ident, iota_dram, gates_dram):
    STEP = 8
    with ExitStack() as ctx:
        def sb(name, shape, dt=F32):
            return ctx.enter_context(nc.sbuf_tensor(f"sg_{name}", shape, dt))

        def sem(name):
            return ctx.enter_context(nc.semaphore(f"sg_{name}"))

        iota = sb("iota", [P, KEYS])
        selT = sb("selT", [P, 3, TOK])
        turn_rows = sb("turn_rows", [P, STEP])
        row = sb("row", [P, STEP, KEYS])
        col = sb("col", [P, STEP, KEYS])
        full = sb("full", [P, 2, KEYS, P])
        ps = ctx.enter_context(nc.psum_tensor("sg_ps", [P, 3 + 2, TOK], F32))
        loaded = sem("loaded")
        turned = sem("turned")
        copied = sem("copied")
        rows_there = sem("rows_there")
        passed = sem("passed")
        row_made = Items(sem("row_made"), STEP)
        col_made = sem("col_made")
        used = Items(sem("used"), STEP)
        filled = Items(sem("filled"), 2)
        stored = [sem("stored0"), sem("stored1")]
        block = ctx.enter_context(nc.Block())
        TURNS = P // STEP
        slots = sel[:].rearrange("p a t h k -> p a t (h k)")

        @block.sync
        def _(sp):
            sp.dma_start(iota[:], iota_dram).then_inc(loaded, 16)
            for t in range(NT):
                sp.wait_ge(filled.sem, filled.after(2 * TURNS * (t + 1) - 1))
                sp.dma_start(gates_dram[t], full[:, t % 2, :, :]).then_inc(stored[t % 2], 16)
            for s in stored:
                sp.wait_ge(s, 16 * NT // 2)

        @block.tensor
        def _(pe):
            pe.wait_ge(loaded, 16)
            for a in range(3):
                for t in range(NT):
                    ins = pe.transpose(ps[:, a, P * t:P * t + P], slots[:, a, t, :], ident[:])
            ins.then_inc(turned, 1)
            used.open(pe)
            with pe.Fori(0, TURNS * NT) as i:
                for n in range(STEP):
                    if n % 4 == 0:
                        pe.wait_ge(filled.sem, filled.after(2 * i + n // 4 - 2))
                    pe.wait_ge(row_made.sem, row_made.after(STEP * i + n))
                    pe.wait_ge(col_made, STEP * i + n + 1)
                    pe.matmul(ps[:, 3 + n // 4, P * (n % 4):P * (n % 4) + P], row[:, n, :], col[:, n, :],
                              start=True, stop=True).then_inc(used.sem, 1)

        @block.gpsimd
        def _(pool):
            row_made.open(pool)
            pool.wait_ge(loaded, 16)
            pool.wait_ge(copied, 1)
            with pool.Fori(0, TURNS * NT) as i:
                pool.wait_ge(row_made.sem, row_made.after(STEP * i - 1))
                pool.tensor_copy(turn_rows[:], selT[:, 1, bass.ds(STEP * i, STEP)]).then_inc(rows_there, 1)
                pool.wait_ge(rows_there, i + 1)
                for n in range(STEP):
                    pool.wait_ge(used.sem, used.after(STEP * i + n - STEP))
                    pool.sem_inc(passed, 1)
                    pool.tensor_scalar(row[:, n, :], iota[:], turn_rows[:, n:n + 1], None,
                                       ALU.is_equal).then_inc(row_made.sem, 1)

        @block.scalar
        def _(act):
            filled.open(act)
            for t in range(NT):
                if t >= 2:
                    act.wait_ge(stored[t % 2], 16 * (t // 2))
                with act.Fori(0, TURNS) as i:
                    for b in range(2):
                        act.wait_ge(used.sem, used.after(STEP * (i + TURNS * t) + 4 * b + 3))
                        act.copy(full[:, t % 2, :, bass.ds(STEP * i + 4 * b, 4)].rearrange("p c t -> p t c"),
                                 ps[:, 3 + b, :].rearrange("p (t c) -> p t c", t=4)).then_inc(filled.sem, 1)

        @block.vector
        def _(dve):
            dve.wait_ge(turned, 1)
            dve.tensor_copy(selT[:].rearrange("p a t -> p (a t)"), ps[:, 0:3, :].rearrange("p a t -> p (a t)")).then_inc(copied, 1)
            dve.wait_ge(loaded, 16)
            dve.wait_ge(copied, 1)
            with dve.Fori(0, TURNS * NT) as i:
                for n in range(STEP):
                    at = bass.ds(STEP * i + n, 1)
                    dve.wait_ge(used.sem, used.after(STEP * i + n - STEP))
                    dve.tensor_scalar(col[:, n, :], iota[:], selT[:, 2, at], selT[:, 0, at], ALU.is_equal,
                                      ALU.mult).then_inc(col_made, 1)


def experts(nc, down_dram, up_dram, gates_dram, h_hi, h_lo, acc, out_dram):
    G = 4
    SLOTS = 2 * G
    TURNS = KEYS // SLOTS
    UP = D // P
    BANKS = 4
    with ExitStack() as ctx:
        def sb(name, shape, dt=F32):
            return ctx.enter_context(nc.sbuf_tensor(f"ex_{name}", shape, dt))

        def sem(name):
            return ctx.enter_context(nc.semaphore(f"ex_{name}"))

        d_raw = sb("d_raw", [P, 2, KD, P])
        d_hi = sb("d_hi", [P, 2, KD, P], F32R)
        d_lo = sb("d_lo", [P, 2, KD, P], F32R)
        u_raw = sb("u_raw", [P, 2, D])
        u_hi = sb("u_hi", [P, SLOTS, D], F32R)
        u_lo = sb("u_lo", [P, SLOTS, D], F32R)
        gates = sb("gates", [P, 2, NT, G, P])
        gelu = sb("gelu", [P, 2, TOK])
        a = sb("a", [P, 2, TOK])
        a_hi = sb("a_hi", [P, SLOTS, TOK], F32R)
        a_lo = sb("a_lo", [P, SLOTS, TOK], F32R)
        ps = ctx.enter_context(nc.psum_tensor("ex_ps", [P, 8, TOK], F32))
        d_in = [sem("d_in0"), sem("d_in1")]
        u_in = [sem("u_in0"), sem("u_in1")]
        g_in = [sem("g_in0"), sem("g_in1")]
        d_hi_made, u_hi_made = Items(sem("d_hi_made"), 0), Items(sem("u_hi_made"), 0)
        d_lo_made, u_lo_made = Items(sem("d_lo_made"), 2), Items(sem("u_lo_made"), 2)
        down_done = Items(sem("down_done"), 2)
        gelu_made = Items(sem("gelu_made"), 2)
        a_made = Items(sem("a_made"), SLOTS)
        a_hi_made, a_lo_made = Items(sem("a_hi_made"), 0), Items(sem("a_lo_made"), 0)
        up_done = Items(sem("up_done"), 2 * UP)
        added = Items(sem("added"), BANKS)
        stored = sem("stored")
        block = ctx.enter_context(nc.Block())
        @block.sync
        def _(sp):
            with sp.Fori(0, TURNS) as i:
                for q in range(SLOTS):
                    n, s = SLOTS * i + q, q % 2
                    sp.wait_ge(d_lo_made.sem, d_lo_made.after(n - 2))
                    sp.dma_start(d_raw[:, s, :, :], down_dram[bass.ds(n, 1), :, :, :].rearrange("a p k c -> (a p) k c")).then_inc(d_in[s], 16)
                    if q % G == 0:
                        sp.wait_ge(a_made.sem, a_made.after(n - SLOTS + G - 1))
                        sp.dma_start(gates[:, q // G, :, :, :], gates_dram[:, :, bass.ds(n, G), :].rearrange("t p c k -> p t c k")).then_inc(g_in[q // G], 16)
                    sp.wait_ge(u_lo_made.sem, u_lo_made.after(n - 2))
                    sp.dma_start(u_raw[:, s, :], up_dram[bass.ds(n, 1), :, :].rearrange("a p c -> (a p) c")).then_inc(u_in[s], 16)
            sp.wait_ge(added.sem, added.after(UP * KEYS // G - 1))
            sp.dma_start(out_dram, acc[:]).then_inc(stored, 16)
            sp.wait_ge(stored, 16)

        @block.gpsimd
        def _(pool):
            d_lo_made.open(pool)
            u_lo_made.open(pool)
            with pool.Fori(0, TURNS) as i:
                for q in range(SLOTS):
                    n, s = SLOTS * i + q, q % 2
                    pool.wait_ge(d_hi_made.sem, d_hi_made.after(n))
                    pool.tensor_tensor(d_lo[:, s, :, :], d_raw[:, s, :, :], d_hi[:, s, :, :].bitcast(F32),
                                       ALU.subtract).then_inc(d_lo_made.sem, 1)
                    pool.wait_ge(u_hi_made.sem, u_hi_made.after(n))
                    pool.tensor_tensor(u_lo[:, q, :], u_raw[:, s, :], u_hi[:, q, :].bitcast(F32),
                                       ALU.subtract).then_inc(u_lo_made.sem, 1)

        @block.scalar
        def _(act):
            def activate(n, q):
                act.wait_ge(down_done.sem, down_done.after(n))
                act.activation(gelu[:, q % 2, :], ps[:, q % 2, :], ACT.Gelu).then_inc(gelu_made.sem, 1)
                act.wait_ge(a_made.sem, a_made.after(n))
                act.copy(a_hi[:, q, :], a[:, q % 2, :]).then_inc(a_hi_made.sem, 1)

            def turn(i, first=False):
                for q in range(SLOTS):
                    n, s = SLOTS * i + q, q % 2
                    act.wait_ge(d_in[s], 16 * (G * i + q // 2 + 1))
                    act.wait_ge(down_done.sem, down_done.after(n - 2))
                    act.copy(d_hi[:, s, :, :], d_raw[:, s, :, :]).then_inc(d_hi_made.sem, 1)
                    act.wait_ge(u_in[s], 16 * (G * i + q // 2 + 1))
                    if q % G == 0:
                        act.wait_ge(up_done.sem, up_done.after(UP * (2 * i + q // G - 1) - 1))
                    act.copy(u_hi[:, q, :], u_raw[:, s, :]).then_inc(u_hi_made.sem, 1)
                    if q or not first:
                        activate(n - 1, (q - 1) % SLOTS)

            gelu_made.open(act)
            turn(0, first=True)
            with act.Fori(1, TURNS) as i:
                turn(i)
            activate(KEYS - 1, SLOTS - 1)

        @block.tensor
        def _(pe):
            def up(g, half, j):
                if j == 0:
                    pe.wait_ge(a_lo_made.sem, a_lo_made.after(G * g + G - 1))
                    pe.wait_ge(u_lo_made.sem, u_lo_made.after(G * g + G - 1))
                for c in (2 * j, 2 * j + 1):
                    pe.wait_ge(added.sem, added.after(UP * g + c - BANKS))
                    for t in range(G):
                        s = G * half + t
                        ins = three_passes(pe, ps[:, 2 + c % BANKS, :], u_hi[:, s, P * c:P * c + P],
                                           u_lo[:, s, P * c:P * c + P], a_hi[:, s, :], a_lo[:, s, :],
                                           t == 0, t == G - 1)
                    ins.then_inc(up_done.sem, 1)

            def turn(i, first=False):
                for q in range(SLOTS):
                    n, s = SLOTS * i + q, q % 2
                    pe.wait_ge(gelu_made.sem, gelu_made.after(n - 2))
                    pe.wait_ge(d_lo_made.sem, d_lo_made.after(n))
                    for k in range(KD):
                        ins = three_passes(pe, ps[:, s, :], d_hi[:, s, k, :], d_lo[:, s, k, :], h_hi[:, k, :],
                                           h_lo[:, k, :], k == 0, k == KD - 1)
                    ins.then_inc(down_done.sem, 1)
                    if q >= G or not first:
                        up(2 * i + q // G - 1, 1 - q // G, q % G)

            down_done.open(pe)
            up_done.open(pe)
            turn(0, first=True)
            with pe.Fori(1, TURNS) as i:
                turn(i)
            for j in range(G):
                up(2 * TURNS - 1, 1, j)

        @block.vector
        def _(dve):
            def sum_up(g, j):
                for c in (2 * j, 2 * j + 1):
                    dve.wait_ge(up_done.sem, up_done.after(UP * g + c))
                    dve.tensor_tensor(acc[:, c, :], acc[:, c, :], ps[:, 2 + c % BANKS, :],
                                      ALU.add).then_inc(added.sem, 1)

            def turn(i, first=False):
                for q in range(SLOTS):
                    n = SLOTS * i + q
                    if q % G == 0:
                        dve.wait_ge(g_in[q // G], 16 * (i + 1))
                        dve.wait_ge(up_done.sem, up_done.after(UP * (2 * i + q // G - 1) - 1))
                    dve.wait_ge(gelu_made.sem, gelu_made.after(n))
                    dve.tensor_tensor(a[:, q % 2, :].rearrange("p (t k) -> p t k", t=NT), gates[:, q // G, :, q % G, :],
                                      gelu[:, q % 2, :].rearrange("p (t k) -> p t k", t=NT),
                                      ALU.mult).then_inc(a_made.sem, 1)
                    dve.wait_ge(a_hi_made.sem, a_hi_made.after(n))
                    dve.tensor_tensor(a_lo[:, q, :], a[:, q % 2, :], a_hi[:, q, :].bitcast(F32),
                                      ALU.subtract).then_inc(a_lo_made.sem, 1)
                    if q >= G or not first:
                        sum_up(2 * i + q // G - 1, q % G)

            a_made.open(dve)
            added.open(dve)
            turn(0, first=True)
            with dve.Fori(1, TURNS) as i:
                turn(i)
            for j in range(G):
                sum_up(2 * TURNS - 1, j)


def build(nc, dram, out):
    with ExitStack() as ctx:
        def sb(name, shape, dt=F32):
            return ctx.enter_context(nc.sbuf_tensor(name, shape, dt))

        xT = sb("xT", [P, KD, TOK])
        ident = sb("ident", [P, P])
        ones = sb("ones", [P, P])
        halves = sb("halves", [P, P])
        h_hi = sb("h_hi", [P, KD, TOK], F32R)
        h_lo = sb("h_lo", [P, KD, TOK], F32R)
        cols = sb("cols", [CH, 4, NCH, HEADS])
        rows_dram = nc.dram_tensor("rows_dram", [HEADS, 3, TOK], F32, kind="Internal").ap()
        gates_dram = nc.dram_tensor("gates_dram", [NT, KEYS, KEYS, P], F32, kind="Internal").ap()

        with nc.sbuf_tensor("h_full", [P, KD, TOK], F32) as h_full:
            norm_and_split(nc, "n1", xT, dram["norm_mix"], ones, h_full, h_hi, h_lo,
                           load=[(xT[:], dram["xT"]), (ident[:], dram["ident"]), (ones[:], dram["ones"]),
                                 (halves[:], dram["halves"])])
            decay_rows(nc, h_full, dram["w_ab"], dram["dt_bias"], dram["a_log"], ident, dram["resets"],
                       rows_dram, cols)
        with nc.sbuf_tensor("o_b", [P, HEADS, TOK], F32) as o_b:
            mixer_b(nc, h_hi, h_lo, dram["w_b"], dram["conv"], dram["b_norm"], rows_dram, cols, ident, ones,
                    dram["masks"], o_b)
            with nc.sbuf_tensor("o_a", [P, A_W // P, TOK], F32) as o_a:
                mixer_a(nc, h_hi, h_lo, dram["w_a"], dram["bias"], dram["a_gains"], ident, halves, o_a)
                with (nc.sbuf_tensor("mixed_hi", [P, KD, TOK], F32R) as mixed_hi,
                      nc.sbuf_tensor("mixed_lo", [P, KD, TOK], F32R) as mixed_lo):
                    merge(nc, "mg", dram["w_merge"], [KD, KD, A_W // P, KD], h_hi, h_lo, o_a, o_b,
                          dram["b_merge"], mixed_hi, mixed_lo)
                    project_out(nc, dram["w_out"], mixed_hi, mixed_lo, xT)
        with nc.sbuf_tensor("hf_full", [P, KD, TOK], F32) as h_full:
            norm_and_split(nc, "n2", xT, dram["norm_ffn"], ones, h_full, h_hi, h_lo)
        with nc.sbuf_tensor("sel", [P, 3, NT, HEADS, TOP], F32) as sel:
            choose_experts(nc, dram["w_query"], dram["keys"], dram["iota16"], h_hi, h_lo, sel)
            spread_gates(nc, sel, ident, dram["iota128"], gates_dram)
        experts(nc, dram["down"], dram["up"], gates_dram, h_hi, h_lo, xT, out)


A_W, B_W = 512, 1024
OFF_B = 3 * A_W
OFF_AB = OFF_B + 3 * B_W
OFF_G = OFF_AB + 16
OFF_M = OFF_G + B_W


def layout(inputs):
    import numpy as np

    def tiles(w):
        k = w.shape[0] // P
        return np.ascontiguousarray(w.reshape(k, P, w.shape[1] // P, P).transpose(2, 1, 0, 3))

    a = {k: np.asarray(v) for k, v in inputs.items()}
    w_in = a["w_in"][0]
    qkv = [tiles(w_in[:, OFF_B + i * B_W:OFF_B + (i + 1) * B_W]) for i in range(3)]
    gate = tiles(w_in[:, OFF_G:OFF_G + B_W])
    out = {
        "xT": a["x"][0].T.reshape(KD, P, TOK).transpose(1, 0, 2),
        "ident": np.eye(P, dtype=np.float32),
        "ones": np.ones((P, P), np.float32),
        "norm_mix": a["norm_mix_w"][0].reshape(KD, P).T,
        "w_ab": w_in[:, OFF_AB:OFF_AB + 16].reshape(KD, P, 16).transpose(1, 0, 2),
        "dt_bias": a["b_dt_bias"][0][:, None],
        "a_log": a["b_a_log"][0][:, None],
        "resets": np.tile((np.arange(TOK) % CH != 0).astype(np.float32), (HEADS, 1)),
        "w_b": np.concatenate(qkv + [gate], 2),
        "conv": a["b_conv_w"][0].reshape(CONV, 3, HEADS, P).transpose(3, 2, 1, 0),
        "b_norm": a["b_norm_w"][0][:, None],
    }
    i, j = np.arange(CH)[:, None], np.arange(CH)[None, :]
    levels = [((i // (2 * s) == j // (2 * s)) & (i // s > j // s)).astype(np.float32) for s in (1, 2, 4, 8, 16, 32)]
    levels.append(np.where(j >= i, 0.0, NEG).astype(np.float32))
    rel = a["a_rel_bias"][0]
    reach = TOK - P
    longer = np.pad(rel, ((0, 0), (0, TOK - rel.shape[1] + P)), mode="edge")
    rev = longer[:, ::-1]
    last = longer.shape[1] - 1
    out["bias"] = np.stack([rev[:, last - (r + reach + P):last - (r + reach + P) + TOK] for r in range(P)], 1) \
        .reshape(HEADS // 2, 2, P, TOK).transpose(0, 2, 1, 3)
    out["a_gains"] = np.stack([np.tile(a["a_q_norm_w"][0], 2), np.tile(a["a_k_norm_w"][0], 2)], 1)
    out["halves"] = np.kron(np.eye(2, dtype=np.float32), np.ones((64, 64), np.float32))
    out["w_a"] = np.concatenate([tiles(w_in[:, A_W * n:A_W * n + A_W]) for n in range(3)], 2)
    merge_w = [tiles(w_in[:, OFF_M + D * n:OFF_M + D * n + D]) for n in range(2)]
    out["w_merge"] = np.concatenate(merge_w + [tiles(a["w_proj_a"][0]), tiles(a["w_proj_b"][0])], 2)
    out["b_merge"] = a["b_merge"][0].reshape(2, KD, P).transpose(2, 0, 1)
    pair = lambda w: np.concatenate([w[0::2], w[1::2]], 2)
    out["w_out"] = pair(tiles(a["w_out"][0]))
    out["norm_ffn"] = a["norm_ffn_w"][0].reshape(KD, P).T
    out["w_query"] = pair(tiles(a["peer_w_query"][0]))
    out["keys"] = np.stack([a["peer_keys_1"][0], a["peer_keys_2"][0]], 0).transpose(1, 3, 0, 2)
    out["iota16"] = np.tile(np.arange(TOP, dtype=np.float32), (P, 1))
    out["iota128"] = np.tile(np.arange(KEYS, dtype=np.float32), (P, 1))
    out["down"] = a["peer_down"][0].reshape(KEYS, KEYS, KD, P).transpose(1, 3, 2, 0)
    out["up"] = a["peer_up"][0].reshape(KEYS, KEYS, D).transpose(1, 0, 2)
    out["masks"] = np.stack(levels, 1)
    return {k: np.ascontiguousarray(v) for k, v in out.items()}


def kernel(**inputs):
    import numpy as np
    import concourse.bacc as bacc
    from concourse.bass_utils import run_bass_kernel_spmd

    arrays = layout(inputs)
    nc = bacc.Bacc("TRN2", target_bir_lowering=False, num_devices=1)
    dram = {k: nc.dram_tensor(f"in_{k}", v.shape, mybir.dt.from_np(v.dtype), kind="ExternalInput").ap()
            for k, v in arrays.items()}
    out = nc.dram_tensor("out_y", [P, KD, TOK], F32, kind="ExternalOutput").ap()
    build(nc, dram, out)
    r = run_bass_kernel_spmd(nc, [{f"in_{k}": v for k, v in arrays.items()}], core_ids=[0])
    y = r.results[0]["out_y"]
    return np.ascontiguousarray(y.transpose(1, 0, 2).reshape(D, TOK).T)[None]
```

```python
import math
from contextlib import ExitStack

import concourse.bass as bass
from concourse import mybir

P = 128
D = 1024
TOK = 512
KD = D // P
NT = TOK // P
CH = 64
NCH = TOK // CH
EPS = 1e-6
HEADS = 8
HD = 128
LEVELS = 6
CONV = 4
NEG = -1e30

F32 = mybir.dt.float32
F32R = mybir.dt.float32r
U32 = mybir.dt.uint32
ALU = mybir.AluOpType
ACT = mybir.ActivationFunctionType
AX = mybir.AxisListType


class Steps:

    def __init__(self, sem, names):
        self.sem = sem
        self.per = len(names)
        self.place = {name: n + 1 for n, name in enumerate(names)}
        assert len(self.place) == self.per

    def open(self, engine):
        engine.sem_inc(self.sem, self.per)

    def after(self, name, turn=0):
        return (turn + 1) * self.per + self.place[name]


class Items:

    def __init__(self, sem, ahead):
        self.sem, self.ahead = sem, ahead

    def open(self, engine):
        engine.sem_inc(self.sem, self.ahead)

    def after(self, n):
        return n + 1 + self.ahead


def three_passes(pe, out, w_hi, w_lo, x_hi, x_lo, first, last):
    pe.matmul(out, w_hi, x_lo, start=first, stop=False)
    pe.matmul(out, w_lo, x_hi, start=False, stop=False)
    return pe.matmul(out, w_hi, x_hi, start=False, stop=last)


class Weights:

    def __init__(self, ctx, nc, tag, dram, pieces, used, names):
        self.dram, self.pieces, self.used, self.names = dram, pieces, used, names
        self.starts = [sum(pieces[:m]) for m in range(len(pieces))]
        self.n = len(pieces)
        shape = [P, sum(pieces), P]
        self.raw = ctx.enter_context(nc.sbuf_tensor(f"{tag}_w_raw", shape, F32))
        self.hi = ctx.enter_context(nc.sbuf_tensor(f"{tag}_w_hi", shape, F32R))
        self.lo = ctx.enter_context(nc.sbuf_tensor(f"{tag}_w_lo", shape, F32R))
        sem = lambda name: ctx.enter_context(nc.semaphore(f"{tag}_{name}"))
        self.raw_in = [sem(f"w_raw_in{m}") for m in range(self.n)]
        self.hi_made = Steps(sem("w_hi_made"), range(self.n))
        self.lo_made = Steps(sem("w_lo_made"), range(self.n))

    def part(self, tensor, m):
        return tensor[:, self.starts[m]:self.starts[m] + self.pieces[m], :]

    def load(self, sp, i):
        for m in range(self.n):
            sp.wait_ge(self.lo_made.sem, self.lo_made.after(m, i - 1))
            src = self.dram[bass.ds(i, 1), :, self.starts[m]:self.starts[m] + self.pieces[m], :]
            sp.dma_start(self.part(self.raw, m), src.rearrange("a p k c -> (a p) k c")).then_inc(self.raw_in[m], 16)

    def high(self, act, i, pieces=None):
        for m in range(self.n) if pieces is None else pieces:
            act.wait_ge(self.raw_in[m], 16 * (i + 1))
            act.wait_ge(self.used.sem, self.used.after(self.names[m], i - 1))
            act.copy(self.part(self.hi, m), self.part(self.raw, m)).then_inc(self.hi_made.sem, 1)

    def low(self, pool, i):
        for m in range(self.n):
            pool.wait_ge(self.hi_made.sem, self.hi_made.after(m, i))
            pool.tensor_tensor(self.part(self.lo, m), self.part(self.raw, m), self.part(self.hi, m).bitcast(F32),
                               ALU.subtract).then_inc(self.lo_made.sem, 1)

    def block(self, pe, i, m, k, out, x_hi, x_lo):
        if k == 0:
            pe.wait_ge(self.lo_made.sem, self.lo_made.after(m, i))
        at = self.starts[m] + k
        return three_passes(pe, out, self.hi[:, at, :], self.lo[:, at, :], x_hi[:, k, :], x_lo[:, k, :],
                            k == 0, k == self.pieces[m] - 1)

    def product(self, pe, i, m, out, x_hi, x_lo):
        for k in range(self.pieces[m]):
            ins = self.block(pe, i, m, k, out, x_hi, x_lo)
        return ins


def norm_and_split(nc, tag, x, gain_dram, ones, h_full, h_hi, h_lo, load=None):
    with ExitStack() as ctx:
        def sb(name, shape, dt=F32):
            return ctx.enter_context(nc.sbuf_tensor(f"{tag}_{name}", shape, dt))

        def sem(name):
            return ctx.enter_context(nc.semaphore(f"{tag}_{name}"))

        sq = sb("sq", [P, KD, TOK])
        var = sb("var", [P, TOK])
        gain = sb("gain", [P, KD])
        sums = ctx.enter_context(nc.psum_tensor(f"{tag}_sums", [P, TOK], F32))
        loaded = sem("loaded")
        n_loads = 1 + len(load or [])
        squared = sem("squared")
        summed = sem("summed")
        biased = sem("biased")
        rooted = sem("rooted")
        inverted = sem("inverted")
        scaled = sem("scaled")
        high = sem("high")
        low = sem("low")
        block = ctx.enter_context(nc.Block())

        @block.sync
        def _(sp):
            for dst, src in load or []:
                sp.dma_start(dst, src).then_inc(loaded, 16)
            sp.dma_start(gain[:], gain_dram).then_inc(loaded, 16)

        @block.scalar
        def _(act):
            act.wait_ge(loaded, 16 * n_loads)
            for k in range(KD):
                act.activation(sq[:, k, :], x[:, k, :], ACT.Square).then_inc(squared, 1)
            act.wait_ge(biased, 1)
            act.activation(var[:], var[:], ACT.Sqrt).then_inc(rooted, 1)
            for k in range(KD):
                act.wait_ge(scaled, k + 1)
                act.copy(h_hi[:, k, :], h_full[:, k, :]).then_inc(high, 1)

        @block.tensor
        def _(pe):
            for k in range(KD):
                pe.wait_ge(squared, k + 1)
                ins = pe.matmul(sums[:], ones[:], sq[:, k, :], start=(k == 0), stop=(k == KD - 1))
            ins.then_inc(summed, 1)

        @block.vector
        def _(dve):
            dve.wait_ge(loaded, 16 * n_loads)
            dve.wait_ge(summed, 1)
            dve.tensor_scalar(var[:], sums[:], 1.0 / D, EPS, ALU.mult, ALU.add).then_inc(biased, 1)
            dve.wait_ge(rooted, 1)
            dve.reciprocal(var[:], var[:]).then_inc(inverted, 1)
            dve.wait_ge(inverted, 1)
            for k in range(KD):
                dve.scalar_tensor_tensor(out=h_full[:, k, :], in0=x[:, k, :], scalar=gain[:, k:k + 1],
                                         in1=var[:], op0=ALU.mult, op1=ALU.mult).then_inc(scaled, 1)
            for k in range(KD):
                dve.wait_ge(high, k + 1)
                dve.tensor_tensor(h_lo[:, k, :], h_full[:, k, :], h_hi[:, k, :].bitcast(F32),
                                  ALU.subtract).then_inc(low, 1)


def decay_rows(nc, h_full, w_ab, dt_bias, a_log, ident8, resets, rows_dram, cols):
    with ExitStack() as ctx:
        def sb(name, shape, dt=F32):
            return ctx.enter_context(nc.sbuf_tensor(f"dr_{name}", shape, dt))

        def sem(name):
            return ctx.enter_context(nc.semaphore(f"dr_{name}"))

        wab = sb("wab", [P, KD, 2 * HEADS])
        bias = sb("bias", [HEADS, 1])
        alog = sb("alog", [HEADS, 1])
        rate = sb("rate", [HEADS, 1])
        mask = sb("mask", [HEADS, TOK])
        rows = sb("rows", [HEADS, 5, TOK])
        tmp = sb("tmp", [HEADS, 6, TOK])
        ps = ctx.enter_context(nc.psum_tensor("dr_ps", [P, 3, TOK], F32))
        loaded = sem("loaded")
        stored = sem("stored")
        dve_done = Steps(sem("dve_done"), ["x", "neg_abs", "e_plus_1", "neg_rate", "part", "rest", "inv", "corr",
                                           "log1p", "pos", "softplus", "g", "gc", "last_minus",
                                           "beta_exp", "cols"])
        act_done = Steps(sem("act_done"), ["beta", "rate", "e", "ln", "egc", "elast"])
        pe_done = Steps(sem("pe_done"), ["a", "b", "turned"])
        block = ctx.enter_context(nc.Block())
        x, ax, e, u, l, g = (tmp[:, i, :] for i in range(6))
        r, d = rows[:, 3, :], rows[:, 4, :]
        gc, beta, egc, begc, elast = (rows[:, i, :] for i in range(5))

        @block.sync
        def _(sp):
            sp.dma_start(wab[:], w_ab).then_inc(loaded, 16)
            sp.dma_start(bias[:], dt_bias).then_inc(loaded, 16)
            sp.dma_start(alog[:], a_log).then_inc(loaded, 16)
            sp.dma_start(mask[:], resets).then_inc(loaded, 16)
            sp.wait_ge(act_done.sem, act_done.after("egc"))
            sp.wait_ge(dve_done.sem, dve_done.after("gc"))
            sp.dma_start(rows_dram, rows[:, 0:3, :]).then_inc(stored, 16)
            sp.wait_ge(stored, 16)

        @block.tensor
        def _(pe):
            pe_done.open(pe)
            pe.wait_ge(loaded, 64)
            for half in range(2):
                for k in range(KD):
                    ins = pe.matmul(ps[0:HEADS, half, :], wab[:, k, HEADS * half:HEADS * half + HEADS],
                                    h_full[:, k, :], start=(k == 0), stop=(k == KD - 1))
                ins.then_inc(pe_done.sem, 1)
            pe.wait_ge(dve_done.sem, dve_done.after("beta_exp"))
            pe.wait_ge(act_done.sem, act_done.after("elast"))
            for n, row in enumerate((beta, gc, begc, elast)):
                for t in range(NT):
                    at = (n * NT + t) * HEADS
                    ins = pe.transpose(ps[:, 2, at:at + HEADS], row[:, t * P:t * P + P],
                                       ident8[0:HEADS, 0:HEADS])
            ins.then_inc(pe_done.sem, 1)

        @block.scalar
        def _(act):
            act_done.open(act)
            act.wait_ge(pe_done.sem, pe_done.after("b"))
            act.activation(beta, ps[0:HEADS, 1, :], ACT.Sigmoid).then_inc(act_done.sem, 1)
            act.wait_ge(loaded, 64)
            act.activation(rate[:], alog[:], ACT.Exp).then_inc(act_done.sem, 1)
            act.wait_ge(dve_done.sem, dve_done.after("neg_abs"))
            act.activation(e, ax, ACT.Exp).then_inc(act_done.sem, 1)
            act.wait_ge(dve_done.sem, dve_done.after("e_plus_1"))
            act.activation(l, u, ACT.Ln).then_inc(act_done.sem, 1)
            act.wait_ge(dve_done.sem, dve_done.after("gc"))
            act.activation(egc, gc, ACT.Exp).then_inc(act_done.sem, 1)
            act.wait_ge(dve_done.sem, dve_done.after("last_minus"))
            act.activation(elast, ax, ACT.Exp).then_inc(act_done.sem, 1)

        @block.vector
        def _(dve):
            def own(name):
                dve.wait_ge(dve_done.sem, dve_done.after(name))

            dve_done.open(dve)
            dve.wait_ge(loaded, 64)
            dve.wait_ge(pe_done.sem, pe_done.after("a"))
            dve.tensor_scalar(x, ps[0:HEADS, 0, :], bias[:, 0:1], None, ALU.add).then_inc(dve_done.sem, 1)
            own("x")
            dve.scalar_tensor_tensor(out=ax, in0=x, scalar=-1.0, in1=x, op0=ALU.mult,
                                     op1=ALU.min).then_inc(dve_done.sem, 1)
            dve.wait_ge(act_done.sem, act_done.after("e"))
            dve.tensor_scalar(u, e, 1.0, None, ALU.add).then_inc(dve_done.sem, 1)
            dve.tensor_scalar(rate[:], rate[:], -1.0, None, ALU.mult).then_inc(dve_done.sem, 1)
            own("e_plus_1")
            dve.tensor_scalar(d, u, -1.0, None, ALU.add).then_inc(dve_done.sem, 1)
            own("part")
            dve.tensor_tensor(d, e, d, ALU.subtract).then_inc(dve_done.sem, 1)
            dve.reciprocal(r, u).then_inc(dve_done.sem, 1)
            own("inv")
            dve.tensor_tensor(d, d, r, ALU.mult).then_inc(dve_done.sem, 1)
            own("corr")
            dve.wait_ge(act_done.sem, act_done.after("ln"))
            dve.tensor_tensor(l, l, d, ALU.add).then_inc(dve_done.sem, 1)
            dve.tensor_scalar(x, x, 0.0, None, ALU.max).then_inc(dve_done.sem, 1)
            own("pos")
            dve.tensor_tensor(g, x, l, ALU.add).then_inc(dve_done.sem, 1)
            own("softplus")
            dve.tensor_scalar(g, g, rate[:, 0:1], None, ALU.mult).then_inc(dve_done.sem, 1)
            own("g")
            dve.tensor_tensor_scan(gc, mask[:], g, 0.0, ALU.mult, ALU.add).then_inc(dve_done.sem, 1)
            own("gc")
            chunks = gc.rearrange("p (c i) -> p c i", i=CH)
            dve.tensor_tensor(ax.rearrange("p (c i) -> p c i", i=CH),
                              chunks[:, :, CH - 1:CH].to_broadcast([HEADS, NCH, CH]), chunks,
                              ALU.subtract).then_inc(dve_done.sem, 1)
            dve.wait_ge(act_done.sem, act_done.after("egc"))
            dve.tensor_tensor(begc, beta, egc, ALU.mult).then_inc(dve_done.sem, 1)
            dve.wait_ge(pe_done.sem, pe_done.after("turned"))
            dve.tensor_copy(cols[:].rearrange("p a t h -> p (a t h)"),
                            ps[:, 2, 0:4 * NT * HEADS]).then_inc(dve_done.sem, 1)


def mixer_b(nc, h_hi, h_lo, w_b, conv_dram, norm_dram, rows_dram, cols, ident, ones, masks_dram, o_b):
    GROUPS = 4 * KD
    with ExitStack() as ctx:
        def sb(name, shape, dt=F32):
            return ctx.enter_context(nc.sbuf_tensor(f"mb_{name}", shape, dt))

        def sem(name):
            return ctx.enter_context(nc.semaphore(f"mb_{name}"))

        conv = sb("conv", [P, HEADS, 3, CONV])
        norm = sb("norm", [P, 1])
        biases = sb("biases", [P, 2])
        masks = sb("masks", [P, LEVELS + 2, CH])
        gc = sb("gc", [P, NT, CH])
        rows = sb("rows", [P, 2, TOK])
        y = sb("y", [P, 3, TOK])
        act_y = sb("act_y", [P, 3, TOK])
        sq = sb("sq", [P, 2, TOK])
        var = sb("var", [P, 2, TOK])
        qT = sb("qT", [P, TOK])
        kT = sb("kT", [P, TOK])
        kbT = sb("kbT", [P, TOK])
        qdT = sb("qdT", [P, TOK])
        decay = sb("decay", [P, NT, CH])
        AT = sb("AT", [P, NT, CH])
        attnT = sb("attnT", [P, NT, CH])
        prod = sb("prod", [P, NT, CH])
        T = sb("T", [P, NT, CH])
        TT = sb("TT", [P, NT, CH])
        vb = sb("vb", [P, NT, HD])
        kbe = sb("kbe", [P, NT, HD])
        kd = sb("kd", [P, NT, HD])
        nwT = sb("nwT", [P, 2, NT, CH])
        egl = sb("egl", [P, NCH])
        vn = sb("vn", [P, HD])
        S = sb("S", [P, 2, HD])
        osq = sb("osq", [P, TOK])
        ovar = sb("ovar", [P, TOK])
        o1 = sb("o1", [P, TOK])
        ps = ctx.enter_context(nc.psum_tensor("mb_ps", [P, 8, TOK], F32))
        FRONT, KEY, OUT, PAIR, LOWER = 0, 4, 5, 6, 7

        consts = sem("consts")
        passed = sem("passed")
        rows_in = sem("rows_in")
        gc_in = sem("gc_in")
        pe_front = Steps(sem("pe_front"), ["project_q", "project_k", "project_v", "sums", "project_g"])
        pe_core = Steps(sem("pe_core"),
                        ["turn_k", "gram", "AxT0", "TxP0", "AxT1", "turn_v", "TxP1"]
                        + [f"{s}{l}" for l in range(2, LEVELS) for s in ("AxT", "TxP")]
                        + ["wT"]
                        + [f"{s}{c}" for c in range(NCH) for s in ("v_new", "state", "out")
                           if (s, c) != ("state", NCH - 1)]
                        + ["out_sums"])
        w = Weights(ctx, nc, "mb", w_b, [KD] * 4, pe_front, ["project_" + t for t in "qkvg"])
        act_front = Steps(sem("act_front"), ["silu_q", "silu_k", "square_q", "square_k", "decay", "ln", "root_q",
                                             "root_k", "silu_v", "gate"])
        act_core = Steps(sem("act_core"), ["square_o", "ln_o", "root_o"])
        dve_front = Steps(sem("dve_front"), [f"conv{s}_{t}" for t in "qk" for s in range(CONV)]
                          + ["diff", "diff_masked"] + [f"conv{s}_v" for s in range(CONV)] + ["q", "k", "kb"])
        dve_core = Steps(sem("dve_core"),
                         ["A", "attn", "P0", "kbe", "T0", "TT0", "P1", "kd", "T1", "TT1", "P2", "vb", "T2", "TT2",
                          "P3", "qd", "egl", "T3", "TT3", "P4", "T4", "TT4", "P5", "TT5", "nw_even", "nw_odd"]
                         + [f"{s}{c}" for c in range(NCH) for s in ("vn", "S")
                            if (s, c) != ("S", NCH - 1)]
                         + ["o_normed", "o"])
        block = ctx.enter_context(nc.Block())
        halves = [(m, a, 2 * m + a, slice(CH * a, CH * a + CH)) for m in range(NT) for a in (0, 1)]
        BETA, GC, BEGC, ELAST = range(4)
        of = lambda bank, n: ps[:, bank, 256 * n:256 * n + 256].rearrange("p (m i) -> p m i", i=CH)
        mask = lambda n: masks[:, n:n + 1, :].to_broadcast([P, NT, CH])
        at_chunk = lambda c: slice(c * CH, c * CH + CH)

        @block.sync
        def _(sp):
            sp.dma_start(conv[:], conv_dram).then_inc(consts, 16)
            sp.dma_start(norm[:], norm_dram).then_inc(consts, 16)
            sp.dma_start(masks[:], masks_dram).then_inc(consts, 16)
            with sp.Fori(0, HEADS) as f:
                w.load(sp, f)
                head = rows_dram[bass.ds(f, 1), :, :]
                sp.wait_ge(dve_front.sem, dve_front.after("diff", f - 1))
                for a in (0, 1):
                    src = head[:, 0, :].rearrange("x (m a i) -> x m a i", a=2, i=CH)[:, :, a, :]
                    sp.dma_start(gc[CH * a:CH * a + CH, :, :], src.rearrange("x m i -> (x m) i").partition_broadcast(CH)) \
                        .then_inc(gc_in, 16)
                sp.wait_ge(dve_core.sem, dve_core.after("egl", f - 1))
                sp.dma_start(rows[:], head[:, 1:3, :].rearrange("x r t -> (x r) t").partition_broadcast(P)).then_inc(rows_in, 16)

        @block.gpsimd
        def _(pool):
            w.lo_made.open(pool)
            with pool.Fori(0, HEADS) as f:
                w.low(pool, f)

        @block.scalar
        def _(act):
            def front(f, prepare):
                for n, t in enumerate("qk"):
                    act.wait_ge(dve_front.sem, dve_front.after(f"conv{CONV - 1}_{t}", f))
                    act.activation(act_y[:, n, :], y[:, n, :], ACT.Silu).then_inc(act_front.sem, 1)
                for n, t in enumerate("qk"):
                    act.wait_ge(act_front.sem, act_front.after(f"silu_{t}", f))
                    act.activation(sq[:, n, :], act_y[:, n, :], ACT.Square).then_inc(act_front.sem, 1)
                if prepare is not None:
                    w.high(act, prepare, (0, 1))
                act.wait_ge(dve_front.sem, dve_front.after("diff_masked", f))
                act.activation(decay[:], decay[:], ACT.Exp).then_inc(act_front.sem, 1)
                act.wait_ge(pe_front.sem, pe_front.after("sums", f))
                act.activation(var[:], ps[:, FRONT:FRONT + 2, :], ACT.Ln, bias=biases[:, 0:1]).then_inc(act_front.sem, 1)
                act.wait_ge(act_front.sem, act_front.after("ln", f))
                act.activation(var[:, 0, :], var[:, 0, :], ACT.Exp, bias=biases[:, 1:2], scale=-0.5).then_inc(act_front.sem, 1)
                act.activation(var[:, 1, :], var[:, 1, :], ACT.Exp, scale=-0.5).then_inc(act_front.sem, 1)
                act.wait_ge(dve_front.sem, dve_front.after(f"conv{CONV - 1}_v", f))
                act.activation(act_y[:, 2, :], y[:, 2, :], ACT.Silu).then_inc(act_front.sem, 1)
                act.wait_ge(pe_front.sem, pe_front.after("project_g", f))
                act.activation(o_b[:, bass.ds(f, 1), :].rearrange("p a t -> p (a t)"), ps[:, FRONT + 3, :],
                               ACT.Silu).then_inc(act_front.sem, 1)
                if prepare is not None:
                    w.high(act, prepare, (2, 3))

            def core(h):
                act.wait_ge(pe_core.sem, pe_core.after(f"out{NCH - 1}", h))
                act.activation(osq[:], ps[:, OUT, :], ACT.Square).then_inc(act_core.sem, 1)
                act.wait_ge(pe_core.sem, pe_core.after("out_sums", h))
                act.activation(ovar[:], ps[:, LOWER, :], ACT.Ln, bias=biases[:, 0:1], scale=1.0 / HD).then_inc(act_core.sem, 1)
                act.wait_ge(act_core.sem, act_core.after("ln_o", h))
                act.activation(ovar[:], ovar[:], ACT.Exp, scale=-0.5).then_inc(act_core.sem, 1)

            w.hi_made.open(act)
            act_front.open(act)
            act_core.open(act)
            act.wait_ge(consts, 50)
            w.high(act, 0)
            front(0, 1)
            with act.Fori(0, HEADS - 2) as h:
                front(h + 1, h + 2)
                core(h)
            front(HEADS - 1, None)
            core(HEADS - 2)
            core(HEADS - 1)

        @block.tensor
        def _(pe):
            def sums(f):
                pe.wait_ge(act_front.sem, act_front.after("square_k", f))
                pe.matmul(ps[:, FRONT, :], ones[:], sq[:, 0, :], start=True, stop=True)
                pe.matmul(ps[:, FRONT + 1, :], ones[:], sq[:, 1, :], start=True, stop=True).then_inc(pe_front.sem, 1)

            class Projection:

                def __init__(self, f):
                    self.f, self.n = f, 0

                def go(self, count):
                    for _ in range(count if self.f is not None else 0):
                        m, k = divmod(self.n, KD)
                        if self.n == 0:
                            pe.wait_ge(act_front.sem, act_front.after("gate", self.f - 1))
                        ins = w.block(pe, self.f, m, k, ps[:, FRONT + m, :], h_hi, h_lo)
                        if k == KD - 1:
                            ins.then_inc(pe_front.sem, 1)
                        self.n += 1

            def core(h, f):
                fill = Projection(f)

                def dve(name):
                    pe.wait_ge(dve_core.sem, dve_core.after(name, h))
                    pe.sem_inc(passed, 1)

                pe.wait_ge(dve_front.sem, dve_front.after("kb", h))
                pe.sem_inc(passed, 1)
                for t in range(NT):
                    ins = pe.transpose(ps[:, KEY, P * t:P * t + P], kT[:, P * t:P * t + P], ident[:])
                ins.then_inc(pe_core.sem, 1)
                for m, a, c, half in halves:
                    pe.matmul(of(PAIR, 0)[half, m, :], kT[:, at_chunk(c)], kbT[:, at_chunk(c)], start=True, stop=True)
                for m, a, c, half in halves:
                    ins = pe.matmul(of(PAIR, 1)[half, m, :], kT[:, at_chunk(c)], qT[:, at_chunk(c)], start=True, stop=True)
                ins.then_inc(pe_core.sem, 1)
                fill.go(2)
                for l in range(LEVELS):
                    dve("A" if l == 0 else f"TT{l - 1}")
                    for m, a, c, half in halves:
                        x = masks[half, LEVELS + 1, :] if l == 0 else T[half, m, :]
                        ins = pe.matmul(of(LOWER, 0)[half, m, :], AT[half, m, :], x, start=True, stop=True)
                    ins.then_inc(pe_core.sem, 1)
                    fill.go(1)
                    if l == 1:
                        pe.wait_ge(dve_core.sem, dve_core.after("o_normed", h - 1))
                        pe.wait_ge(act_front.sem, act_front.after("silu_v", h))
                        pe.sem_inc(passed, 1)
                        for t in range(NT):
                            ins = pe.transpose(ps[:, OUT, P * t:P * t + P], act_y[:, 2, P * t:P * t + P], ident[:])
                        ins.then_inc(pe_core.sem, 1)
                    dve(f"P{l}")
                    for m, a, c, half in halves:
                        tt = masks[half, LEVELS + 1, :] if l == 0 else TT[half, m, :]
                        ins = pe.matmul(of(PAIR, 1)[half, m, :], prod[half, m, :], tt, start=True, stop=True)
                    if l < LEVELS - 1:
                        for m, a, c, half in halves:
                            tt = masks[half, LEVELS + 1, :] if l == 0 else TT[half, m, :]
                            ins = pe.matmul(of(PAIR, 0)[half, m, :], tt, prod[half, m, :], start=True, stop=True)
                    ins.then_inc(pe_core.sem, 1)
                    fill.go(2 if l < 2 else 1)
                dve(f"TT{LEVELS - 1}")
                for m, a, c, half in halves:
                    ins = pe.matmul(of((KEY, LOWER)[a], 0)[:, m, :], kbe[half, m, :], TT[half, m, :], start=True,
                                    stop=True)
                ins.then_inc(pe_core.sem, 1)
                fill.go(1)
                dve("nw_odd")
                for m, a, c, half in halves:
                    state = S[:, c % 2, :]
                    bank = PAIR + c % 2
                    ins = pe.matmul(ps[half, bank, 0:HD], TT[half, m, :], vb[half, m, :], start=True, stop=(c == 0))
                    if c == 0:
                        ins.then_inc(pe_core.sem, 1)
                    else:
                        dve(f"S{c - 1}")
                        pe.matmul(ps[half, bank, 0:HD], nwT[:, a, m, :], state, start=False,
                                  stop=True).then_inc(pe_core.sem, 1)
                        pe.matmul(ps[:, OUT, at_chunk(c)], state, qdT[:, at_chunk(c)], start=True, stop=False)
                    fill.go(1)
                    dve(f"vn{c}")
                    if c < NCH - 1:
                        pe.matmul(ps[:, KEY, HD * (c % 2):HD * (c % 2) + HD], kd[half, m, :], vn[half, :], start=True,
                                  stop=True).then_inc(pe_core.sem, 1)
                    pe.matmul(ps[:, OUT, at_chunk(c)], vn[half, :], attnT[half, m, :], start=(c == 0),
                              stop=True).then_inc(pe_core.sem, 1)
                    if c < NCH - 1:
                        if c == 3 and f is not None:
                            sums(f)
                        fill.go(1)
                assert f is None or fill.n == GROUPS
                pe.wait_ge(act_core.sem, act_core.after("square_o", h))
                pe.matmul(ps[:, LOWER, :], ones[:], osq[:], start=True, stop=True).then_inc(pe_core.sem, 1)

            pe_front.open(pe)
            pe_core.open(pe)
            first = Projection(0)
            first.go(3 * KD)
            sums(0)
            first.go(KD)
            with pe.Fori(0, HEADS - 1) as h:
                core(h, h + 1)
            core(HEADS - 1, None)

        @block.vector
        def _(dve):
            def own_front(name, f):
                dve.wait_ge(dve_front.sem, dve_front.after(name, f))

            def tap(f, t, s):
                if f is None:
                    return
                n = "qkv".index(t)
                x = conv[:, bass.ds(f, 1), n, CONV - 1 - s:CONV - s].rearrange("p a b -> p (a b)")
                if s == 0:
                    dve.wait_ge(pe_front.sem, pe_front.after(f"project_{t}", f))
                    dve.tensor_scalar(y[:, n, :], ps[:, FRONT + n, :], x, None, ALU.mult).then_inc(dve_front.sem, 1)
                else:
                    own_front(f"conv{s - 1}_{t}", f)
                    dve.scalar_tensor_tensor(out=y[:, n, s:], in0=ps[:, FRONT + n, :TOK - s], scalar=x, in1=y[:, n, s:],
                                             op0=ALU.mult, op1=ALU.add).then_inc(dve_front.sem, 1)

            def head_col(h, kind, width):
                return cols[:, kind, :, bass.ds(h, 1)].to_broadcast([P, NT, width])

            def diff(f):
                if f is None:
                    return
                dve.wait_ge(gc_in, 32 * (f + 1))
                dve.tensor_tensor(decay[:], gc[:], head_col(f, GC, CH), ALU.subtract).then_inc(dve_front.sem, 1)

            def diff_masked(f):
                if f is None:
                    return
                own_front("diff", f)
                dve.tensor_tensor(decay[:], decay[:], mask(LEVELS), ALU.add).then_inc(dve_front.sem, 1)

            def normed(f, t):
                if f is None:
                    return
                dve.wait_ge(act_front.sem, act_front.after(f"root_{t}", f))
                n = "qk".index(t)
                dve.tensor_tensor((qT, kT)[n][:], act_y[:, n, :], var[:, n, :], ALU.mult).then_inc(dve_front.sem, 1)

            def beta_keys(f):
                if f is None:
                    return
                own_front("k", f)
                dve.wait_ge(rows_in, 16 * (f + 1))
                dve.tensor_tensor(kbT[:], kT[:], rows[:, 0, :], ALU.mult).then_inc(dve_front.sem, 1)

            def core(h, f):
                done = dve_core.sem

                def pe(name):
                    dve.wait_ge(pe_core.sem, pe_core.after(name, h))

                four = lambda bank: ps[:, bank, :].rearrange("p (m e) -> p m e", e=HD)
                pe("gram")
                dve.wait_ge(act_front.sem, act_front.after("decay", h))
                dve.tensor_tensor(AT[:], of(PAIR, 0), decay[:], ALU.mult).then_inc(done, 1)
                dve.tensor_tensor(attnT[:], of(PAIR, 1), decay[:], ALU.mult).then_inc(done, 1)
                for l in range(LEVELS):
                    pe(f"AxT{l}")
                    dve.tensor_tensor(prod[:], of(LOWER, 0), mask(l), ALU.mult).then_inc(done, 1)
                    if l == 0:
                        dve.tensor_tensor(kbe[:], four(KEY), head_col(h, BEGC, HD), ALU.mult).then_inc(done, 1)
                    if l == 1:
                        dve.tensor_tensor(kd[:], four(KEY), head_col(h, ELAST, HD), ALU.mult).then_inc(done, 1)
                    if l == 2:
                        pe("turn_v")
                        dve.tensor_tensor(vb[:], four(OUT), head_col(h, BETA, HD), ALU.mult).then_inc(done, 1)
                    if l == 3:
                        dve.tensor_tensor(qdT[:], qT[:], rows[:, 1, :], ALU.mult).then_inc(done, 1)
                        dve.tensor_copy(egl[:], rows[:, 1, CH - 1:TOK:CH]).then_inc(done, 1)
                    if l >= 4:
                        tap(f, "q", l - 4)
                    pe(f"TxP{l}")
                    if l < LEVELS - 1:
                        dve.tensor_tensor(T[:], mask(LEVELS + 1) if l == 0 else T[:], of(PAIR, 0),
                                          ALU.subtract).then_inc(done, 1)
                    dve.tensor_tensor(TT[:], mask(LEVELS + 1) if l == 0 else TT[:], of(PAIR, 1),
                                      ALU.subtract).then_inc(done, 1)
                tap(f, "q", 2)
                pe("wT")
                for a, bank in enumerate((KEY, LOWER)):
                    dve.tensor_scalar(nwT[:, a], of(bank, 0), -1.0, None, ALU.mult).then_inc(done, 1)
                fillers = [[lambda: tap(f, "q", 3), lambda: tap(f, "k", 0)],
                           [lambda: tap(f, "k", 1), lambda: tap(f, "k", 2)],
                           [lambda: tap(f, "k", 3), lambda: diff(f)],
                           [lambda: diff_masked(f), lambda: None],
                           [lambda: tap(f, "v", 0), lambda: tap(f, "v", 1)],
                           [lambda: tap(f, "v", 2), lambda: tap(f, "v", 3)],
                           [lambda: normed(f, "q"), lambda: normed(f, "k")],
                           [lambda: beta_keys(f), lambda: None]]
                for m, a, c, half in halves:
                    pe(f"v_new{c}")
                    dve.tensor_copy(vn[half, :], ps[half, PAIR + c % 2, 0:HD]).then_inc(done, 1)
                    fillers[c][0]()
                    state = ps[:, KEY, HD * (c % 2):HD * (c % 2) + HD]
                    if c == 0:
                        pe("state0")
                        dve.tensor_copy(S[:, 1, :], state).then_inc(done, 1)
                    elif c < NCH - 1:
                        pe(f"state{c}")
                        dve.scalar_tensor_tensor(out=S[:, (c + 1) % 2, :], in0=S[:, c % 2, :],
                                                 scalar=egl[:, c:c + 1], in1=state,
                                                 op0=ALU.mult, op1=ALU.add).then_inc(done, 1)
                    fillers[c][1]()
                dve.wait_ge(act_core.sem, act_core.after("root_o", h))
                dve.tensor_tensor(o1[:], ps[:, OUT, :], ovar[:], ALU.mult).then_inc(done, 1)
                dve.wait_ge(done, dve_core.after("o_normed", h))
                at = o_b[:, bass.ds(h, 1), :].rearrange("p a t -> p (a t)")
                dve.scalar_tensor_tensor(out=at, in0=o1[:], scalar=norm[:, 0:1], in1=at, op0=ALU.mult,
                                         op1=ALU.mult).then_inc(done, 1)

            dve_front.open(dve)
            dve_core.open(dve)
            dve.memset(biases[:, 0:1], EPS).then_inc(consts, 1)
            dve.memset(biases[:, 1:2], -0.5 * math.log(HD)).then_inc(consts, 1)
            dve.wait_ge(consts, 50)
            for t in "qk":
                for s in range(CONV):
                    tap(0, t, s)
            diff(0)
            diff_masked(0)
            for s in range(CONV):
                tap(0, "v", s)
            normed(0, "q")
            normed(0, "k")
            beta_keys(0)
            with dve.Fori(0, HEADS - 1) as h:
                core(h, h + 1)
            core(HEADS - 1, None)


def mixer_a(nc, h_hi, h_lo, w_a, bias_dram, gains_dram, ident, halves, o_a):
    HW = 64
    with ExitStack() as ctx:
        def sb(name, shape, dt=F32):
            return ctx.enter_context(nc.sbuf_tensor(f"ma_{name}", shape, dt))

        def sem(name):
            return ctx.enter_context(nc.semaphore(f"ma_{name}"))

        gains = sb("gains", [P, 2])
        bias = sb("bias", [P, 2, TOK])
        sq = sb("sq", [P, 2, TOK])
        var = sb("var", [P, 2, TOK])
        q = sb("q", [P, TOK])
        kk = sb("k", [P, TOK])
        vT = sb("vT", [P, TOK])
        v = sb("v", [P, NT, P])
        sc = sb("sc", [P, 2, NT, TOK])
        top = sb("top", [P, 2, NT])
        total = sb("total", [P, 2, NT])
        pT = sb("pT", [P, 2, NT, TOK])
        ps = ctx.enter_context(nc.psum_tensor("ma_ps", [P, 8, TOK], F32))
        consts = sem("consts")
        passed = sem("passed")
        bias_in = sem("bias_in")
        bias_masked = sem("bias_masked")
        T = range(NT)
        pe_done = Steps(sem("pe_done"), ["q", "k", "v", "sums", "turn_v"]
                        + [f"{n}" for a in (0, 1) for n in [f"score{a}{t}" for t in T] + [f"turn{a}{b}" for b in T]
                           + [f"pv{a}"]])
        w = Weights(ctx, nc, "ma", w_a, [KD, KD, KD], pe_done, ["q", "k", "v"])
        act_done = Steps(sem("act_done"), ["sq_q", "sq_k", "v", "root"]
                         + [n for a in (0, 1) for n in [f"exp{a}{t}" for t in T] + [f"pT{a}{b}" for b in T]])
        dve_done = Steps(sem("dve_done"), ["var", "inv", "q", "k", "v"]
                         + [n for a in (0, 1) for n in [f"{s}{a}{t}" for t in T for s in ("sc", "top")]
                            + [f"{s}{a}{t}" for t in T for s in ("inv", "p")] + [f"o{a}"]])
        block = ctx.enter_context(nc.Block())
        TURNS = HEADS // 2
        half = lambda a: slice(HW * a, HW * a + HW)
        width = lambda t: P * (t + 1)

        @block.sync
        def _(sp):
            sp.dma_start(gains[:], gains_dram).then_inc(consts, 16)
            with sp.Fori(0, TURNS) as j:
                sp.wait_ge(dve_done.sem, dve_done.after(f"sc1{NT - 1}", j - 1))
                sp.dma_start(bias[:], bias_dram[bass.ds(j, 1), :, :, :].rearrange("a p h t -> (a p) h t")).then_inc(bias_in, 16)
                w.load(sp, j)

        @block.gpsimd
        def _(pool):
            w.lo_made.open(pool)
            with pool.Fori(0, TURNS) as j:
                pool.wait_ge(bias_in, 16 * (j + 1))
                pool.sem_inc(passed, 1)
                pool.memset(bias[0:CH, :, TOK - CH:TOK], NEG).then_inc(bias_masked, 1)
                w.low(pool, j)

        @block.scalar
        def _(act):
            w.hi_made.open(act)
            act_done.open(act)
            with act.Fori(0, TURNS) as j:
                w.high(act, j)
                for n, t in enumerate("qk"):
                    act.wait_ge(pe_done.sem, pe_done.after(t, j))
                    act.activation(sq[:, n, :], ps[:, n, :], ACT.Square).then_inc(act_done.sem, 1)
                act.wait_ge(pe_done.sem, pe_done.after("v", j))
                act.copy(vT[:], ps[:, 2, :]).then_inc(act_done.sem, 1)
                act.wait_ge(dve_done.sem, dve_done.after("var", j))
                act.activation(var[:], var[:], ACT.Sqrt).then_inc(act_done.sem, 1)
                for a in (0, 1):
                    for t in T:
                        act.wait_ge(dve_done.sem, dve_done.after(f"top{a}{t}", j))
                        act.activation(sc[:, a, t, 0:width(t)], sc[:, a, t, 0:width(t)], ACT.Exp,
                                       bias=top[:, a, t:t + 1],
                                       accum_out=total[:, a, t:t + 1]).then_inc(act_done.sem, 1)
                    for b in T:
                        act.wait_ge(pe_done.sem, pe_done.after(f"turn{a}{b}", j))
                        act.copy(pT[:, a, b, P * b:TOK], ps[:, b % 2, P * b:TOK]).then_inc(act_done.sem, 1)

        @block.tensor
        def _(pe):
            pe_done.open(pe)
            pe.wait_ge(consts, 16)
            with pe.Fori(0, TURNS) as j:
                def dve(name):
                    pe.wait_ge(dve_done.sem, dve_done.after(name, j))
                    pe.sem_inc(passed, 1)

                def act(name):
                    pe.wait_ge(act_done.sem, act_done.after(name, j))
                    pe.sem_inc(passed, 1)

                for m in range(3):
                    if m == 2:
                        pe.wait_ge(dve_done.sem, dve_done.after("o1", j - 1))
                    w.product(pe, j, m, ps[:, m, :], h_hi, h_lo).then_inc(pe_done.sem, 1)
                act("sq_k")
                pe.matmul(ps[:, 3, :], halves[:], sq[:, 0, :], start=True, stop=True)
                pe.matmul(ps[:, 4, :], halves[:], sq[:, 1, :], start=True, stop=True).then_inc(pe_done.sem, 1)
                act("v")
                for t in T:
                    ins = pe.transpose(ps[:, 5, P * t:P * t + P], vT[:, P * t:P * t + P], ident[:])
                ins.then_inc(pe_done.sem, 1)
                dve("v")
                for a in (0, 1):
                    for t in T:
                        if a == 1:
                            dve(f"sc0{t}")
                        pe.matmul(ps[:, 4 + t, 0:width(t)], q[half(a), P * t:P * t + P], kk[half(a), 0:width(t)],
                                  start=True, stop=True).then_inc(pe_done.sem, 1)
                    for b in T:
                        if b >= 2:
                            act(f"pT{a}{b - 2}")
                        for t in range(b, NT):
                            if b == 0:
                                dve(f"p{a}{t}")
                            ins = pe.transpose(ps[:, b % 2, P * t:P * t + P], sc[:, a, t, P * b:P * b + P], ident[:])
                        ins.then_inc(pe_done.sem, 1)
                    for b in T:
                        act(f"pT{a}{b}")
                        ins = pe.matmul(ps[:, 2 + a, P * b:TOK], v[:, b, :], pT[:, a, b, P * b:TOK], start=(b == 0),
                                        stop=(b == NT - 1))
                    ins.then_inc(pe_done.sem, 1)

        @block.vector
        def _(dve):
            dve_done.open(dve)
            dve.wait_ge(consts, 16)
            with dve.Fori(0, TURNS) as j:
                done = dve_done.sem

                def own(name):
                    dve.wait_ge(done, dve_done.after(name, j))

                def pe(name):
                    dve.wait_ge(pe_done.sem, pe_done.after(name, j))

                pe("sums")
                dve.tensor_scalar(var[:], ps[:, 3:5, :], 1.0 / HW, EPS, ALU.mult, ALU.add).then_inc(done, 1)
                dve.wait_ge(act_done.sem, act_done.after("root", j))
                dve.reciprocal(var[:], var[:]).then_inc(done, 1)
                own("inv")
                dve.scalar_tensor_tensor(out=q[:], in0=ps[:, 0, :], scalar=gains[:, 0:1], in1=var[:, 0, :],
                                         op0=ALU.mult, op1=ALU.mult).then_inc(done, 1)
                dve.scalar_tensor_tensor(out=kk[:], in0=ps[:, 1, :], scalar=gains[:, 1:2], in1=var[:, 1, :],
                                         op0=ALU.mult, op1=ALU.mult).then_inc(done, 1)
                pe("turn_v")
                dve.tensor_copy(v[:].rearrange("p t c -> p (t c)"), ps[:, 5, :]).then_inc(done, 1)
                dve.wait_ge(bias_masked, j + 1)
                for a in (0, 1):
                    for t in T:
                        s_t = sc[:, a, t, 0:width(t)]
                        pe(f"score{a}{t}")
                        dve.scalar_tensor_tensor(out=s_t, in0=ps[:, 4 + t, 0:width(t)], scalar=HW ** -0.5,
                                                 in1=bias[:, a, TOK - width(t):TOK], op0=ALU.mult,
                                                 op1=ALU.add).then_inc(done, 1)
                        own(f"sc{a}{t}")
                        dve.tensor_reduce(top[:, a, t:t + 1], s_t, AX.X, ALU.max, negate=True).then_inc(done, 1)
                    for t in T:
                        s_t = sc[:, a, t, 0:width(t)]
                        dve.wait_ge(act_done.sem, act_done.after(f"exp{a}{t}", j))
                        dve.reciprocal(total[:, a, t:t + 1], total[:, a, t:t + 1]).then_inc(done, 1)
                        own(f"inv{a}{t}")
                        dve.tensor_scalar(s_t, s_t, total[:, a, t:t + 1], None, ALU.mult).then_inc(done, 1)
                    pe(f"pv{a}")
                    dve.tensor_copy(o_a[half(a), bass.ds(j, 1), :].rearrange("p a t -> p (a t)"),
                                    ps[half(a), 2 + a, :]).then_inc(done, 1)


def merge(nc, tag, w_dram, pieces, h_hi, h_lo, o_a, ob, b_merge_dram, mixed_hi, mixed_lo):
    with ExitStack() as ctx:
        def sb(name, shape, dt=F32):
            return ctx.enter_context(nc.sbuf_tensor(f"{tag}_{name}", shape, dt))

        def sem(name):
            return ctx.enter_context(nc.semaphore(f"{tag}_{name}"))

        NA = A_W // P
        oa_parts = sb("oa_parts", [P, 2, NA, TOK], F32R)
        ob_parts = sb("ob_parts", [P, 2, KD, TOK], F32R)
        b_merge = sb("b_merge", [P, 2, KD])
        gates = sb("gates", [P, 2, TOK])
        full = sb("full", [P, TOK])
        ps = ctx.enter_context(nc.psum_tensor(f"{tag}_ps", [P, 4, TOK], F32))
        loaded = sem("loaded")
        x_hi = sem("x_hi")
        x_lo = sem("x_lo")
        pe_done = Steps(sem("pe_done"), ["gate_a", "gate_b", "proj_a", "proj_b"])
        w = Weights(ctx, nc, tag, w_dram, pieces, pe_done, ["gate_a", "gate_b", "proj_a", "proj_b"])
        act_done = Steps(sem("act_done"), ["gate_a", "gate_b", "high"])
        dve_done = Steps(sem("dve_done"), ["part_a", "part_b", "sum", "low"])
        block = ctx.enter_context(nc.Block())

        @block.sync
        def _(sp):
            sp.dma_start(b_merge[:], b_merge_dram).then_inc(loaded, 16)
            with sp.Fori(0, KD) as n:
                w.load(sp, n)

        @block.gpsimd
        def _(pool):
            w.lo_made.open(pool)
            with pool.Fori(0, KD) as n:
                w.low(pool, n)

        @block.scalar
        def _(act):
            w.hi_made.open(act)
            act_done.open(act)
            act.wait_ge(loaded, 16)

            def turn(n, last=False):
                for g, name in enumerate(("gate_a", "gate_b")):
                    act.wait_ge(pe_done.sem, pe_done.after(name, n))
                    act.activation(gates[:, g, :], ps[:, g, :], ACT.Sigmoid,
                                   bias=b_merge[:, g, bass.ds(n, 1)]).then_inc(act_done.sem, 1)
                    if not last:
                        w.high(act, n + 1, [g])
                if not last:
                    w.high(act, n + 1, [2, 3])
                act.wait_ge(dve_done.sem, dve_done.after("sum", n))
                act.copy(mixed_hi[:, bass.ds(n, 1), :].rearrange("p a t -> p (a t)"), full[:]).then_inc(act_done.sem, 1)

            w.high(act, 0, [0, 1])
            act.copy(oa_parts[:, 0, :, :], o_a[:]).then_inc(x_hi, 1)
            act.copy(ob_parts[:, 0, :, :], ob[:]).then_inc(x_hi, 1)
            w.high(act, 0, [2, 3])
            with act.Fori(0, KD - 1) as n:
                turn(n)
            turn(KD - 1, last=True)

        @block.tensor
        def _(pe):
            pe_done.open(pe)
            with pe.Fori(0, KD) as n:
                w.product(pe, n, 0, ps[:, 0, :], h_hi, h_lo).then_inc(pe_done.sem, 1)
                w.product(pe, n, 1, ps[:, 1, :], h_hi, h_lo).then_inc(pe_done.sem, 1)
                pe.wait_ge(x_lo, 2)
                pe.wait_ge(dve_done.sem, dve_done.after("part_b", n - 1))
                w.product(pe, n, 2, ps[:, 2, :], oa_parts[:, 0, :, :], oa_parts[:, 1, :, :]).then_inc(pe_done.sem, 1)
                w.product(pe, n, 3, ps[:, 3, :], ob_parts[:, 0, :, :], ob_parts[:, 1, :, :]).then_inc(pe_done.sem, 1)

        @block.vector
        def _(dve):
            dve_done.open(dve)
            dve.wait_ge(x_hi, 2)
            dve.tensor_tensor(oa_parts[:, 1, :, :], o_a[:], oa_parts[:, 0, :, :].bitcast(F32), ALU.subtract).then_inc(x_lo, 1)
            dve.tensor_tensor(ob_parts[:, 1, :, :], ob[:], ob_parts[:, 0, :, :].bitcast(F32), ALU.subtract).then_inc(x_lo, 1)
            with dve.Fori(0, KD) as n:
                for g, name in enumerate(("gate_a", "gate_b")):
                    dve.wait_ge(pe_done.sem, pe_done.after("proj" + name[4:], n))
                    dve.wait_ge(act_done.sem, act_done.after(name, n))
                    dve.tensor_tensor(gates[:, g, :], gates[:, g, :], ps[:, 2 + g, :], ALU.mult).then_inc(dve_done.sem, 1)
                dve.wait_ge(dve_done.sem, dve_done.after("part_b", n))
                dve.tensor_tensor(full[:], gates[:, 0, :], gates[:, 1, :], ALU.add).then_inc(dve_done.sem, 1)
                dve.wait_ge(act_done.sem, act_done.after("high", n))
                at = bass.ds(n, 1)
                dve.tensor_tensor(mixed_lo[:, at, :].rearrange("p a t -> p (a t)"), full[:],
                                  mixed_hi[:, at, :].bitcast(F32).rearrange("p a t -> p (a t)"),
                                  ALU.subtract).then_inc(dve_done.sem, 1)


def project_out(nc, w_dram, mixed_hi, mixed_lo, xT):
    with ExitStack() as ctx:
        sem = lambda name: ctx.enter_context(nc.semaphore(f"po_{name}"))
        ps = ctx.enter_context(nc.psum_tensor("po_ps", [P, 2, TOK], F32))
        made = Steps(sem("made"), range(2))
        added = Steps(sem("added"), range(2))
        w = Weights(ctx, nc, "po", w_dram, [KD, KD], made, range(2))
        block = ctx.enter_context(nc.Block())
        TURNS = KD // 2

        @block.sync
        def _(sp):
            with sp.Fori(0, TURNS) as n:
                w.load(sp, n)

        @block.gpsimd
        def _(pool):
            w.lo_made.open(pool)
            with pool.Fori(0, TURNS) as n:
                w.low(pool, n)

        @block.scalar
        def _(act):
            w.hi_made.open(act)
            with act.Fori(0, TURNS) as n:
                w.high(act, n)

        @block.tensor
        def _(pe):
            made.open(pe)
            with pe.Fori(0, TURNS) as n:
                for m in range(2):
                    pe.wait_ge(added.sem, added.after(m, n - 1))
                    w.product(pe, n, m, ps[:, m, :], mixed_hi, mixed_lo).then_inc(made.sem, 1)

        @block.vector
        def _(dve):
            added.open(dve)
            with dve.Fori(0, TURNS) as n:
                for m in range(2):
                    x = xT[:, bass.ds(2 * n + m, 1), :].rearrange("p a t -> p (a t)")
                    dve.wait_ge(made.sem, made.after(m, n))
                    dve.tensor_tensor(x, x, ps[:, m, :], ALU.add).then_inc(added.sem, 1)


KEYS = 128
TOP = 16


def choose_experts(nc, w_dram, keys_dram, iota_dram, h_hi, h_lo, sel):
    with ExitStack() as ctx:
        def sb(name, shape, dt=F32):
            return ctx.enter_context(nc.sbuf_tensor(f"ce_{name}", shape, dt))

        def sem(name):
            return ctx.enter_context(nc.semaphore(f"ce_{name}"))

        keys = sb("keys", [P, 2, KEYS])
        iota = sb("iota", [P, TOP])
        q = sb("q", [P, 2, TOK])
        s = sb("s", [P, 2, NT, KEYS])
        rest = sb("rest", [P, 2, NT, KEYS])
        best = sb("best", [P, 2, NT, TOP])
        place = sb("place", [P, 2, NT, TOP], U32)
        place_f = sb("place_f", [P, 2, NT, TOP])
        cand = sb("cand", [P, NT, TOP * TOP])
        cand_rest = sb("cand_rest", [P, NT, TOP * TOP])
        top = sb("top", [P, NT, TOP])
        pos = sb("pos", [P, NT, TOP], U32)
        pos_part = sb("pos_part", [P, 2, NT, TOP], U32)
        pos_f = sb("pos_f", [P, 2, NT, TOP])
        hot = sb("hot", [P, 2, NT * TOP, TOP])
        e = sb("e", [P, NT, HEADS, TOP])
        total = sb("total", [P, NT, HEADS])
        ps = ctx.enter_context(nc.psum_tensor("ce_ps", [P, 4, TOK], F32))
        consts = sem("consts")
        keys_in = sem("keys_in")
        passed = sem("passed")
        pe_done = Steps(sem("pe_done"), ["q0", "q1", "s0", "s1"])
        w = Weights(ctx, nc, "ce", w_dram, [KD, KD], pe_done, ["q0", "q1"])
        act_done = Steps(sem("act_done"), ["q0", "q1", "s0", "s1"])
        exp_made = sem("exp_made")
        softmax = sem("softmax")
        dve_done = Steps(sem("dve_done"), ["max1", "at1", "drop", "max2", "at2", "index0", "index1", "place_f", "cand", "cmax1", "cat1",
                                           "cdrop", "cmax2", "cat2", "row", "col", "pos_f", "hot0", "hot1", "minus"])
        pool_done = Steps(sem("pool_done"), ["pick0", "pick1"])
        block = ctx.enter_context(nc.Block())

        @block.sync
        def _(sp):
            sp.dma_start(iota[:], iota_dram).then_inc(consts, 16)
            with sp.Fori(0, HEADS) as h:
                w.load(sp, h)
                sp.wait_ge(pe_done.sem, pe_done.after("s1", h - 1))
                sp.dma_start(keys[:], keys_dram[bass.ds(h, 1), :, :, :].rearrange("a p s k -> (a p) s k")).then_inc(keys_in, 16)

        @block.gpsimd
        def _(pool):
            w.lo_made.open(pool)
            pool_done.open(pool)

            def turn(h, last=False):
                if not last:
                    w.low(pool, h + 1)
                for m in (0, 1):
                    four = hot[:, m, :, :].rearrange("p (t k) r -> p t k r", t=NT)
                    pool.wait_ge(dve_done.sem, dve_done.after(f"hot{m}", h))
                    pool.sem_inc(passed, 1)
                    pool.tensor_tensor(four, four, place_f[:, m, :, :].unsqueeze(2).to_broadcast([P, NT, TOP, TOP]),
                                       ALU.mult).then_inc(pool_done.sem, 1)

            w.low(pool, 0)
            with pool.Fori(0, HEADS - 1) as h:
                turn(h)
            turn(HEADS - 1, last=True)

        @block.scalar
        def _(act):
            w.hi_made.open(act)
            act_done.open(act)

            def turn(h, last=False):
                for m in (0, 1):
                    act.wait_ge(pe_done.sem, pe_done.after(f"q{m}", h))
                    act.copy(q[:, m, :], ps[:, m, :]).then_inc(act_done.sem, 1)
                    if not last:
                        w.high(act, h + 1, [m])
                act.wait_ge(dve_done.sem, dve_done.after("drop", h - 1))
                for m in (0, 1):
                    act.wait_ge(pe_done.sem, pe_done.after(f"s{m}", h))
                    act.copy(s[:, m, :, :].rearrange("p t k -> p (t k)"), ps[:, 2 + m, :]).then_inc(act_done.sem, 1)

            w.high(act, 0)
            with act.Fori(0, HEADS - 1) as h:
                turn(h)
            turn(HEADS - 1, last=True)
            act.wait_ge(dve_done.sem, dve_done.after("minus", HEADS - 1))
            act.activation(e[:], e[:], ACT.Exp).then_inc(exp_made, 1)

        @block.tensor
        def _(pe):
            pe_done.open(pe)
            with pe.Fori(0, HEADS) as h:
                for m in (0, 1):
                    w.product(pe, h, m, ps[:, m, :], h_hi, h_lo).then_inc(pe_done.sem, 1)
                pe.wait_ge(keys_in, 16 * (h + 1))
                for m in (0, 1):
                    pe.wait_ge(act_done.sem, act_done.after(f"q{m}", h))
                    for t in range(NT):
                        ins = pe.matmul(ps[:, 2 + m, P * t:P * t + P], q[:, m, P * t:P * t + P], keys[:, m, :],
                                        start=True, stop=True)
                    ins.then_inc(pe_done.sem, 1)

        @block.vector
        def _(dve):
            done = dve_done.sem

            def index(h):
                for m in (0, 1):
                    dve.wait_ge(pool_done.sem, pool_done.after(f"pick{m}", h))
                    dve.sem_inc(passed, 1)
                    dve.tensor_reduce(sel[:, 1 + m, :, bass.ds(h, 1), :].rearrange("p t a k -> p t (a k)"),
                                      hot[:, m, :, :].rearrange("p (t k) r -> p t k r", t=NT), AX.X,
                                      ALU.add).then_inc(done, 1)

            def turn(h, is_first=False):
                first, second = slice(0, 8), slice(8, 16)
                pairs = [(m, t) for m in (0, 1) for t in range(NT)]

                def own(name):
                    dve.wait_ge(done, dve_done.after(name, h))
                    dve.sem_inc(passed, 1)

                dve.wait_ge(act_done.sem, act_done.after("s1", h))
                dve.sem_inc(passed, 1)
                for m, t in pairs:
                    ins = dve.max(best[:, m, t, first], s[:, m, t, :])
                ins.then_inc(done, 1)
                own("max1")
                for m, t in pairs:
                    ins = dve.max_index(place[:, m, t, first], best[:, m, t, first], s[:, m, t, :])
                ins.then_inc(done, 1)
                for m, t in pairs:
                    ins = dve.match_replace(rest[:, m, t, :], best[:, m, t, first], s[:, m, t, :], -3.0e38)
                ins.then_inc(done, 1)
                own("drop")
                for m, t in pairs:
                    ins = dve.max(best[:, m, t, second], rest[:, m, t, :])
                ins.then_inc(done, 1)
                own("max2")
                for m, t in pairs:
                    ins = dve.max_index(place[:, m, t, second], best[:, m, t, second], rest[:, m, t, :])
                ins.then_inc(done, 1)
                own("at2")
                if is_first:
                    dve.sem_inc(done, 2)
                else:
                    index(h - 1)
                dve.tensor_copy(place_f[:], place[:]).then_inc(done, 1)
                dve.tensor_tensor(cand[:].rearrange("p t (a b) -> p t a b", a=TOP),
                                  best[:, 0, :, :].unsqueeze(3).to_broadcast([P, NT, TOP, TOP]),
                                  best[:, 1, :, :].unsqueeze(2).to_broadcast([P, NT, TOP, TOP]),
                                  ALU.add).then_inc(done, 1)
                own("cand")
                for t in range(NT):
                    ins = dve.max(top[:, t, first], cand[:, t, :])
                ins.then_inc(done, 1)
                own("cmax1")
                for t in range(NT):
                    ins = dve.max_index(pos[:, t, first], top[:, t, first], cand[:, t, :])
                ins.then_inc(done, 1)
                for t in range(NT):
                    ins = dve.match_replace(cand_rest[:, t, :], top[:, t, first], cand[:, t, :], -3.0e38)
                ins.then_inc(done, 1)
                own("cdrop")
                for t in range(NT):
                    ins = dve.max(top[:, t, second], cand_rest[:, t, :])
                ins.then_inc(done, 1)
                own("cmax2")
                for t in range(NT):
                    ins = dve.max_index(pos[:, t, second], top[:, t, second], cand_rest[:, t, :])
                ins.then_inc(done, 1)
                own("cat2")
                dve.tensor_scalar(pos_part[:, 0, :, :], pos[:], 4, None, ALU.logical_shift_right).then_inc(done, 1)
                dve.tensor_scalar(pos_part[:, 1, :, :], pos[:], TOP - 1, None, ALU.bitwise_and).then_inc(done, 1)
                own("col")
                dve.tensor_copy(pos_f[:], pos_part[:]).then_inc(done, 1)
                own("pos_f")
                for m in (0, 1):
                    dve.tensor_tensor(hot[:, m, :, :],
                                      pos_f[:, m, :, :].rearrange("p t k -> p (t k)").unsqueeze(2).to_broadcast([P, NT * TOP, TOP]),
                                      iota[:].unsqueeze(1).to_broadcast([P, NT * TOP, TOP]),
                                      ALU.is_equal).then_inc(done, 1)
                dve.tensor_tensor(e[:, :, bass.ds(h, 1), :].rearrange("p t a k -> p t (a k)"), top[:],
                                  top[:, :, 0:1].to_broadcast([P, NT, TOP]), ALU.subtract).then_inc(done, 1)
            dve_done.open(dve)
            dve.wait_ge(consts, 16)
            turn(0, is_first=True)
            with dve.Fori(1, HEADS) as h:
                turn(h)
            index(HEADS - 1)
            dve.wait_ge(exp_made, 1)
            dve.tensor_reduce(total[:], e[:], AX.X, ALU.add).then_inc(softmax, 1)
            dve.wait_ge(softmax, 1)
            dve.reciprocal(total[:], total[:]).then_inc(softmax, 1)
            dve.wait_ge(softmax, 2)
            dve.tensor_tensor(sel[:, 0, :, :, :].rearrange("p t h k -> p (t h) k"), e[:].rearrange("p t h k -> p (t h) k"),
                              total[:].rearrange("p t h -> p (t h)").unsqueeze(2).to_broadcast([P, NT * HEADS, TOP]),
                              ALU.mult).then_inc(softmax, 1)


def spread_gates(nc, sel, ident, iota_dram, gates_dram):
    STEP = 4
    DEEP = 4
    BLOCK = gates_dram.shape[3]
    BATCHES = TOK // STEP
    PER_BLOCK = BLOCK // STEP
    BLOCKS = TOK // BLOCK
    with ExitStack() as ctx:
        def sb(name, shape, dt=F32):
            return ctx.enter_context(nc.sbuf_tensor(f"sg_{name}", shape, dt))

        def sem(name):
            return ctx.enter_context(nc.semaphore(f"sg_{name}"))

        iota = sb("iota", [P, KEYS])
        selT = sb("selT", [P, 3, TOK])
        row = sb("row", [P, DEEP, STEP, KEYS])
        col = sb("col", [P, DEEP, STEP, KEYS])
        gated = sb("gated", [P, DEEP, STEP, KEYS])
        full = sb("full", [P, 2, KEYS, BLOCK])
        ps = ctx.enter_context(nc.psum_tensor("sg_ps", [P, 3 + DEEP, TOK], F32))
        loaded = sem("loaded")
        turned = sem("turned")
        copied = sem("copied")
        passed = sem("passed")
        row_made, col_made, gated_made = (Items(sem(f"{x}_made"), DEEP) for x in ("row", "col", "gated"))
        used = Items(sem("used"), DEEP)
        filled = Items(sem("filled"), DEEP)
        stored = [sem("stored0"), sem("stored1")]
        block = ctx.enter_context(nc.Block())
        slots = sel[:].rearrange("p a t h k -> p a t (h k)")
        iota_all = iota[:].unsqueeze(1).to_broadcast([P, STEP, KEYS])

        def of_batch(kind, n):
            return selT[:, kind, bass.ds(STEP * n, STEP)].unsqueeze(2).to_broadcast([P, STEP, KEYS])

        @block.sync
        def _(sp):
            sp.dma_start(iota[:], iota_dram).then_inc(loaded, 16)
            for t in range(BLOCKS):
                sp.wait_ge(filled.sem, filled.after(PER_BLOCK * (t + 1) - 1))
                sp.dma_start(gates_dram[t], full[:, t % 2, :, :]).then_inc(stored[t % 2], 16)
            for s in stored:
                sp.wait_ge(s, 16 * BLOCKS // 2)

        @block.tensor
        def _(pe):
            pe.wait_ge(loaded, 16)
            for a in range(3):
                for t in range(NT):
                    ins = pe.transpose(ps[:, a, P * t:P * t + P], slots[:, a, t, :], ident[:])
            ins.then_inc(turned, 1)
            used.open(pe)
            with pe.Fori(0, BATCHES // DEEP) as i:
                for b in range(DEEP):
                    n = DEEP * i + b
                    pe.wait_ge(row_made.sem, row_made.after(n))
                    pe.wait_ge(gated_made.sem, gated_made.after(n))
                    pe.wait_ge(filled.sem, filled.after(n - DEEP))
                    for m in range(STEP):
                        ins = pe.matmul(ps[:, 3 + b, P * m:P * m + P], row[:, b, m, :], gated[:, b, m, :],
                                        start=True, stop=True)
                    ins.then_inc(used.sem, 1)

        @block.gpsimd
        def _(pool):
            gated_made.open(pool)
            pool.wait_ge(copied, 1)
            with pool.Fori(0, BATCHES // DEEP) as i:
                for b in range(DEEP):
                    n = DEEP * i + b
                    pool.wait_ge(col_made.sem, col_made.after(n))
                    pool.wait_ge(used.sem, used.after(n - DEEP))
                    pool.sem_inc(passed, 1)
                    pool.tensor_tensor(gated[:, b, :, :], col[:, b, :, :], of_batch(0, n), ALU.mult).then_inc(gated_made.sem, 1)

        @block.scalar
        def _(act):
            filled.open(act)
            for t in range(BLOCKS):
                if t >= 2:
                    act.wait_ge(stored[t % 2], 16 * (t // 2))
                with act.Fori(0, PER_BLOCK // DEEP) as i:
                    for b in range(DEEP):
                        act.wait_ge(used.sem, used.after(PER_BLOCK * t + DEEP * i + b))
                        act.copy(full[:, t % 2, :, bass.ds(STEP * (DEEP * i + b), STEP)].rearrange("p c t -> p t c"),
                                 ps[:, 3 + b, :].rearrange("p (t c) -> p t c", t=STEP)).then_inc(filled.sem, 1)

        @block.vector
        def _(dve):
            row_made.open(dve)
            col_made.open(dve)
            dve.wait_ge(turned, 1)
            dve.tensor_copy(selT[:].rearrange("p a t -> p (a t)"), ps[:, 0:3, :].rearrange("p a t -> p (a t)")).then_inc(copied, 1)
            dve.wait_ge(loaded, 16)
            dve.wait_ge(copied, 1)
            with dve.Fori(0, BATCHES // DEEP) as i:
                for b in range(DEEP):
                    n = DEEP * i + b
                    dve.wait_ge(used.sem, used.after(n - DEEP))
                    dve.tensor_tensor(row[:, b, :, :], iota_all, of_batch(1, n), ALU.is_equal).then_inc(row_made.sem, 1)
                    dve.wait_ge(gated_made.sem, gated_made.after(n - DEEP))
                    dve.tensor_tensor(col[:, b, :, :], iota_all, of_batch(2, n), ALU.is_equal).then_inc(col_made.sem, 1)


def experts(nc, down_dram, up_dram, gates_dram, h_hi, h_lo, acc, out_dram):
    G = 4
    SLOTS = 2 * G
    TURNS = KEYS // SLOTS
    UP = D // P
    BANKS = 4
    with ExitStack() as ctx:
        def sb(name, shape, dt=F32):
            return ctx.enter_context(nc.sbuf_tensor(f"ex_{name}", shape, dt))

        def sem(name):
            return ctx.enter_context(nc.semaphore(f"ex_{name}"))

        d_raw = sb("d_raw", [P, 2, KD, P])
        d_hi = sb("d_hi", [P, 2, KD, P], F32R)
        d_lo = sb("d_lo", [P, 2, KD, P], F32R)
        u_raw = sb("u_raw", [P, 2, D])
        u_hi = sb("u_hi", [P, SLOTS, D], F32R)
        u_lo = sb("u_lo", [P, SLOTS, D], F32R)
        BLOCKS, _, _, BLOCK = gates_dram.shape
        gates = sb("gates", [P, 2, BLOCKS, G, BLOCK])
        gelu = sb("gelu", [P, 2, TOK])
        a = sb("a", [P, 2, TOK])
        a_hi = sb("a_hi", [P, SLOTS, TOK], F32R)
        a_lo = sb("a_lo", [P, SLOTS, TOK], F32R)
        ps = ctx.enter_context(nc.psum_tensor("ex_ps", [P, 8, TOK], F32))
        d_in = [sem("d_in0"), sem("d_in1")]
        u_in = [sem("u_in0"), sem("u_in1")]
        g_in = [sem("g_in0"), sem("g_in1")]
        d_hi_made, u_hi_made = Items(sem("d_hi_made"), 0), Items(sem("u_hi_made"), 0)
        d_lo_made, u_lo_made = Items(sem("d_lo_made"), 2), Items(sem("u_lo_made"), 2)
        down_done = Items(sem("down_done"), 2)
        gelu_made = Items(sem("gelu_made"), 2)
        a_made = Items(sem("a_made"), SLOTS)
        a_hi_made, a_lo_made = Items(sem("a_hi_made"), 0), Items(sem("a_lo_made"), 0)
        up_done = Items(sem("up_done"), 2 * UP)
        added = Items(sem("added"), BANKS)
        stored = sem("stored")
        block = ctx.enter_context(nc.Block())
        @block.sync
        def _(sp):
            with sp.Fori(0, TURNS) as i:
                for q in range(SLOTS):
                    n, s = SLOTS * i + q, q % 2
                    sp.wait_ge(d_lo_made.sem, d_lo_made.after(n - 2))
                    sp.dma_start(d_raw[:, s, :, :], down_dram[bass.ds(n, 1), :, :, :].rearrange("a p k c -> (a p) k c")).then_inc(d_in[s], 16)
                    if q % G == 0:
                        sp.wait_ge(a_made.sem, a_made.after(n - SLOTS + G - 1))
                        sp.dma_start(gates[:, q // G, :, :, :], gates_dram[:, :, bass.ds(n, G), :].rearrange("t p c k -> p t c k")).then_inc(g_in[q // G], 16)
                    sp.wait_ge(u_lo_made.sem, u_lo_made.after(n - 2))
                    sp.dma_start(u_raw[:, s, :], up_dram[bass.ds(n, 1), :, :].rearrange("a p c -> (a p) c")).then_inc(u_in[s], 16)
            sp.wait_ge(added.sem, added.after(UP * KEYS // G - 1))
            sp.dma_start(out_dram, acc[:]).then_inc(stored, 16)
            sp.wait_ge(stored, 16)

        @block.gpsimd
        def _(pool):
            d_lo_made.open(pool)
            u_lo_made.open(pool)
            with pool.Fori(0, TURNS) as i:
                for q in range(SLOTS):
                    n, s = SLOTS * i + q, q % 2
                    pool.wait_ge(d_hi_made.sem, d_hi_made.after(n))
                    pool.tensor_tensor(d_lo[:, s, :, :], d_raw[:, s, :, :], d_hi[:, s, :, :].bitcast(F32),
                                       ALU.subtract).then_inc(d_lo_made.sem, 1)
                    pool.wait_ge(u_hi_made.sem, u_hi_made.after(n))
                    pool.tensor_tensor(u_lo[:, q, :], u_raw[:, s, :], u_hi[:, q, :].bitcast(F32),
                                       ALU.subtract).then_inc(u_lo_made.sem, 1)

        @block.scalar
        def _(act):
            def activate(n, q):
                act.wait_ge(down_done.sem, down_done.after(n))
                act.activation(gelu[:, q % 2, :], ps[:, q % 2, :], ACT.Gelu).then_inc(gelu_made.sem, 1)
                act.wait_ge(a_made.sem, a_made.after(n))
                act.copy(a_hi[:, q, :], a[:, q % 2, :]).then_inc(a_hi_made.sem, 1)

            def turn(i, first=False):
                for q in range(SLOTS):
                    n, s = SLOTS * i + q, q % 2
                    act.wait_ge(d_in[s], 16 * (G * i + q // 2 + 1))
                    act.wait_ge(down_done.sem, down_done.after(n - 2))
                    act.copy(d_hi[:, s, :, :], d_raw[:, s, :, :]).then_inc(d_hi_made.sem, 1)
                    act.wait_ge(u_in[s], 16 * (G * i + q // 2 + 1))
                    if q % G == 0:
                        act.wait_ge(up_done.sem, up_done.after(UP * (2 * i + q // G - 1) - 1))
                    act.copy(u_hi[:, q, :], u_raw[:, s, :]).then_inc(u_hi_made.sem, 1)
                    if q or not first:
                        activate(n - 1, (q - 1) % SLOTS)

            gelu_made.open(act)
            turn(0, first=True)
            with act.Fori(1, TURNS) as i:
                turn(i)
            activate(KEYS - 1, SLOTS - 1)

        @block.tensor
        def _(pe):
            def up(g, half, j):
                if j == 0:
                    pe.wait_ge(a_lo_made.sem, a_lo_made.after(G * g + G - 1))
                    pe.wait_ge(u_lo_made.sem, u_lo_made.after(G * g + G - 1))
                for c in (2 * j, 2 * j + 1):
                    pe.wait_ge(added.sem, added.after(UP * g + c - BANKS))
                    for t in range(G):
                        s = G * half + t
                        ins = three_passes(pe, ps[:, 2 + c % BANKS, :], u_hi[:, s, P * c:P * c + P],
                                           u_lo[:, s, P * c:P * c + P], a_hi[:, s, :], a_lo[:, s, :],
                                           t == 0, t == G - 1)
                    ins.then_inc(up_done.sem, 1)

            def turn(i, first=False):
                for q in range(SLOTS):
                    n, s = SLOTS * i + q, q % 2
                    pe.wait_ge(gelu_made.sem, gelu_made.after(n - 2))
                    pe.wait_ge(d_lo_made.sem, d_lo_made.after(n))
                    for k in range(KD):
                        ins = three_passes(pe, ps[:, s, :], d_hi[:, s, k, :], d_lo[:, s, k, :], h_hi[:, k, :],
                                           h_lo[:, k, :], k == 0, k == KD - 1)
                    ins.then_inc(down_done.sem, 1)
                    if q >= G or not first:
                        up(2 * i + q // G - 1, 1 - q // G, q % G)

            down_done.open(pe)
            up_done.open(pe)
            turn(0, first=True)
            with pe.Fori(1, TURNS) as i:
                turn(i)
            for j in range(G):
                up(2 * TURNS - 1, 1, j)

        @block.vector
        def _(dve):
            def sum_up(g, j):
                for c in (2 * j, 2 * j + 1):
                    dve.wait_ge(up_done.sem, up_done.after(UP * g + c))
                    dve.tensor_tensor(acc[:, c, :], acc[:, c, :], ps[:, 2 + c % BANKS, :],
                                      ALU.add).then_inc(added.sem, 1)

            def turn(i, first=False):
                for q in range(SLOTS):
                    n = SLOTS * i + q
                    if q % G == 0:
                        dve.wait_ge(g_in[q // G], 16 * (i + 1))
                        dve.wait_ge(up_done.sem, up_done.after(UP * (2 * i + q // G - 1) - 1))
                    dve.wait_ge(gelu_made.sem, gelu_made.after(n))
                    dve.tensor_tensor(a[:, q % 2, :].rearrange("p (t k) -> p t k", t=BLOCKS), gates[:, q // G, :, q % G, :],
                                      gelu[:, q % 2, :].rearrange("p (t k) -> p t k", t=BLOCKS),
                                      ALU.mult).then_inc(a_made.sem, 1)
                    dve.wait_ge(a_hi_made.sem, a_hi_made.after(n))
                    dve.tensor_tensor(a_lo[:, q, :], a[:, q % 2, :], a_hi[:, q, :].bitcast(F32),
                                      ALU.subtract).then_inc(a_lo_made.sem, 1)
                    if q >= G or not first:
                        sum_up(2 * i + q // G - 1, q % G)

            a_made.open(dve)
            added.open(dve)
            turn(0, first=True)
            with dve.Fori(1, TURNS) as i:
                turn(i)
            for j in range(G):
                sum_up(2 * TURNS - 1, j)


def build(nc, dram, out):
    with ExitStack() as ctx:
        def sb(name, shape, dt=F32):
            return ctx.enter_context(nc.sbuf_tensor(name, shape, dt))

        xT = sb("xT", [P, KD, TOK])
        ident = sb("ident", [P, P])
        ones = sb("ones", [P, P])
        halves = sb("halves", [P, P])
        h_hi = sb("h_hi", [P, KD, TOK], F32R)
        h_lo = sb("h_lo", [P, KD, TOK], F32R)
        cols = sb("cols", [P, 4, NT, HEADS])
        rows_dram = nc.dram_tensor("rows_dram", [HEADS, 3, TOK], F32, kind="Internal").ap()
        gates_dram = nc.dram_tensor("gates_dram", [NCH, KEYS, KEYS, TOK // NCH], F32, kind="Internal").ap()

        with nc.sbuf_tensor("h_full", [P, KD, TOK], F32) as h_full:
            norm_and_split(nc, "n1", xT, dram["norm_mix"], ones, h_full, h_hi, h_lo,
                           load=[(xT[:], dram["xT"]), (ident[:], dram["ident"]), (ones[:], dram["ones"]),
                                 (halves[:], dram["halves"])])
            decay_rows(nc, h_full, dram["w_ab"], dram["dt_bias"], dram["a_log"], ident, dram["resets"],
                       rows_dram, cols)
        with nc.sbuf_tensor("o_b", [P, HEADS, TOK], F32) as o_b:
            mixer_b(nc, h_hi, h_lo, dram["w_b"], dram["conv"], dram["b_norm"], rows_dram, cols, ident, ones,
                    dram["masks"], o_b)
            with nc.sbuf_tensor("o_a", [P, A_W // P, TOK], F32) as o_a:
                mixer_a(nc, h_hi, h_lo, dram["w_a"], dram["bias"], dram["a_gains"], ident, halves, o_a)
                with (nc.sbuf_tensor("mixed_hi", [P, KD, TOK], F32R) as mixed_hi,
                      nc.sbuf_tensor("mixed_lo", [P, KD, TOK], F32R) as mixed_lo):
                    merge(nc, "mg", dram["w_merge"], [KD, KD, A_W // P, KD], h_hi, h_lo, o_a, o_b,
                          dram["b_merge"], mixed_hi, mixed_lo)
                    project_out(nc, dram["w_out"], mixed_hi, mixed_lo, xT)
        with nc.sbuf_tensor("hf_full", [P, KD, TOK], F32) as h_full:
            norm_and_split(nc, "n2", xT, dram["norm_ffn"], ones, h_full, h_hi, h_lo)
        with nc.sbuf_tensor("sel", [P, 3, NT, HEADS, TOP], F32) as sel:
            choose_experts(nc, dram["w_query"], dram["keys"], dram["iota16"], h_hi, h_lo, sel)
            spread_gates(nc, sel, ident, dram["iota128"], gates_dram)
        experts(nc, dram["down"], dram["up"], gates_dram, h_hi, h_lo, xT, out)


A_W, B_W = 512, 1024
OFF_B = 3 * A_W
OFF_AB = OFF_B + 3 * B_W
OFF_G = OFF_AB + 16
OFF_M = OFF_G + B_W


def layout(inputs):
    import numpy as np

    def tiles(w):
        k = w.shape[0] // P
        return np.ascontiguousarray(w.reshape(k, P, w.shape[1] // P, P).transpose(2, 1, 0, 3))

    a = {k: np.asarray(v) for k, v in inputs.items()}
    w_in = a["w_in"][0]
    qkv = [tiles(w_in[:, OFF_B + i * B_W:OFF_B + (i + 1) * B_W]) for i in range(3)]
    gate = tiles(w_in[:, OFF_G:OFF_G + B_W])
    out = {
        "xT": a["x"][0].T.reshape(KD, P, TOK).transpose(1, 0, 2),
        "ident": np.eye(P, dtype=np.float32),
        "ones": np.ones((P, P), np.float32),
        "norm_mix": a["norm_mix_w"][0].reshape(KD, P).T,
        "w_ab": w_in[:, OFF_AB:OFF_AB + 16].reshape(KD, P, 16).transpose(1, 0, 2),
        "dt_bias": a["b_dt_bias"][0][:, None],
        "a_log": a["b_a_log"][0][:, None],
        "resets": np.tile((np.arange(TOK) % CH != 0).astype(np.float32), (HEADS, 1)),
        "w_b": np.concatenate(qkv + [gate], 2),
        "conv": a["b_conv_w"][0].reshape(CONV, 3, HEADS, P).transpose(3, 2, 1, 0),
        "b_norm": a["b_norm_w"][0][:, None],
    }
    i, j = np.arange(CH)[:, None], np.arange(CH)[None, :]
    levels = [((i // (2 * s) == j // (2 * s)) & (i // s > j // s)).astype(np.float32) for s in (1, 2, 4, 8, 16, 32)]
    levels.append(np.where(j >= i, 0.0, NEG).astype(np.float32))
    rel = a["a_rel_bias"][0]
    reach = TOK - P
    longer = np.pad(rel, ((0, 0), (0, TOK - rel.shape[1] + P)), mode="edge")
    rev = longer[:, ::-1]
    last = longer.shape[1] - 1
    out["bias"] = np.stack([rev[:, last - (r + reach + P):last - (r + reach + P) + TOK] for r in range(P)], 1) \
        .reshape(HEADS // 2, 2, P, TOK).transpose(0, 2, 1, 3)
    out["a_gains"] = np.stack([np.tile(a["a_q_norm_w"][0], 2), np.tile(a["a_k_norm_w"][0], 2)], 1)
    out["halves"] = np.kron(np.eye(2, dtype=np.float32), np.ones((64, 64), np.float32))
    out["w_a"] = np.concatenate([tiles(w_in[:, A_W * n:A_W * n + A_W]) for n in range(3)], 2)
    merge_w = [tiles(w_in[:, OFF_M + D * n:OFF_M + D * n + D]) for n in range(2)]
    out["w_merge"] = np.concatenate(merge_w + [tiles(a["w_proj_a"][0]), tiles(a["w_proj_b"][0])], 2)
    out["b_merge"] = a["b_merge"][0].reshape(2, KD, P).transpose(2, 0, 1)
    pair = lambda w: np.concatenate([w[0::2], w[1::2]], 2)
    out["w_out"] = pair(tiles(a["w_out"][0]))
    out["norm_ffn"] = a["norm_ffn_w"][0].reshape(KD, P).T
    out["w_query"] = pair(tiles(a["peer_w_query"][0]))
    out["keys"] = np.stack([a["peer_keys_1"][0], a["peer_keys_2"][0]], 0).transpose(1, 3, 0, 2)
    out["iota16"] = np.tile(np.arange(TOP, dtype=np.float32), (P, 1))
    out["iota128"] = np.tile(np.arange(KEYS, dtype=np.float32), (P, 1))
    out["down"] = a["peer_down"][0].reshape(KEYS, KEYS, KD, P).transpose(1, 3, 2, 0)
    out["up"] = a["peer_up"][0].reshape(KEYS, KEYS, D).transpose(1, 0, 2)
    levels.append(np.eye(CH, dtype=np.float32))
    out["masks"] = np.tile(np.stack(levels, 1), (2, 1, 1))
    return {k: np.ascontiguousarray(v) for k, v in out.items()}


def kernel(**inputs):
    import numpy as np
    import concourse.bacc as bacc
    from concourse.bass_utils import run_bass_kernel_spmd

    arrays = layout(inputs)
    nc = bacc.Bacc("TRN2", target_bir_lowering=False, num_devices=1)
    dram = {k: nc.dram_tensor(f"in_{k}", v.shape, mybir.dt.from_np(v.dtype), kind="ExternalInput").ap()
            for k, v in arrays.items()}
    out = nc.dram_tensor("out_y", [P, KD, TOK], F32, kind="ExternalOutput").ap()
    build(nc, dram, out)
    r = run_bass_kernel_spmd(nc, [{f"in_{k}": v for k, v in arrays.items()}], core_ids=[0])
    y = r.results[0]["out_y"]
    return np.ascontiguousarray(y.transpose(1, 0, 2).reshape(D, TOK).T)[None]
```

```python
import math
from contextlib import ExitStack

import concourse.bass as bass
from concourse import mybir

P = 128
D = 1024
TOK = 512
KD = D // P
NT = TOK // P
CH = 64
NCH = TOK // CH
EPS = 1e-6
HEADS = 8
HD = 128
LEVELS = 6
CONV = 4
NEG = -1e30

F32 = mybir.dt.float32
F32R = mybir.dt.float32r
U32 = mybir.dt.uint32
ALU = mybir.AluOpType
ACT = mybir.ActivationFunctionType
AX = mybir.AxisListType


class Steps:

    def __init__(self, sem, names):
        self.sem = sem
        self.per = len(names)
        self.place = {name: n + 1 for n, name in enumerate(names)}
        assert len(self.place) == self.per

    def open(self, engine):
        engine.sem_inc(self.sem, self.per)

    def after(self, name, turn=0):
        return (turn + 1) * self.per + self.place[name]


class Items:

    def __init__(self, sem, ahead):
        self.sem, self.ahead = sem, ahead

    def open(self, engine):
        engine.sem_inc(self.sem, self.ahead)

    def after(self, n):
        return n + 1 + self.ahead


def three_passes(pe, out, w_hi, w_lo, x_hi, x_lo, first, last):
    pe.matmul(out, w_hi, x_lo, start=first, stop=False)
    pe.matmul(out, w_lo, x_hi, start=False, stop=False)
    return pe.matmul(out, w_hi, x_hi, start=False, stop=last)


class Weights:

    def __init__(self, ctx, nc, tag, source, pieces, used=None, names=None):
        self.source, self.pieces, self.used, self.names = source, pieces, used, names
        self.starts = [sum(pieces[:m]) for m in range(len(pieces))]
        self.n = len(pieces)
        shape = [P, sum(pieces), P]
        self.raw = ctx.enter_context(nc.sbuf_tensor(f"{tag}_w_raw", shape, F32))
        self.hi = ctx.enter_context(nc.sbuf_tensor(f"{tag}_w_hi", shape, F32R))
        self.lo = ctx.enter_context(nc.sbuf_tensor(f"{tag}_w_lo", shape, F32R))
        sem = lambda name: ctx.enter_context(nc.semaphore(f"{tag}_{name}"))
        self.raw_in = [sem(f"w_raw_in{m}") for m in range(self.n)]
        self.hi_made = Steps(sem("w_hi_made"), range(self.n))
        self.lo_made = Steps(sem("w_lo_made"), range(self.n))

    def part(self, tensor, m):
        return tensor[:, self.starts[m]:self.starts[m] + self.pieces[m], :]

    def serve(self, used, names):
        self.used, self.names = used, names

    def load(self, sp, i, fresh=False):
        for m in range(self.n):
            if not fresh:
                sp.wait_ge(self.lo_made.sem, self.lo_made.after(m, i - 1))
            if callable(self.source):
                src = self.source(i, m)
            else:
                src = self.source[bass.ds(i, 1), :, self.starts[m]:self.starts[m] + self.pieces[m], :]
            sp.dma_start(self.part(self.raw, m), src.rearrange("a p k c -> (a p) k c")).then_inc(self.raw_in[m], 16)

    def high(self, act, i, pieces=None, fresh=False):
        for m in range(self.n) if pieces is None else pieces:
            act.wait_ge(self.raw_in[m], 16 * (i + 1))
            if not fresh:
                act.wait_ge(self.used.sem, self.used.after(self.names[m], i - 1))
            act.copy(self.part(self.hi, m), self.part(self.raw, m)).then_inc(self.hi_made.sem, 1)

    def high_ahead(self, act):
        self.hi_made.open(act)
        self.high(act, 0, fresh=True)

    def low_ahead(self, pool):
        self.lo_made.open(pool)
        self.low(pool, 0)

    def low(self, pool, i):
        for m in range(self.n):
            pool.wait_ge(self.hi_made.sem, self.hi_made.after(m, i))
            pool.tensor_tensor(self.part(self.lo, m), self.part(self.raw, m), self.part(self.hi, m).bitcast(F32),
                               ALU.subtract).then_inc(self.lo_made.sem, 1)

    def block(self, pe, i, m, k, out, x_hi, x_lo):
        if k == 0:
            pe.wait_ge(self.lo_made.sem, self.lo_made.after(m, i))
        at = self.starts[m] + k
        return three_passes(pe, out, self.hi[:, at, :], self.lo[:, at, :], x_hi[:, k, :], x_lo[:, k, :],
                            k == 0, k == self.pieces[m] - 1)

    def product(self, pe, i, m, out, x_hi, x_lo):
        for k in range(self.pieces[m]):
            ins = self.block(pe, i, m, k, out, x_hi, x_lo)
        return ins


def norm_and_split(nc, tag, x, gain_dram, ones, h_full, h_hi, h_lo, x_dram=None, load=(), ahead=()):
    POOL_LOW = 5
    with ExitStack() as ctx:
        def sb(name, shape, dt=F32):
            return ctx.enter_context(nc.sbuf_tensor(f"{tag}_{name}", shape, dt))

        def sem(name):
            return ctx.enter_context(nc.semaphore(f"{tag}_{name}"))

        sq = sb("sq", [P, KD, TOK])
        var = sb("var", [P, TOK])
        gain = sb("gain", [P, KD])
        sums = ctx.enter_context(nc.psum_tensor(f"{tag}_sums", [P, TOK], F32))
        loaded = sem("loaded")
        n_loads = 1 + len(load)
        x_in = [sem("x_in0"), sem("x_in1")]
        squared = sem("squared")
        summed = sem("summed")
        biased = sem("biased")
        rooted = sem("rooted")
        inverted = sem("inverted")
        scaled = sem("scaled")
        high = sem("high")
        low = sem("low")
        block = ctx.enter_context(nc.Block())

        @block.sync
        def _(sp):
            for n in (0, 1) if x_dram is not None else ():
                half = slice(n * KD // 2, (n + 1) * KD // 2)
                sp.dma_start(x[:, half, :], x_dram[:, half, :]).then_inc(x_in[n], 16)
            for dst, src in load:
                sp.dma_start(dst, src).then_inc(loaded, 16)
            sp.dma_start(gain[:], gain_dram).then_inc(loaded, 16)
            for w in ahead:
                w.load(sp, 0, fresh=True)

        @block.scalar
        def _(act):
            for k in range(KD):
                if x_dram is not None and k % (KD // 2) == 0:
                    act.wait_ge(x_in[k // (KD // 2)], 16)
                act.activation(sq[:, k, :], x[:, k, :], ACT.Square).then_inc(squared, 1)
            for w in ahead:
                w.high_ahead(act)
            act.wait_ge(biased, 1)
            act.activation(var[:], var[:], ACT.Sqrt).then_inc(rooted, 1)
            for k in range(KD):
                act.wait_ge(scaled, k + 1)
                act.copy(h_hi[:, k, :], h_full[:, k, :]).then_inc(high, 1)

        @block.tensor
        def _(pe):
            pe.wait_ge(loaded, 16 * n_loads)
            for k in range(KD):
                pe.wait_ge(squared, k + 1)
                ins = pe.matmul(sums[:], ones[:], sq[:, k, :], start=(k == 0), stop=(k == KD - 1))
            ins.then_inc(summed, 1)

        @block.gpsimd
        def _(pool):
            for w in ahead:
                w.low_ahead(pool)
            for k in range(POOL_LOW):
                pool.wait_ge(high, k + 1)
                pool.tensor_tensor(h_lo[:, k, :], h_full[:, k, :], h_hi[:, k, :].bitcast(F32),
                                   ALU.subtract).then_inc(low, 1)

        @block.vector
        def _(dve):
            dve.wait_ge(loaded, 16 * n_loads)
            dve.wait_ge(summed, 1)
            dve.tensor_scalar(var[:], sums[:], 1.0 / D, EPS, ALU.mult, ALU.add).then_inc(biased, 1)
            dve.wait_ge(rooted, 1)
            dve.reciprocal(var[:], var[:]).then_inc(inverted, 1)
            dve.wait_ge(inverted, 1)
            for k in range(KD):
                dve.scalar_tensor_tensor(out=h_full[:, k, :], in0=x[:, k, :], scalar=gain[:, k:k + 1],
                                         in1=var[:], op0=ALU.mult, op1=ALU.mult).then_inc(scaled, 1)
            for k in range(POOL_LOW, KD):
                dve.wait_ge(high, k + 1)
                dve.tensor_tensor(h_lo[:, k, :], h_full[:, k, :], h_hi[:, k, :].bitcast(F32),
                                  ALU.subtract).then_inc(low, 1)


def decay_rows(nc, h_full, w_ab, dt_bias, a_log, ident8, resets, rows_dram, cols, ahead):
    with ExitStack() as ctx:
        def sb(name, shape, dt=F32):
            return ctx.enter_context(nc.sbuf_tensor(f"dr_{name}", shape, dt))

        def sem(name):
            return ctx.enter_context(nc.semaphore(f"dr_{name}"))

        wab = sb("wab", [P, KD, 2 * HEADS])
        bias = sb("bias", [HEADS, 1])
        alog = sb("alog", [HEADS, 1])
        rate = sb("rate", [HEADS, 1])
        mask = sb("mask", [HEADS, TOK])
        rows = sb("rows", [HEADS, 5, TOK])
        tmp = sb("tmp", [HEADS, 6, TOK])
        ps = ctx.enter_context(nc.psum_tensor("dr_ps", [P, 3, TOK], F32))
        loaded = sem("loaded")
        stored = sem("stored")
        dve_done = Steps(sem("dve_done"), ["x", "neg_abs", "e_plus_1", "neg_rate", "part", "rest", "inv", "corr",
                                           "log1p", "pos", "softplus", "g", "gc", "last_minus",
                                           "beta_exp", "cols"])
        act_done = Steps(sem("act_done"), ["rate", "e", "ln", "beta", "egc", "elast"])
        pe_done = Steps(sem("pe_done"), ["a", "b", "turned"])
        block = ctx.enter_context(nc.Block())
        x, ax, e, u, l, g = (tmp[:, i, :] for i in range(6))
        r, d = rows[:, 3, :], rows[:, 4, :]
        gc, beta, egc, begc, elast = (rows[:, i, :] for i in range(5))

        @block.sync
        def _(sp):
            sp.dma_start(wab[:], w_ab).then_inc(loaded, 16)
            sp.dma_start(bias[:], dt_bias).then_inc(loaded, 16)
            sp.dma_start(alog[:], a_log).then_inc(loaded, 16)
            sp.dma_start(mask[:], resets).then_inc(loaded, 16)
            ahead.load(sp, 0, fresh=True)
            sp.wait_ge(act_done.sem, act_done.after("egc"))
            sp.wait_ge(dve_done.sem, dve_done.after("gc"))
            sp.dma_start(rows_dram, rows[:, 0:3, :]).then_inc(stored, 16)
            sp.wait_ge(stored, 16)

        @block.tensor
        def _(pe):
            pe_done.open(pe)
            pe.wait_ge(loaded, 64)
            for half in range(2):
                for k in range(KD):
                    ins = pe.matmul(ps[0:HEADS, half, :], wab[:, k, HEADS * half:HEADS * half + HEADS],
                                    h_full[:, k, :], start=(k == 0), stop=(k == KD - 1))
                ins.then_inc(pe_done.sem, 1)
            pe.wait_ge(dve_done.sem, dve_done.after("beta_exp"))
            pe.wait_ge(act_done.sem, act_done.after("elast"))
            for n, row in enumerate((beta, gc, begc, elast)):
                for t in range(NT):
                    at = (n * NT + t) * HEADS
                    ins = pe.transpose(ps[:, 2, at:at + HEADS], row[:, t * P:t * P + P],
                                       ident8[0:HEADS, 0:HEADS])
            ins.then_inc(pe_done.sem, 1)

        @block.scalar
        def _(act):
            act_done.open(act)
            act.wait_ge(loaded, 64)
            act.activation(rate[:], alog[:], ACT.Exp).then_inc(act_done.sem, 1)
            act.wait_ge(dve_done.sem, dve_done.after("neg_abs"))
            act.activation(e, ax, ACT.Exp).then_inc(act_done.sem, 1)
            act.wait_ge(dve_done.sem, dve_done.after("e_plus_1"))
            act.activation(l, u, ACT.Ln).then_inc(act_done.sem, 1)
            act.wait_ge(pe_done.sem, pe_done.after("b"))
            act.activation(beta, ps[0:HEADS, 1, :], ACT.Sigmoid).then_inc(act_done.sem, 1)
            ahead.high_ahead(act)
            act.wait_ge(dve_done.sem, dve_done.after("gc"))
            act.activation(egc, gc, ACT.Exp).then_inc(act_done.sem, 1)
            act.wait_ge(dve_done.sem, dve_done.after("last_minus"))
            act.activation(elast, ax, ACT.Exp).then_inc(act_done.sem, 1)

        @block.gpsimd
        def _(pool):
            ahead.low_ahead(pool)

        @block.vector
        def _(dve):
            def own(name):
                dve.wait_ge(dve_done.sem, dve_done.after(name))

            dve_done.open(dve)
            dve.wait_ge(loaded, 64)
            dve.wait_ge(pe_done.sem, pe_done.after("a"))
            dve.tensor_scalar(x, ps[0:HEADS, 0, :], bias[:, 0:1], None, ALU.add).then_inc(dve_done.sem, 1)
            own("x")
            dve.scalar_tensor_tensor(out=ax, in0=x, scalar=-1.0, in1=x, op0=ALU.mult,
                                     op1=ALU.min).then_inc(dve_done.sem, 1)
            dve.wait_ge(act_done.sem, act_done.after("e"))
            dve.tensor_scalar(u, e, 1.0, None, ALU.add).then_inc(dve_done.sem, 1)
            dve.tensor_scalar(rate[:], rate[:], -1.0, None, ALU.mult).then_inc(dve_done.sem, 1)
            own("e_plus_1")
            dve.tensor_scalar(d, u, -1.0, None, ALU.add).then_inc(dve_done.sem, 1)
            own("part")
            dve.tensor_tensor(d, e, d, ALU.subtract).then_inc(dve_done.sem, 1)
            dve.reciprocal(r, u).then_inc(dve_done.sem, 1)
            own("inv")
            dve.tensor_tensor(d, d, r, ALU.mult).then_inc(dve_done.sem, 1)
            own("corr")
            dve.wait_ge(act_done.sem, act_done.after("ln"))
            dve.tensor_tensor(l, l, d, ALU.add).then_inc(dve_done.sem, 1)
            dve.tensor_scalar(x, x, 0.0, None, ALU.max).then_inc(dve_done.sem, 1)
            own("pos")
            dve.tensor_tensor(g, x, l, ALU.add).then_inc(dve_done.sem, 1)
            own("softplus")
            dve.tensor_scalar(g, g, rate[:, 0:1], None, ALU.mult).then_inc(dve_done.sem, 1)
            own("g")
            dve.tensor_tensor_scan(gc, mask[:], g, 0.0, ALU.mult, ALU.add).then_inc(dve_done.sem, 1)
            own("gc")
            chunks = gc.rearrange("p (c i) -> p c i", i=CH)
            dve.tensor_tensor(ax.rearrange("p (c i) -> p c i", i=CH),
                              chunks[:, :, CH - 1:CH].to_broadcast([HEADS, NCH, CH]), chunks,
                              ALU.subtract).then_inc(dve_done.sem, 1)
            dve.wait_ge(act_done.sem, act_done.after("egc"))
            dve.tensor_tensor(begc, beta, egc, ALU.mult).then_inc(dve_done.sem, 1)
            dve.wait_ge(pe_done.sem, pe_done.after("turned"))
            dve.tensor_copy(cols[:].rearrange("p a t h -> p (a t h)"),
                            ps[:, 2, 0:4 * NT * HEADS]).then_inc(dve_done.sem, 1)


def mixer_b(nc, h_hi, h_lo, w, conv_dram, norm_dram, rows_dram, cols, ident, ones, masks_dram, o_b):
    GROUPS = 4 * KD
    with ExitStack() as ctx:
        def sb(name, shape, dt=F32):
            return ctx.enter_context(nc.sbuf_tensor(f"mb_{name}", shape, dt))

        def sem(name):
            return ctx.enter_context(nc.semaphore(f"mb_{name}"))

        conv = sb("conv", [P, HEADS, 3, CONV])
        norm = sb("norm", [P, 1])
        biases = sb("biases", [P, 2])
        masks = sb("masks", [P, LEVELS + 2, CH])
        gc = sb("gc", [P, NT, CH])
        rows = sb("rows", [P, 2, TOK])
        y = sb("y", [P, 3, TOK])
        act_y = sb("act_y", [P, 3, TOK])
        sq = sb("sq", [P, 2, TOK])
        var = sb("var", [P, 2, TOK])
        qT = sb("qT", [P, TOK])
        kT = sb("kT", [P, TOK])
        kbT = sb("kbT", [P, TOK])
        qdT = sb("qdT", [P, TOK])
        decay = sb("decay", [P, NT, CH])
        AT = sb("AT", [P, NT, CH])
        attnT = sb("attnT", [P, NT, CH])
        prod = sb("prod", [P, NT, CH])
        T = sb("T", [P, NT, CH])
        TT = sb("TT", [P, NT, CH])
        vb = sb("vb", [P, NT, HD])
        kbe = sb("kbe", [P, NT, HD])
        kd = sb("kd", [P, NT, HD])
        nwT = sb("nwT", [P, 2, NT, CH])
        egl = sb("egl", [P, NCH])
        vn = sb("vn", [P, HD])
        S = sb("S", [P, 2, HD])
        osq = sb("osq", [P, TOK])
        ovar = sb("ovar", [P, TOK])
        o1 = sb("o1", [P, TOK])
        ps = ctx.enter_context(nc.psum_tensor("mb_ps", [P, 8, TOK], F32))
        FRONT, KEY, OUT, PAIR, LOWER = 0, 4, 5, 6, 7

        consts = sem("consts")
        passed = sem("passed")
        rows_in = sem("rows_in")
        gc_in = sem("gc_in")
        pe_front = Steps(sem("pe_front"), ["project_q", "project_k", "project_v", "sums", "project_g"])
        pe_core = Steps(sem("pe_core"),
                        ["turn_k", "gram", "AxT0", "TxP0", "AxT1", "turn_v", "TxP1"]
                        + [f"{s}{l}" for l in range(2, LEVELS) for s in ("AxT", "TxP")]
                        + ["wT"]
                        + [f"{s}{c}" for c in range(NCH) for s in ("v_new", "state", "out")
                           if (s, c) != ("state", NCH - 1)])
        pe_tail = Steps(sem("pe_tail"), ["out_sums"])
        w.serve(pe_front, ["project_" + t for t in "qkvg"])
        act_front = Steps(sem("act_front"), ["silu_q", "silu_k", "square_q", "square_k", "decay", "ln", "root_q",
                                             "root_k", "silu_v", "gate"])
        act_tail = Steps(sem("act_tail"), ["square_o", "ln_o", "root_o"])
        dve_front = Steps(sem("dve_front"), [f"conv{s}_{t}" for t in "qk" for s in range(CONV)]
                          + ["diff", "diff_masked"] + [f"conv{s}_v" for s in range(CONV)] + ["q", "k", "kb"])
        dve_core = Steps(sem("dve_core"),
                         ["A", "attn", "P0", "kbe", "T0", "TT0", "P1", "kd", "T1", "TT1", "P2", "vb", "T2", "TT2",
                          "P3", "qd", "egl", "T3", "TT3", "P4", "T4", "TT4", "P5", "TT5", "nw_even", "nw_odd"]
                         + [f"{s}{c}" for c in range(NCH) for s in ("vn", "S")
                            if (s, c) != ("S", NCH - 1)])
        dve_tail = Steps(sem("dve_tail"), ["o_normed", "o"])
        block = ctx.enter_context(nc.Block())
        halves = [(m, a, 2 * m + a, slice(CH * a, CH * a + CH)) for m in range(NT) for a in (0, 1)]
        BETA, GC, BEGC, ELAST = range(4)
        of = lambda bank, n: ps[:, bank, 256 * n:256 * n + 256].rearrange("p (m i) -> p m i", i=CH)
        mask = lambda n: masks[:, n:n + 1, :].to_broadcast([P, NT, CH])
        at_chunk = lambda c: slice(c * CH, c * CH + CH)

        @block.sync
        def _(sp):
            sp.dma_start(conv[:], conv_dram).then_inc(consts, 16)
            sp.dma_start(norm[:], norm_dram).then_inc(consts, 16)
            sp.dma_start(masks[:], masks_dram).then_inc(consts, 16)

            def rows_of(f):
                head = rows_dram[bass.ds(f, 1), :, :]
                sp.wait_ge(dve_front.sem, dve_front.after("diff", f - 1))
                for a in (0, 1):
                    src = head[:, 0, :].rearrange("x (m a i) -> x m a i", a=2, i=CH)[:, :, a, :]
                    sp.dma_start(gc[CH * a:CH * a + CH, :, :], src.rearrange("x m i -> (x m) i").partition_broadcast(CH)) \
                        .then_inc(gc_in, 16)
                sp.wait_ge(dve_core.sem, dve_core.after("egl", f - 1))
                sp.dma_start(rows[:], head[:, 1:3, :].rearrange("x r t -> (x r) t").partition_broadcast(P)).then_inc(rows_in, 16)

            rows_of(0)
            with sp.Fori(1, HEADS) as f:
                w.load(sp, f)
                rows_of(f)

        @block.gpsimd
        def _(pool):
            with pool.Fori(1, HEADS) as f:
                w.low(pool, f)

        @block.scalar
        def _(act):
            def front(f, prepare):
                for n, t in enumerate("qk"):
                    act.wait_ge(dve_front.sem, dve_front.after(f"conv{CONV - 1}_{t}", f))
                    act.activation(act_y[:, n, :], y[:, n, :], ACT.Silu).then_inc(act_front.sem, 1)
                for n, t in enumerate("qk"):
                    act.wait_ge(act_front.sem, act_front.after(f"silu_{t}", f))
                    act.activation(sq[:, n, :], act_y[:, n, :], ACT.Square).then_inc(act_front.sem, 1)
                if prepare is not None:
                    w.high(act, prepare, (0, 1))
                act.wait_ge(dve_front.sem, dve_front.after("diff_masked", f))
                act.activation(decay[:], decay[:], ACT.Exp).then_inc(act_front.sem, 1)
                act.wait_ge(pe_front.sem, pe_front.after("sums", f))
                act.activation(var[:], ps[:, FRONT:FRONT + 2, :], ACT.Ln, bias=biases[:, 0:1]).then_inc(act_front.sem, 1)
                act.wait_ge(act_front.sem, act_front.after("ln", f))
                act.activation(var[:, 0, :], var[:, 0, :], ACT.Exp, bias=biases[:, 1:2], scale=-0.5).then_inc(act_front.sem, 1)
                act.activation(var[:, 1, :], var[:, 1, :], ACT.Exp, scale=-0.5).then_inc(act_front.sem, 1)
                act.wait_ge(dve_front.sem, dve_front.after(f"conv{CONV - 1}_v", f))
                act.activation(act_y[:, 2, :], y[:, 2, :], ACT.Silu).then_inc(act_front.sem, 1)
                act.wait_ge(pe_front.sem, pe_front.after("project_g", f))
                act.activation(o_b[:, bass.ds(f, 1), :].rearrange("p a t -> p (a t)"), ps[:, FRONT + 3, :],
                               ACT.Silu).then_inc(act_front.sem, 1)

            def square(h):
                act.wait_ge(pe_core.sem, pe_core.after(f"out{NCH - 1}", h))
                act.activation(osq[:], ps[:, OUT, :], ACT.Square).then_inc(act_tail.sem, 1)

            def tail(h):
                act.wait_ge(pe_tail.sem, pe_tail.after("out_sums", h))
                act.activation(ovar[:], ps[:, FRONT + 3, :], ACT.Ln, bias=biases[:, 0:1], scale=1.0 / HD).then_inc(act_tail.sem, 1)
                act.wait_ge(act_tail.sem, act_tail.after("ln_o", h))
                act.activation(ovar[:], ovar[:], ACT.Exp, scale=-0.5).then_inc(act_tail.sem, 1)

            act_front.open(act)
            act_tail.open(act)
            act.wait_ge(consts, 50)
            front(0, 1)
            w.high(act, 1, (2, 3))
            front(1, 2)
            square(0)
            w.high(act, 2, (2, 3))
            with act.Fori(1, HEADS - 2) as h:
                tail(h - 1)
                front(h + 1, h + 2)
                square(h)
                w.high(act, h + 2, (2, 3))
            tail(HEADS - 3)
            front(HEADS - 1, None)
            square(HEADS - 2)
            tail(HEADS - 2)
            square(HEADS - 1)
            tail(HEADS - 1)

        @block.tensor
        def _(pe):
            def sums(f):
                pe.wait_ge(act_front.sem, act_front.after("square_k", f))
                pe.matmul(ps[:, FRONT, :], ones[:], sq[:, 0, :], start=True, stop=True)
                pe.matmul(ps[:, FRONT + 1, :], ones[:], sq[:, 1, :], start=True, stop=True).then_inc(pe_front.sem, 1)

            class Projection:

                def __init__(self, f):
                    self.f, self.n = f, 0

                def go(self, count):
                    for _ in range(count if self.f is not None else 0):
                        m, k = divmod(self.n, KD)
                        if self.n == 0:
                            pe.wait_ge(act_front.sem, act_front.after("gate", self.f - 1))
                        ins = w.block(pe, self.f, m, k, ps[:, FRONT + m, :], h_hi, h_lo)
                        if k == KD - 1:
                            ins.then_inc(pe_front.sem, 1)
                        self.n += 1

            def tail(h):
                pe.wait_ge(act_tail.sem, act_tail.after("square_o", h))
                pe.matmul(ps[:, FRONT + 3, :], ones[:], osq[:], start=True, stop=True).then_inc(pe_tail.sem, 1)

            def core(h, f, last=None):
                fill = Projection(f)

                def dve(name):
                    pe.wait_ge(dve_core.sem, dve_core.after(name, h))
                    pe.sem_inc(passed, 1)

                pe.wait_ge(dve_front.sem, dve_front.after("kb", h))
                pe.sem_inc(passed, 1)
                for t in range(NT):
                    ins = pe.transpose(ps[:, KEY, P * t:P * t + P], kT[:, P * t:P * t + P], ident[:])
                ins.then_inc(pe_core.sem, 1)
                for m, a, c, half in halves:
                    pe.matmul(of(PAIR, 0)[half, m, :], kT[:, at_chunk(c)], kbT[:, at_chunk(c)], start=True, stop=True)
                for m, a, c, half in halves:
                    ins = pe.matmul(of(PAIR, 1)[half, m, :], kT[:, at_chunk(c)], qT[:, at_chunk(c)], start=True, stop=True)
                ins.then_inc(pe_core.sem, 1)
                fill.go(2)
                for l in range(LEVELS):
                    dve("A" if l == 0 else f"T{l - 1}")
                    for m, a, c, half in halves:
                        x = masks[half, LEVELS + 1, :] if l == 0 else T[half, m, :]
                        ins = pe.matmul(of(LOWER, 0)[half, m, :], AT[half, m, :], x, start=True, stop=True)
                    ins.then_inc(pe_core.sem, 1)
                    if l == 0 and last is not None:
                        tail(last)
                    fill.go(1)
                    if l == 1:
                        pe.wait_ge(dve_tail.sem, dve_tail.after("o_normed", h - 1))
                        pe.wait_ge(act_front.sem, act_front.after("silu_v", h))
                        pe.sem_inc(passed, 1)
                        for t in range(NT):
                            ins = pe.transpose(ps[:, OUT, P * t:P * t + P], act_y[:, 2, P * t:P * t + P], ident[:])
                        ins.then_inc(pe_core.sem, 1)
                    dve(f"P{l}")
                    for m, a, c, half in halves:
                        tt = masks[half, LEVELS + 1, :] if l == 0 else TT[half, m, :]
                        ins = pe.matmul(of(PAIR, 1)[half, m, :], prod[half, m, :], tt, start=True, stop=True)
                    if l < LEVELS - 1:
                        for m, a, c, half in halves:
                            tt = masks[half, LEVELS + 1, :] if l == 0 else TT[half, m, :]
                            ins = pe.matmul(of(PAIR, 0)[half, m, :], tt, prod[half, m, :], start=True, stop=True)
                    ins.then_inc(pe_core.sem, 1)
                    fill.go(2 if l < 2 else 1)
                dve(f"TT{LEVELS - 1}")
                for m, a, c, half in halves:
                    ins = pe.matmul(of((KEY, LOWER)[a], 0)[:, m, :], kbe[half, m, :], TT[half, m, :], start=True,
                                    stop=True)
                ins.then_inc(pe_core.sem, 1)
                fill.go(1)
                dve("nw_odd")
                for m, a, c, half in halves:
                    state = S[:, c % 2, :]
                    bank = PAIR + c % 2
                    ins = pe.matmul(ps[half, bank, 0:HD], TT[half, m, :], vb[half, m, :], start=True, stop=(c == 0))
                    if c == 0:
                        ins.then_inc(pe_core.sem, 1)
                    else:
                        dve(f"S{c - 1}")
                        pe.matmul(ps[half, bank, 0:HD], nwT[:, a, m, :], state, start=False,
                                  stop=True).then_inc(pe_core.sem, 1)
                        pe.matmul(ps[:, OUT, at_chunk(c)], state, qdT[:, at_chunk(c)], start=True, stop=False)
                    fill.go(1)
                    dve(f"vn{c}")
                    if c < NCH - 1:
                        pe.matmul(ps[:, KEY, HD * (c % 2):HD * (c % 2) + HD], kd[half, m, :], vn[half, :], start=True,
                                  stop=True).then_inc(pe_core.sem, 1)
                    pe.matmul(ps[:, OUT, at_chunk(c)], vn[half, :], attnT[half, m, :], start=(c == 0),
                              stop=True).then_inc(pe_core.sem, 1)
                    if c < NCH - 1:
                        if c == 3 and f is not None:
                            sums(f)
                        fill.go(1)
                assert f is None or fill.n == GROUPS

            pe_front.open(pe)
            pe_core.open(pe)
            pe_tail.open(pe)
            first = Projection(0)
            first.go(3 * KD)
            sums(0)
            first.go(KD)
            core(0, 1)
            with pe.Fori(1, HEADS - 1) as h:
                core(h, h + 1, h - 1)
            core(HEADS - 1, None, HEADS - 2)
            tail(HEADS - 1)

        @block.vector
        def _(dve):
            def own_front(name, f):
                dve.wait_ge(dve_front.sem, dve_front.after(name, f))

            def tap(f, t, s):
                if f is None:
                    return
                n = "qkv".index(t)
                x = conv[:, bass.ds(f, 1), n, CONV - 1 - s:CONV - s].rearrange("p a b -> p (a b)")
                if s == 0:
                    dve.wait_ge(pe_front.sem, pe_front.after(f"project_{t}", f))
                    dve.tensor_scalar(y[:, n, :], ps[:, FRONT + n, :], x, None, ALU.mult).then_inc(dve_front.sem, 1)
                else:
                    own_front(f"conv{s - 1}_{t}", f)
                    dve.scalar_tensor_tensor(out=y[:, n, s:], in0=ps[:, FRONT + n, :TOK - s], scalar=x, in1=y[:, n, s:],
                                             op0=ALU.mult, op1=ALU.add).then_inc(dve_front.sem, 1)

            def head_col(h, kind, width):
                return cols[:, kind, :, bass.ds(h, 1)].to_broadcast([P, NT, width])

            def diff(f):
                if f is None:
                    return
                dve.wait_ge(gc_in, 32 * (f + 1))
                dve.tensor_tensor(decay[:], gc[:], head_col(f, GC, CH), ALU.subtract).then_inc(dve_front.sem, 1)

            def diff_masked(f):
                if f is None:
                    return
                own_front("diff", f)
                dve.tensor_tensor(decay[:], decay[:], mask(LEVELS), ALU.add).then_inc(dve_front.sem, 1)

            def normed(f, t):
                if f is None:
                    return
                dve.wait_ge(act_front.sem, act_front.after(f"root_{t}", f))
                n = "qk".index(t)
                dve.tensor_tensor((qT, kT)[n][:], act_y[:, n, :], var[:, n, :], ALU.mult).then_inc(dve_front.sem, 1)

            def beta_keys(f):
                if f is None:
                    return
                own_front("k", f)
                dve.wait_ge(rows_in, 16 * (f + 1))
                dve.tensor_tensor(kbT[:], kT[:], rows[:, 0, :], ALU.mult).then_inc(dve_front.sem, 1)

            def tail(h):
                dve.wait_ge(act_tail.sem, act_tail.after("root_o", h))
                dve.tensor_tensor(o1[:], ps[:, OUT, :], ovar[:], ALU.mult).then_inc(dve_tail.sem, 1)
                dve.wait_ge(dve_tail.sem, dve_tail.after("o_normed", h))
                at = o_b[:, bass.ds(h, 1), :].rearrange("p a t -> p (a t)")
                dve.scalar_tensor_tensor(out=at, in0=o1[:], scalar=norm[:, 0:1], in1=at, op0=ALU.mult,
                                         op1=ALU.mult).then_inc(dve_tail.sem, 1)

            def core(h, f, last=None):
                done = dve_core.sem

                def pe(name):
                    dve.wait_ge(pe_core.sem, pe_core.after(name, h))

                four = lambda bank: ps[:, bank, :].rearrange("p (m e) -> p m e", e=HD)
                pe("gram")
                dve.wait_ge(act_front.sem, act_front.after("decay", h))
                dve.tensor_tensor(AT[:], of(PAIR, 0), decay[:], ALU.mult).then_inc(done, 1)
                dve.tensor_tensor(attnT[:], of(PAIR, 1), decay[:], ALU.mult).then_inc(done, 1)
                for l in range(LEVELS):
                    pe(f"AxT{l}")
                    dve.tensor_tensor(prod[:], of(LOWER, 0), mask(l), ALU.mult).then_inc(done, 1)
                    if l == 0:
                        dve.tensor_tensor(kbe[:], four(KEY), head_col(h, BEGC, HD), ALU.mult).then_inc(done, 1)
                        if last is not None:
                            tail(last)
                    if l == 1:
                        dve.tensor_tensor(kd[:], four(KEY), head_col(h, ELAST, HD), ALU.mult).then_inc(done, 1)
                    if l == 2:
                        pe("turn_v")
                        dve.tensor_tensor(vb[:], four(OUT), head_col(h, BETA, HD), ALU.mult).then_inc(done, 1)
                    if l == 3:
                        dve.tensor_tensor(qdT[:], qT[:], rows[:, 1, :], ALU.mult).then_inc(done, 1)
                        dve.tensor_copy(egl[:], rows[:, 1, CH - 1:TOK:CH]).then_inc(done, 1)
                    if l >= 4:
                        tap(f, "q", l - 4)
                    pe(f"TxP{l}")
                    if l < LEVELS - 1:
                        dve.tensor_tensor(T[:], mask(LEVELS + 1) if l == 0 else T[:], of(PAIR, 0),
                                          ALU.subtract).then_inc(done, 1)
                    dve.tensor_tensor(TT[:], mask(LEVELS + 1) if l == 0 else TT[:], of(PAIR, 1),
                                      ALU.subtract).then_inc(done, 1)
                tap(f, "q", 2)
                pe("wT")
                for a, bank in enumerate((KEY, LOWER)):
                    dve.tensor_scalar(nwT[:, a], of(bank, 0), -1.0, None, ALU.mult).then_inc(done, 1)
                fillers = [[lambda: tap(f, "q", 3), lambda: tap(f, "k", 0)],
                           [lambda: tap(f, "k", 1), lambda: tap(f, "k", 2)],
                           [lambda: tap(f, "k", 3), lambda: diff(f)],
                           [lambda: diff_masked(f), lambda: None],
                           [lambda: tap(f, "v", 0), lambda: tap(f, "v", 1)],
                           [lambda: tap(f, "v", 2), lambda: tap(f, "v", 3)],
                           [lambda: normed(f, "q"), lambda: normed(f, "k")],
                           [lambda: beta_keys(f), lambda: None]]
                for m, a, c, half in halves:
                    pe(f"v_new{c}")
                    dve.tensor_copy(vn[half, :], ps[half, PAIR + c % 2, 0:HD]).then_inc(done, 1)
                    fillers[c][0]()
                    state = ps[:, KEY, HD * (c % 2):HD * (c % 2) + HD]
                    if c == 0:
                        pe("state0")
                        dve.tensor_copy(S[:, 1, :], state).then_inc(done, 1)
                    elif c < NCH - 1:
                        pe(f"state{c}")
                        dve.scalar_tensor_tensor(out=S[:, (c + 1) % 2, :], in0=S[:, c % 2, :],
                                                 scalar=egl[:, c:c + 1], in1=state,
                                                 op0=ALU.mult, op1=ALU.add).then_inc(done, 1)
                    fillers[c][1]()

            dve_front.open(dve)
            dve_core.open(dve)
            dve_tail.open(dve)
            dve.memset(biases[:, 0:1], EPS).then_inc(consts, 1)
            dve.memset(biases[:, 1:2], -0.5 * math.log(HD)).then_inc(consts, 1)
            dve.wait_ge(consts, 50)
            for t in "qk":
                for s in range(CONV):
                    tap(0, t, s)
            diff(0)
            diff_masked(0)
            for s in range(CONV):
                tap(0, "v", s)
            normed(0, "q")
            normed(0, "k")
            beta_keys(0)
            core(0, 1)
            with dve.Fori(1, HEADS - 1) as h:
                core(h, h + 1, h - 1)
            core(HEADS - 1, None, HEADS - 2)
            tail(HEADS - 1)


def mixer_a(nc, h_hi, h_lo, w_a, bias_dram, gains_dram, ident, halves, o_a):
    HW = 64
    with ExitStack() as ctx:
        def sb(name, shape, dt=F32):
            return ctx.enter_context(nc.sbuf_tensor(f"ma_{name}", shape, dt))

        def sem(name):
            return ctx.enter_context(nc.semaphore(f"ma_{name}"))

        gains = sb("gains", [P, 2])
        eps = sb("eps", [P, 1])
        bias = sb("bias", [P, 2, TOK])
        sq = sb("sq", [P, 2, TOK])
        var = sb("var", [P, 2, TOK])
        q = sb("q", [P, TOK])
        kk = sb("k", [P, TOK])
        vT = sb("vT", [P, TOK])
        v = sb("v", [P, NT, P])
        sc = sb("sc", [P, 2, NT, TOK])
        top = sb("top", [P, 2, NT])
        total = sb("total", [P, 2, NT])
        pT = sb("pT", [P, 2, NT, TOK])
        ps = ctx.enter_context(nc.psum_tensor("ma_ps", [P, 8, TOK], F32))
        SUMS, TURN = 3, 6
        SCORE = [(3, 0), (3, P), (4, 0), (5, 0)]
        consts = sem("consts")
        passed = sem("passed")
        bias_in = sem("bias_in")
        bias_masked = sem("bias_masked")
        T = range(NT)
        pe_front = Steps(sem("pe_front"), ["q", "k", "sums", "v"])
        pe_core = Steps(sem("pe_core"), ["turn_v"] + [f"score{a}{t}" for a in (0, 1) for t in T if t]
                        + [n for a in (0, 1) for n in [f"turn{a}{b}" for b in T] + [f"pv{a}"]])
        w = Weights(ctx, nc, "ma", w_a, [KD, KD, KD], pe_front, ["q", "k", "v"])
        act_front = Steps(sem("act_front"), ["sq_q", "sq_k", "ln", "root", "v"])
        act_core = Steps(sem("act_core"), [f"exp{a}{t}" for a in (0, 1) for t in T] + [f"pT{a}{b}" for a in (0, 1) for b in T])
        dve_front = Steps(sem("dve_front"), ["q", "k"])
        dve_core = Steps(sem("dve_core"), ["v"] + [f"{s}{a}{t}" for a in (0, 1) for t in T for s in ("sc", "top")]
                         + [f"{s}{a}{t}" for a in (0, 1) for t in T for s in ("inv", "p")] + ["o0", "o1"])
        block = ctx.enter_context(nc.Block())
        TURNS = HEADS // 2
        half = lambda a: slice(HW * a, HW * a + HW)
        width = lambda t: P * (t + 1)

        def scores(t):
            bank, at = SCORE[t]
            return ps[:, bank, at:at + width(t)]

        @block.sync
        def _(sp):
            sp.dma_start(gains[:], gains_dram).then_inc(consts, 16)
            with sp.Fori(0, TURNS) as j:
                w.load(sp, j)
                sp.wait_ge(dve_core.sem, dve_core.after(f"sc1{NT - 1}", j - 1))
                sp.dma_start(bias[:], bias_dram[bass.ds(j, 1), :, :, :].rearrange("a p h t -> (a p) h t")).then_inc(bias_in, 16)

        @block.gpsimd
        def _(pool):
            def mask(j):
                pool.wait_ge(bias_in, 16 * (j + 1))
                pool.sem_inc(passed, 1)
                pool.memset(bias[0:CH, :, TOK - CH:TOK], NEG).then_inc(bias_masked, 1)

            w.lo_made.open(pool)
            w.low(pool, 0)
            with pool.Fori(0, TURNS - 1) as j:
                mask(j)
                w.low(pool, j + 1)
            mask(TURNS - 1)

        @block.scalar
        def _(act):
            def squares(f):
                for n, t in enumerate("qk"):
                    act.wait_ge(pe_front.sem, pe_front.after(t, f))
                    act.activation(sq[:, n, :], ps[:, n, :], ACT.Square).then_inc(act_front.sem, 1)

            def roots(f):
                act.wait_ge(pe_front.sem, pe_front.after("sums", f))
                act.activation(var[:], ps[:, SUMS:SUMS + 2, :], ACT.Ln, bias=eps[:], scale=1.0 / HW).then_inc(act_front.sem, 1)
                act.wait_ge(act_front.sem, act_front.after("ln", f))
                act.activation(var[:], var[:], ACT.Exp, scale=-0.5).then_inc(act_front.sem, 1)

            def values(f):
                act.wait_ge(pe_front.sem, pe_front.after("v", f))
                act.copy(vT[:], ps[:, 2, :]).then_inc(act_front.sem, 1)

            def turn_over(h, a):
                for b in T:
                    act.wait_ge(pe_core.sem, pe_core.after(f"turn{a}{b}", h))
                    act.copy(pT[:, a, b, P * b:TOK], ps[:, TURN + (a + b) % 2, P * b:TOK]).then_inc(act_core.sem, 1)

            def turn(h, f, prepare):
                for a in (0, 1):
                    for t in T:
                        act.wait_ge(dve_core.sem, dve_core.after(f"top{a}{t}", h))
                        act.activation(sc[:, a, t, 0:width(t)], sc[:, a, t, 0:width(t)], ACT.Exp,
                                       bias=top[:, a, t:t + 1],
                                       accum_out=total[:, a, t:t + 1]).then_inc(act_core.sem, 1)
                if f is not None:
                    squares(f)
                turn_over(h, 0)
                if f is not None:
                    roots(f)
                turn_over(h, 1)
                if f is not None:
                    values(f)
                if prepare is not None:
                    w.high(act, prepare)

            w.hi_made.open(act)
            act_front.open(act)
            act_core.open(act)
            act.wait_ge(consts, 17)
            w.high(act, 0)
            squares(0)
            roots(0)
            values(0)
            w.high(act, 1)
            with act.Fori(0, TURNS - 2) as h:
                turn(h, h + 1, h + 2)
            turn(TURNS - 2, TURNS - 1, None)
            turn(TURNS - 1, None, None)

        @block.tensor
        def _(pe):
            class Projection:

                def __init__(self, f):
                    self.f, self.n = f, 0

                def go(self, count):
                    for _ in range(count if self.f is not None else 0):
                        m, k = divmod(self.n, KD)
                        ins = w.block(pe, self.f, m, k, ps[:, m, :], h_hi, h_lo)
                        if k == KD - 1:
                            ins.then_inc(pe_front.sem, 1)
                        self.n += 1

            def sums(f):
                pe.wait_ge(act_front.sem, act_front.after("sq_k", f))
                pe.matmul(ps[:, SUMS, :], halves[:], sq[:, 0, :], start=True, stop=True)
                pe.matmul(ps[:, SUMS + 1, :], halves[:], sq[:, 1, :], start=True, stop=True).then_inc(pe_front.sem, 1)

            def core(h, f):
                fill = Projection(f)

                def dve(name, turn=h):
                    pe.wait_ge(dve_core.sem, dve_core.after(name, turn))
                    pe.sem_inc(passed, 1)

                def act(name):
                    pe.wait_ge(act_core.sem, act_core.after(name, h))
                    pe.sem_inc(passed, 1)

                def score(a):
                    for t in T:
                        if a == 1:
                            dve(f"sc0{max(t, 1)}")
                        ins = pe.matmul(scores(t), q[half(a), P * t:P * t + P], kk[half(a), 0:width(t)],
                                        start=True, stop=True)
                        if t:
                            ins.then_inc(pe_core.sem, 1)

                def turn_over(a, fills):
                    for b in T:
                        if b >= 2:
                            act(f"pT{a}{b - 2}")
                        elif b == 1:
                            dve(*(("o0", h) if a == 1 else ("o1", h - 1)))
                        for t in range(b, NT):
                            if b == 0:
                                dve(f"p{a}{t}")
                            ins = pe.transpose(ps[:, TURN + (a + b) % 2, P * t:P * t + P], sc[:, a, t, P * b:P * b + P],
                                               ident[:])
                        ins.then_inc(pe_core.sem, 1)
                        fill.go(fills)
                    for b in T:
                        act(f"pT{a}{max(b, NT - 2)}")
                        ins = pe.matmul(ps[:, TURN + a, P * b:TOK], v[:, b, :], pT[:, a, b, P * b:TOK], start=(b == 0),
                                        stop=(b == NT - 1))
                    ins.then_inc(pe_core.sem, 1)

                pe.wait_ge(act_front.sem, act_front.after("v", h))
                dve("o1", h - 1)
                for t in T:
                    ins = pe.transpose(ps[:, TURN + 1, P * t:P * t + P], vT[:, P * t:P * t + P], ident[:])
                ins.then_inc(pe_core.sem, 1)
                pe.wait_ge(dve_front.sem, dve_front.after("k", h))
                pe.sem_inc(passed, 1)
                score(0)
                fill.go(4)
                score(1)
                fill.go(12)
                turn_over(0, 1)
                if f is not None:
                    dve(f"sc1{NT - 2}")
                    sums(f)
                turn_over(1, 1)
                assert f is None or fill.n == 3 * KD

            pe_front.open(pe)
            pe_core.open(pe)
            first = Projection(0)
            first.go(2 * KD)
            sums(0)
            first.go(KD)
            with pe.Fori(0, TURNS - 1) as h:
                core(h, h + 1)
            core(TURNS - 1, None)

        @block.vector
        def _(dve):
            def normed(f):
                if f is None:
                    return
                dve.wait_ge(act_front.sem, act_front.after("root", f))
                for n, out in enumerate((q, kk)):
                    dve.scalar_tensor_tensor(out=out[:], in0=ps[:, n, :], scalar=gains[:, n:n + 1], in1=var[:, n, :],
                                             op0=ALU.mult, op1=ALU.mult).then_inc(dve_front.sem, 1)

            def core(h, f):
                done = dve_core.sem

                def own(name):
                    dve.wait_ge(done, dve_core.after(name, h))

                def pe(name):
                    dve.wait_ge(pe_core.sem, pe_core.after(name, h))

                def output(a):
                    pe(f"pv{a}")
                    dve.tensor_copy(o_a[half(a), bass.ds(h, 1), :].rearrange("p a t -> p (a t)"),
                                    ps[half(a), TURN + a, :]).then_inc(done, 1)

                pe("turn_v")
                dve.tensor_copy(v[:].rearrange("p t c -> p (t c)"), ps[:, TURN + 1, :]).then_inc(done, 1)
                dve.wait_ge(bias_masked, h + 1)
                for a in (0, 1):
                    for t in T:
                        s_t = sc[:, a, t, 0:width(t)]
                        pe(f"score{a}{max(t, 1)}")
                        dve.scalar_tensor_tensor(out=s_t, in0=scores(t), scalar=HW ** -0.5,
                                                 in1=bias[:, a, TOK - width(t):TOK], op0=ALU.mult,
                                                 op1=ALU.add).then_inc(done, 1)
                        own(f"sc{a}{t}")
                        dve.tensor_reduce(top[:, a, t:t + 1], s_t, AX.X, ALU.max, negate=True).then_inc(done, 1)
                for a in (0, 1):
                    for t in T:
                        s_t = sc[:, a, t, 0:width(t)]
                        dve.wait_ge(act_core.sem, act_core.after(f"exp{a}{t}", h))
                        dve.reciprocal(total[:, a, t:t + 1], total[:, a, t:t + 1]).then_inc(done, 1)
                        own(f"inv{a}{t}")
                        dve.tensor_scalar(s_t, s_t, total[:, a, t:t + 1], None, ALU.mult).then_inc(done, 1)
                output(0)
                normed(f)
                output(1)

            dve_front.open(dve)
            dve_core.open(dve)
            dve.memset(eps[:], EPS).then_inc(consts, 1)
            dve.wait_ge(consts, 17)
            normed(0)
            with dve.Fori(0, TURNS - 1) as h:
                core(h, h + 1)
            core(TURNS - 1, None)


def merge(nc, tag, w_dram, pieces, h_hi, h_lo, o_a, ob, b_merge_dram, mixed_hi, mixed_lo):
    with ExitStack() as ctx:
        def sb(name, shape, dt=F32):
            return ctx.enter_context(nc.sbuf_tensor(f"{tag}_{name}", shape, dt))

        def sem(name):
            return ctx.enter_context(nc.semaphore(f"{tag}_{name}"))

        NA = A_W // P
        oa_parts = sb("oa_parts", [P, 2, NA, TOK], F32R)
        ob_parts = sb("ob_parts", [P, 2, KD, TOK], F32R)
        b_merge = sb("b_merge", [P, 2, KD])
        gates = sb("gates", [P, 2, TOK])
        full = sb("full", [P, TOK])
        ps = ctx.enter_context(nc.psum_tensor(f"{tag}_ps", [P, 4, TOK], F32))
        loaded = sem("loaded")
        x_hi = sem("x_hi")
        x_lo = sem("x_lo")
        pe_done = Steps(sem("pe_done"), ["gate_a", "gate_b", "proj_a", "proj_b"])
        w = Weights(ctx, nc, tag, w_dram, pieces, pe_done, ["gate_a", "gate_b", "proj_a", "proj_b"])
        act_done = Steps(sem("act_done"), ["gate_a", "gate_b", "high"])
        dve_done = Steps(sem("dve_done"), ["part_a", "part_b", "sum", "low"])
        block = ctx.enter_context(nc.Block())

        @block.sync
        def _(sp):
            sp.dma_start(b_merge[:], b_merge_dram).then_inc(loaded, 16)
            with sp.Fori(0, KD) as n:
                w.load(sp, n)

        @block.gpsimd
        def _(pool):
            w.lo_made.open(pool)
            with pool.Fori(0, KD) as n:
                w.low(pool, n)

        @block.scalar
        def _(act):
            w.hi_made.open(act)
            act_done.open(act)
            act.wait_ge(loaded, 16)

            def turn(n, last=False):
                for g, name in enumerate(("gate_a", "gate_b")):
                    act.wait_ge(pe_done.sem, pe_done.after(name, n))
                    act.activation(gates[:, g, :], ps[:, g, :], ACT.Sigmoid,
                                   bias=b_merge[:, g, bass.ds(n, 1)]).then_inc(act_done.sem, 1)
                    if not last:
                        w.high(act, n + 1, [g])
                if not last:
                    w.high(act, n + 1, [2, 3])
                act.wait_ge(dve_done.sem, dve_done.after("sum", n))
                act.copy(mixed_hi[:, bass.ds(n, 1), :].rearrange("p a t -> p (a t)"), full[:]).then_inc(act_done.sem, 1)

            w.high(act, 0, [0, 1])
            act.copy(oa_parts[:, 0, :, :], o_a[:]).then_inc(x_hi, 1)
            act.copy(ob_parts[:, 0, :, :], ob[:]).then_inc(x_hi, 1)
            w.high(act, 0, [2, 3])
            with act.Fori(0, KD - 1) as n:
                turn(n)
            turn(KD - 1, last=True)

        @block.tensor
        def _(pe):
            pe_done.open(pe)
            with pe.Fori(0, KD) as n:
                w.product(pe, n, 0, ps[:, 0, :], h_hi, h_lo).then_inc(pe_done.sem, 1)
                w.product(pe, n, 1, ps[:, 1, :], h_hi, h_lo).then_inc(pe_done.sem, 1)
                pe.wait_ge(x_lo, 2)
                pe.wait_ge(dve_done.sem, dve_done.after("part_b", n - 1))
                w.product(pe, n, 2, ps[:, 2, :], oa_parts[:, 0, :, :], oa_parts[:, 1, :, :]).then_inc(pe_done.sem, 1)
                w.product(pe, n, 3, ps[:, 3, :], ob_parts[:, 0, :, :], ob_parts[:, 1, :, :]).then_inc(pe_done.sem, 1)

        @block.vector
        def _(dve):
            dve_done.open(dve)
            dve.wait_ge(x_hi, 2)
            dve.tensor_tensor(oa_parts[:, 1, :, :], o_a[:], oa_parts[:, 0, :, :].bitcast(F32), ALU.subtract).then_inc(x_lo, 1)
            dve.tensor_tensor(ob_parts[:, 1, :, :], ob[:], ob_parts[:, 0, :, :].bitcast(F32), ALU.subtract).then_inc(x_lo, 1)
            with dve.Fori(0, KD) as n:
                for g, name in enumerate(("gate_a", "gate_b")):
                    dve.wait_ge(pe_done.sem, pe_done.after("proj" + name[4:], n))
                    dve.wait_ge(act_done.sem, act_done.after(name, n))
                    dve.tensor_tensor(gates[:, g, :], gates[:, g, :], ps[:, 2 + g, :], ALU.mult).then_inc(dve_done.sem, 1)
                dve.wait_ge(dve_done.sem, dve_done.after("part_b", n))
                dve.tensor_tensor(full[:], gates[:, 0, :], gates[:, 1, :], ALU.add).then_inc(dve_done.sem, 1)
                dve.wait_ge(act_done.sem, act_done.after("high", n))
                at = bass.ds(n, 1)
                dve.tensor_tensor(mixed_lo[:, at, :].rearrange("p a t -> p (a t)"), full[:],
                                  mixed_hi[:, at, :].bitcast(F32).rearrange("p a t -> p (a t)"),
                                  ALU.subtract).then_inc(dve_done.sem, 1)


def project_out(nc, w_dram, mixed_hi, mixed_lo, xT):
    with ExitStack() as ctx:
        sem = lambda name: ctx.enter_context(nc.semaphore(f"po_{name}"))
        ps = ctx.enter_context(nc.psum_tensor("po_ps", [P, 2, TOK], F32))
        made = Steps(sem("made"), range(2))
        added = Steps(sem("added"), range(2))
        w = Weights(ctx, nc, "po", w_dram, [KD, KD], made, range(2))
        block = ctx.enter_context(nc.Block())
        TURNS = KD // 2

        @block.sync
        def _(sp):
            with sp.Fori(0, TURNS) as n:
                w.load(sp, n)

        @block.gpsimd
        def _(pool):
            w.lo_made.open(pool)
            with pool.Fori(0, TURNS) as n:
                w.low(pool, n)

        @block.scalar
        def _(act):
            w.hi_made.open(act)
            with act.Fori(0, TURNS) as n:
                w.high(act, n)

        @block.tensor
        def _(pe):
            made.open(pe)
            with pe.Fori(0, TURNS) as n:
                for m in range(2):
                    pe.wait_ge(added.sem, added.after(m, n - 1))
                    w.product(pe, n, m, ps[:, m, :], mixed_hi, mixed_lo).then_inc(made.sem, 1)

        @block.vector
        def _(dve):
            added.open(dve)
            with dve.Fori(0, TURNS) as n:
                for m in range(2):
                    x = xT[:, bass.ds(2 * n + m, 1), :].rearrange("p a t -> p (a t)")
                    dve.wait_ge(made.sem, made.after(m, n))
                    dve.tensor_tensor(x, x, ps[:, m, :], ALU.add).then_inc(added.sem, 1)


KEYS = 128
TOP = 16


def choose_experts(nc, w, wd, keys_dram, iota_dram, h_hi, h_lo, sel, early_dram):
    PAIRS = early_dram.shape[0] // 2
    with ExitStack() as ctx:
        def sb(name, shape, dt=F32):
            return ctx.enter_context(nc.sbuf_tensor(f"ce_{name}", shape, dt))

        def sem(name):
            return ctx.enter_context(nc.semaphore(f"ce_{name}"))

        keys = sb("keys", [P, 2, KEYS])
        iota = sb("iota", [P, TOP])
        q = sb("q", [P, 2, TOK])
        s = sb("s", [P, 2, NT, KEYS])
        rest = sb("rest", [P, 2, NT, KEYS])
        best = sb("best", [P, 2, NT, TOP])
        place = sb("place", [P, 2, NT, TOP], U32)
        place_f = sb("place_f", [P, 2, NT, TOP])
        cand = sb("cand", [P, NT, TOP * TOP])
        cand_rest = sb("cand_rest", [P, NT, TOP * TOP])
        top = sb("top", [P, NT, TOP])
        pos = sb("pos", [P, NT, TOP], U32)
        pos_part = sb("pos_part", [P, 2, NT, TOP], U32)
        pos_f = sb("pos_f", [P, 2, NT, TOP])
        hot = sb("hot", [P, 2, NT * TOP, TOP])
        e = sb("e", [P, NT, HEADS, TOP])
        total = sb("total", [P, NT, HEADS])
        gelu = sb("gelu", [P, 2, TOK])
        ps = ctx.enter_context(nc.psum_tensor("ce_ps", [P, 6, TOK], F32))
        consts = sem("consts")
        keys_in = sem("keys_in")
        passed = sem("passed")
        pe_done = Steps(sem("pe_done"), ["q0", "q1", "s0", "s1"])
        w.serve(pe_done, ["q0", "q1"])
        pe_down = Steps(sem("pe_down"), range(2))
        wd.serve(pe_down, range(2))
        act_done = Steps(sem("act_done"), ["q0", "q1", "s0", "s1"])
        act_gelu = Steps(sem("act_gelu"), range(2))
        early_stored = [sem("early_stored0"), sem("early_stored1")]
        exp_made = sem("exp_made")
        softmax = sem("softmax")
        dve_done = Steps(sem("dve_done"), ["max1", "at1", "drop", "max2", "at2", "index0", "index1", "place_f", "cand", "cmax1", "cat1",
                                           "cdrop", "cmax2", "cat2", "row", "col", "pos_f", "hot0", "hot1", "minus"])
        pool_done = Steps(sem("pool_done"), ["pick0", "pick1"])
        block = ctx.enter_context(nc.Block())

        @block.sync
        def _(sp):
            sp.dma_start(iota[:], iota_dram).then_inc(consts, 16)

            def load_keys(h):
                sp.wait_ge(pe_done.sem, pe_done.after("s1", h - 1))
                sp.dma_start(keys[:], keys_dram[bass.ds(h, 1), :, :, :].rearrange("a p s k -> (a p) s k")).then_inc(keys_in, 16)

            load_keys(0)
            with sp.Fori(1, HEADS) as h:
                w.load(sp, h)
                wd.load(sp, h)
                load_keys(h)
            for d in range(HEADS, PAIRS):
                wd.load(sp, d)

        @block.gpsimd
        def _(pool):
            pool_done.open(pool)

            def turn(h, last=False):
                if not last:
                    w.low(pool, h + 1)
                    wd.low(pool, h + 1)
                else:
                    for d in range(HEADS, PAIRS):
                        wd.low(pool, d)
                for m in (0, 1):
                    four = hot[:, m, :, :].rearrange("p (t k) r -> p t k r", t=NT)
                    pool.wait_ge(dve_done.sem, dve_done.after(f"hot{m}", h))
                    pool.sem_inc(passed, 1)
                    pool.tensor_tensor(four, four, place_f[:, m, :, :].unsqueeze(2).to_broadcast([P, NT, TOP, TOP]),
                                       ALU.mult).then_inc(pool_done.sem, 1)

            with pool.Fori(0, HEADS - 1) as h:
                turn(h)
            turn(HEADS - 1, last=True)

        @block.scalar
        def _(act):
            act_done.open(act)
            act_gelu.open(act)
            for stored in early_stored:
                act.sem_inc(stored, 16)

            def down(d, m, last=False):
                act.wait_ge(early_stored[m], 16 * (d + 1))
                act.wait_ge(pe_down.sem, pe_down.after(m, d))
                act.activation(gelu[:, m, :], ps[:, 4 + m, :], ACT.Gelu).then_inc(act_gelu.sem, 1)
                if not last:
                    wd.high(act, d + 1, [m])
                act.wait_ge(act_gelu.sem, act_gelu.after(m, d))
                act.dma_start(early_dram[bass.ds(2 * d + m, 1), :, :].rearrange("a p t -> (a p) t"),
                              gelu[:, m, :]).then_inc(early_stored[m], 16)

            def turn(h, last=False):
                for m in (0, 1):
                    act.wait_ge(pe_done.sem, pe_done.after(f"q{m}", h))
                    act.copy(q[:, m, :], ps[:, m, :]).then_inc(act_done.sem, 1)
                    if not last:
                        w.high(act, h + 1, [m])
                down(h, 0)
                act.wait_ge(dve_done.sem, dve_done.after("drop", h - 1))
                for m in (0, 1):
                    act.wait_ge(pe_done.sem, pe_done.after(f"s{m}", h))
                    act.copy(s[:, m, :, :].rearrange("p t k -> p (t k)"), ps[:, 2 + m, :]).then_inc(act_done.sem, 1)
                down(h, 1)

            with act.Fori(0, HEADS - 1) as h:
                turn(h)
            turn(HEADS - 1, last=True)
            for d in range(HEADS, PAIRS):
                for m in (0, 1):
                    if (d, m) == (PAIRS - 1, 1):
                        act.wait_ge(dve_done.sem, dve_done.after("minus", HEADS - 1))
                        act.activation(e[:], e[:], ACT.Exp).then_inc(exp_made, 1)
                    down(d, m, last=(d == PAIRS - 1))
            for stored in early_stored:
                act.wait_ge(stored, 16 * (PAIRS + 1))

        @block.tensor
        def _(pe):
            def down(d, m):
                wd.product(pe, d, m, ps[:, 4 + m, :], h_hi, h_lo).then_inc(pe_down.sem, 1)

            pe_done.open(pe)
            pe_down.open(pe)
            with pe.Fori(0, HEADS) as h:
                for m in (0, 1):
                    w.product(pe, h, m, ps[:, m, :], h_hi, h_lo).then_inc(pe_done.sem, 1)
                down(h, 0)
                pe.wait_ge(keys_in, 16 * (h + 1))
                for m in (0, 1):
                    pe.wait_ge(act_done.sem, act_done.after(f"q{m}", h))
                    for t in range(NT):
                        ins = pe.matmul(ps[:, 2 + m, P * t:P * t + P], q[:, m, P * t:P * t + P], keys[:, m, :],
                                        start=True, stop=True)
                    ins.then_inc(pe_done.sem, 1)
                down(h, 1)
            for d in range(HEADS, PAIRS):
                down(d, 0)
                down(d, 1)

        @block.vector
        def _(dve):
            done = dve_done.sem

            def index(h):
                for m in (0, 1):
                    dve.wait_ge(pool_done.sem, pool_done.after(f"pick{m}", h))
                    dve.sem_inc(passed, 1)
                    dve.tensor_reduce(sel[:, 1 + m, :, bass.ds(h, 1), :].rearrange("p t a k -> p t (a k)"),
                                      hot[:, m, :, :].rearrange("p (t k) r -> p t k r", t=NT), AX.X,
                                      ALU.add).then_inc(done, 1)

            def turn(h, is_first=False):
                first, second = slice(0, 8), slice(8, 16)
                pairs = [(m, t) for m in (0, 1) for t in range(NT)]

                def own(name):
                    dve.wait_ge(done, dve_done.after(name, h))
                    dve.sem_inc(passed, 1)

                dve.wait_ge(act_done.sem, act_done.after("s1", h))
                dve.sem_inc(passed, 1)
                for m, t in pairs:
                    ins = dve.max(best[:, m, t, first], s[:, m, t, :])
                ins.then_inc(done, 1)
                own("max1")
                for m, t in pairs:
                    ins = dve.max_index(place[:, m, t, first], best[:, m, t, first], s[:, m, t, :])
                ins.then_inc(done, 1)
                for m, t in pairs:
                    ins = dve.match_replace(rest[:, m, t, :], best[:, m, t, first], s[:, m, t, :], -3.0e38)
                ins.then_inc(done, 1)
                own("drop")
                for m, t in pairs:
                    ins = dve.max(best[:, m, t, second], rest[:, m, t, :])
                ins.then_inc(done, 1)
                own("max2")
                for m, t in pairs:
                    ins = dve.max_index(place[:, m, t, second], best[:, m, t, second], rest[:, m, t, :])
                ins.then_inc(done, 1)
                own("at2")
                if is_first:
                    dve.sem_inc(done, 2)
                else:
                    index(h - 1)
                dve.tensor_copy(place_f[:], place[:]).then_inc(done, 1)
                dve.tensor_tensor(cand[:].rearrange("p t (a b) -> p t a b", a=TOP),
                                  best[:, 0, :, :].unsqueeze(3).to_broadcast([P, NT, TOP, TOP]),
                                  best[:, 1, :, :].unsqueeze(2).to_broadcast([P, NT, TOP, TOP]),
                                  ALU.add).then_inc(done, 1)
                own("cand")
                for t in range(NT):
                    ins = dve.max(top[:, t, first], cand[:, t, :])
                ins.then_inc(done, 1)
                own("cmax1")
                for t in range(NT):
                    ins = dve.max_index(pos[:, t, first], top[:, t, first], cand[:, t, :])
                ins.then_inc(done, 1)
                for t in range(NT):
                    ins = dve.match_replace(cand_rest[:, t, :], top[:, t, first], cand[:, t, :], -3.0e38)
                ins.then_inc(done, 1)
                own("cdrop")
                for t in range(NT):
                    ins = dve.max(top[:, t, second], cand_rest[:, t, :])
                ins.then_inc(done, 1)
                own("cmax2")
                for t in range(NT):
                    ins = dve.max_index(pos[:, t, second], top[:, t, second], cand_rest[:, t, :])
                ins.then_inc(done, 1)
                own("cat2")
                dve.tensor_scalar(pos_part[:, 0, :, :], pos[:], 4, None, ALU.logical_shift_right).then_inc(done, 1)
                dve.tensor_scalar(pos_part[:, 1, :, :], pos[:], TOP - 1, None, ALU.bitwise_and).then_inc(done, 1)
                own("col")
                dve.tensor_copy(pos_f[:], pos_part[:]).then_inc(done, 1)
                own("pos_f")
                for m in (0, 1):
                    dve.tensor_tensor(hot[:, m, :, :],
                                      pos_f[:, m, :, :].rearrange("p t k -> p (t k)").unsqueeze(2).to_broadcast([P, NT * TOP, TOP]),
                                      iota[:].unsqueeze(1).to_broadcast([P, NT * TOP, TOP]),
                                      ALU.is_equal).then_inc(done, 1)
                dve.tensor_tensor(e[:, :, bass.ds(h, 1), :].rearrange("p t a k -> p t (a k)"), top[:],
                                  top[:, :, 0:1].to_broadcast([P, NT, TOP]), ALU.subtract).then_inc(done, 1)
            dve_done.open(dve)
            dve.wait_ge(consts, 16)
            turn(0, is_first=True)
            with dve.Fori(1, HEADS) as h:
                turn(h)
            index(HEADS - 1)
            dve.wait_ge(exp_made, 1)
            dve.tensor_reduce(total[:], e[:], AX.X, ALU.add).then_inc(softmax, 1)
            dve.wait_ge(softmax, 1)
            dve.reciprocal(total[:], total[:]).then_inc(softmax, 1)
            dve.wait_ge(softmax, 2)
            dve.tensor_tensor(sel[:, 0, :, :, :].rearrange("p t h k -> p (t h) k"), e[:].rearrange("p t h k -> p (t h) k"),
                              total[:].rearrange("p t h -> p (t h)").unsqueeze(2).to_broadcast([P, NT * HEADS, TOP]),
                              ALU.mult).then_inc(softmax, 1)


SLOTS = 8


class ExpertTiles:

    def __init__(self, ctx, nc, down_dram, up_dram):
        self.down_dram, self.up_dram = down_dram, up_dram
        self.down = ctx.enter_context(nc.sbuf_tensor("raw_down", [P, 2, KD, P], F32))
        self.up = ctx.enter_context(nc.sbuf_tensor("raw_up", [P, 2, D], F32))
        self.down_in = [ctx.enter_context(nc.semaphore(f"raw_down_in{s}")) for s in (0, 1)]
        self.up_in = [ctx.enter_context(nc.semaphore(f"raw_up_in{s}")) for s in (0, 1)]

    def load_down(self, sp, n, s):
        sp.dma_start(self.down[:, s, :, :], self.down_dram[bass.ds(n, 1), :, :, :].rearrange("a p k c -> (a p) k c")) \
            .then_inc(self.down_in[s], 16)

    def load_up(self, sp, n, s):
        sp.dma_start(self.up[:, s, :], self.up_dram[bass.ds(n, 1), :, :].rearrange("a p c -> (a p) c")) \
            .then_inc(self.up_in[s], 16)


def spread_gates(nc, sel, ident, iota_dram, gates_dram, odd, odd_stored, raw):
    STEP = 4
    DEEP = 4
    BLOCK = gates_dram.shape[3]
    BATCHES = TOK // STEP
    PER_BLOCK = BLOCK // STEP
    BLOCKS = TOK // BLOCK
    with ExitStack() as ctx:
        def sb(name, shape, dt=F32):
            return ctx.enter_context(nc.sbuf_tensor(f"sg_{name}", shape, dt))

        def sem(name):
            return ctx.enter_context(nc.semaphore(f"sg_{name}"))

        iota = sb("iota", [P, KEYS])
        selT = sb("selT", [P, 3, TOK])
        row = sb("row", [P, DEEP, STEP, KEYS])
        col = sb("col", [P, DEEP, STEP, KEYS])
        apart = sb("apart", [P, STEP, KEYS])
        one = sb("one", [P, 1])
        gated = sb("gated", [P, DEEP, STEP, KEYS])
        even = sb("even", [P, KEYS, BLOCK])
        full = [even[:], odd]
        ps = ctx.enter_context(nc.psum_tensor("sg_ps", [P, 3 + DEEP, TOK], F32))
        loaded = sem("loaded")
        turned = sem("turned")
        copied = sem("copied")
        passed = sem("passed")
        col_made, gated_made = (Items(sem(f"{x}_made"), DEEP) for x in ("col", "gated"))
        row_made = Items(sem("row_made"), DEEP - 1)
        last_made = Items(sem("last_made"), 1)
        squared = Items(sem("squared"), 1)
        used = Items(sem("used"), DEEP)
        filled = Items(sem("filled"), DEEP)
        stored = [sem("stored_even"), odd_stored]
        block = ctx.enter_context(nc.Block())
        slots = sel[:].rearrange("p a t h k -> p a t (h k)")
        iota_all = iota[:].unsqueeze(1).to_broadcast([P, STEP, KEYS])

        def of_batch(kind, n):
            return selT[:, kind, bass.ds(STEP * n, STEP)].unsqueeze(2).to_broadcast([P, STEP, KEYS])

        @block.sync
        def _(sp):
            sp.dma_start(iota[:], iota_dram).then_inc(loaded, 16)
            for t in range(BLOCKS):
                if t == BLOCKS - 1:
                    for s in (0, 1):
                        raw.load_down(sp, s, s)
                        raw.load_up(sp, s, s)
                sp.wait_ge(filled.sem, filled.after(PER_BLOCK * (t + 1) - 1))
                sp.dma_start(gates_dram[t], full[t % 2]).then_inc(stored[t % 2], 16)
            sp.wait_ge(stored[0], 16 * BLOCKS // 2)

        @block.tensor
        def _(pe):
            pe.wait_ge(loaded, 16)
            for a in range(3):
                for t in range(NT):
                    ins = pe.transpose(ps[:, a, P * t:P * t + P], slots[:, a, t, :], ident[:])
            ins.then_inc(turned, 1)
            used.open(pe)
            with pe.Fori(0, BATCHES // DEEP) as i:
                for b in range(DEEP):
                    n = DEEP * i + b
                    if b < DEEP - 1:
                        pe.wait_ge(row_made.sem, row_made.after((DEEP - 1) * i + b))
                    else:
                        pe.wait_ge(last_made.sem, last_made.after(i))
                    pe.wait_ge(gated_made.sem, gated_made.after(n))
                    pe.wait_ge(filled.sem, filled.after(n - DEEP))
                    for m in range(STEP):
                        ins = pe.matmul(ps[:, 3 + b, P * m:P * m + P], row[:, b, m, :], gated[:, b, m, :],
                                        start=True, stop=True)
                    ins.then_inc(used.sem, 1)

        @block.gpsimd
        def _(pool):
            gated_made.open(pool)
            pool.wait_ge(copied, 2)
            with pool.Fori(0, BATCHES // DEEP) as i:
                for b in range(DEEP):
                    n = DEEP * i + b
                    pool.wait_ge(col_made.sem, col_made.after(n))
                    pool.wait_ge(used.sem, used.after(n - DEEP))
                    pool.sem_inc(passed, 1)
                    pool.tensor_tensor(gated[:, b, :, :], col[:, b, :, :], of_batch(0, n), ALU.mult).then_inc(gated_made.sem, 1)

        @block.scalar
        def _(act):
            def last_row(i):
                for m in range(STEP):
                    ins = act.activation(apart[:, m, :], iota[:], ACT.Square,
                                         bias=selT[:, 1, bass.ds(STEP * (DEEP * i + DEEP - 1) + m, 1)], scale=-1.0)
                ins.then_inc(squared.sem, 1)
                act.wait_ge(squared.sem, squared.after(i))
                act.wait_ge(used.sem, used.after(DEEP * i - 1))
                act.activation(row[:, DEEP - 1, :, :], apart[:], ACT.Relu, bias=one[:],
                               scale=-2.0).then_inc(last_made.sem, 1)

            filled.open(act)
            last_made.open(act)
            squared.open(act)
            act.wait_ge(loaded, 16)
            act.wait_ge(copied, 2)
            for t in range(BLOCKS):
                if t >= 2:
                    act.wait_ge(stored[t % 2], 16 * (t // 2))
                with act.Fori(0, PER_BLOCK // DEEP) as i:
                    last_row(PER_BLOCK // DEEP * t + i)
                    for b in range(DEEP):
                        act.wait_ge(used.sem, used.after(PER_BLOCK * t + DEEP * i + b))
                        act.copy(full[t % 2][:, :, bass.ds(STEP * (DEEP * i + b), STEP)].rearrange("p c t -> p t c"),
                                 ps[:, 3 + b, :].rearrange("p (t c) -> p t c", t=STEP)).then_inc(filled.sem, 1)

        @block.vector
        def _(dve):
            row_made.open(dve)
            col_made.open(dve)
            dve.memset(one[:], 1.0).then_inc(copied, 1)
            dve.wait_ge(turned, 1)
            dve.tensor_copy(selT[:].rearrange("p a t -> p (a t)"), ps[:, 0:3, :].rearrange("p a t -> p (a t)")).then_inc(copied, 1)
            dve.wait_ge(loaded, 16)
            dve.wait_ge(copied, 2)
            with dve.Fori(0, BATCHES // DEEP) as i:
                for b in range(DEEP):
                    n = DEEP * i + b
                    if b < DEEP - 1:
                        dve.wait_ge(used.sem, used.after(n - DEEP))
                        dve.tensor_tensor(row[:, b, :, :], iota_all, of_batch(1, n), ALU.is_equal).then_inc(row_made.sem, 1)
                    dve.wait_ge(gated_made.sem, gated_made.after(n - DEEP))
                    dve.tensor_tensor(col[:, b, :, :], iota_all, of_batch(2, n), ALU.is_equal).then_inc(col_made.sem, 1)


def experts(nc, raw, gates_dram, gates_stored, early_dram, h_hi, h_lo, a_parts, acc, out_dram):
    G = SLOTS // 2
    TURNS = KEYS // SLOTS
    FROM = KEYS - early_dram.shape[0]
    EARLY_TURNS = -(-early_dram.shape[0] // SLOTS)

    def early(n):
        return isinstance(n, int) and n >= FROM

    UP = D // P
    BANKS = 4
    with ExitStack() as ctx:
        def sb(name, shape, dt=F32):
            return ctx.enter_context(nc.sbuf_tensor(f"ex_{name}", shape, dt))

        def sem(name):
            return ctx.enter_context(nc.semaphore(f"ex_{name}"))

        d_hi = sb("d_hi", [P, 2, KD, P], F32R)
        d_lo = sb("d_lo", [P, 2, KD, P], F32R)
        u_hi = sb("u_hi", [P, SLOTS, D], F32R)
        u_lo = sb("u_lo", [P, SLOTS, D], F32R)
        BLOCKS, _, _, BLOCK = gates_dram.shape
        gates = sb("gates", [P, 2, BLOCKS, G, BLOCK])
        gelu = sb("gelu", [P, 2, TOK])
        a = sb("a", [P, 2, TOK])
        a_hi, a_lo = a_parts[:, 0, :, :], a_parts[:, 1, :, :]
        ps = ctx.enter_context(nc.psum_tensor("ex_ps", [P, 8, TOK], F32))
        d_in, u_in = raw.down_in, raw.up_in
        g_in = [sem("g_in0"), sem("g_in1")]
        early_in = [sem("early_in0"), sem("early_in1")]
        d_hi_made, u_hi_made = Items(sem("d_hi_made"), 0), Items(sem("u_hi_made"), 0)
        d_lo_made, u_lo_made = Items(sem("d_lo_made"), 2), Items(sem("u_lo_made"), 2)
        down_done = Items(sem("down_done"), 2)
        gelu_made = Items(sem("gelu_made"), 2)
        a_made = Items(sem("a_made"), SLOTS)
        a_hi_made, a_lo_made = Items(sem("a_hi_made"), 0), Items(sem("a_lo_made"), 0)
        up_done = Items(sem("up_done"), 2 * UP)
        added = Items(sem("added"), BANKS)
        stored = sem("stored")
        block = ctx.enter_context(nc.Block())
        @block.sync
        def _(sp):
            def load_gates(half, n):
                sp.wait_ge(a_made.sem, a_made.after(n - SLOTS + G - 1))
                sp.dma_start(gates[:, half, :, :, :], gates_dram[:, :, bass.ds(n, G), :].rearrange("t p c k -> p t c k")).then_inc(g_in[half], 16)

            def turn(i, first=False):
                for q in range(SLOTS):
                    n, s = SLOTS * i + q, q % 2
                    if early(n):
                        sp.wait_ge(a_made.sem, a_made.after(n - 2))
                        sp.dma_start(gelu[:, s, :], early_dram[n - FROM]).then_inc(early_in[s], 16)
                    elif q >= 2 or not first:
                        sp.wait_ge(d_lo_made.sem, d_lo_made.after(n - 2))
                        raw.load_down(sp, n, s)
                    if q % G == 0 and not first:
                        load_gates(q // G, n)
                    if q >= 2 or not first:
                        sp.wait_ge(u_lo_made.sem, u_lo_made.after(n - 2))
                        raw.load_up(sp, n, s)
                    if first and q == 0:
                        sp.wait_ge(gates_stored, 16 * BLOCKS // 2)
                        for half in (0, 1):
                            load_gates(half, G * half)

            turn(0, first=True)
            with sp.Fori(1, TURNS - EARLY_TURNS) as i:
                turn(i)
            for i in range(TURNS - EARLY_TURNS, TURNS):
                turn(i)
            sp.wait_ge(added.sem, added.after(UP * KEYS // G - 1))
            sp.dma_start(out_dram, acc[:]).then_inc(stored, 16)
            sp.wait_ge(stored, 16)

        @block.gpsimd
        def _(pool):
            d_lo_made.open(pool)
            u_lo_made.open(pool)

            def turn(i):
                for q in range(SLOTS):
                    n, s = SLOTS * i + q, q % 2
                    if not early(n):
                        pool.wait_ge(d_hi_made.sem, d_hi_made.after(n))
                        pool.tensor_tensor(d_lo[:, s, :, :], raw.down[:, s, :, :], d_hi[:, s, :, :].bitcast(F32),
                                           ALU.subtract).then_inc(d_lo_made.sem, 1)
                    pool.wait_ge(u_hi_made.sem, u_hi_made.after(n))
                    pool.tensor_tensor(u_lo[:, q, :], raw.up[:, s, :], u_hi[:, q, :].bitcast(F32),
                                       ALU.subtract).then_inc(u_lo_made.sem, 1)

            with pool.Fori(0, TURNS - EARLY_TURNS) as i:
                turn(i)
            for i in range(TURNS - EARLY_TURNS, TURNS):
                turn(i)

        @block.scalar
        def _(act):
            def activate(n, q):
                if not early(n):
                    act.wait_ge(down_done.sem, down_done.after(n))
                    act.activation(gelu[:, q % 2, :], ps[:, q % 2, :], ACT.Gelu).then_inc(gelu_made.sem, 1)
                act.wait_ge(a_made.sem, a_made.after(n))
                act.copy(a_hi[:, q, :], a[:, q % 2, :]).then_inc(a_hi_made.sem, 1)

            def turn(i, first=False):
                for q in range(SLOTS):
                    n, s = SLOTS * i + q, q % 2
                    if not early(n):
                        act.wait_ge(d_in[s], 16 * (G * i + q // 2 + 1))
                        act.wait_ge(down_done.sem, down_done.after(n - 2))
                        act.copy(d_hi[:, s, :, :], raw.down[:, s, :, :]).then_inc(d_hi_made.sem, 1)
                    if q or not first:
                        activate(n - 1, (q - 1) % SLOTS)
                    act.wait_ge(u_in[s], 16 * (G * i + q // 2 + 1))
                    if q % G == 0:
                        act.wait_ge(up_done.sem, up_done.after(UP * (2 * i + q // G - 1) - 1))
                    act.copy(u_hi[:, q, :], raw.up[:, s, :]).then_inc(u_hi_made.sem, 1)

            gelu_made.open(act)
            turn(0, first=True)
            with act.Fori(1, TURNS - EARLY_TURNS) as i:
                turn(i)
            for i in range(TURNS - EARLY_TURNS, TURNS):
                turn(i)
            activate(KEYS - 1, SLOTS - 1)

        @block.tensor
        def _(pe):
            def up(g, half, j):
                if j == 0:
                    pe.wait_ge(a_lo_made.sem, a_lo_made.after(G * g + G - 1))
                    pe.wait_ge(u_lo_made.sem, u_lo_made.after(G * g + G - 1))
                for c in (2 * j, 2 * j + 1):
                    pe.wait_ge(added.sem, added.after(UP * g + c - BANKS))
                    for t in range(G):
                        s = G * half + t
                        ins = three_passes(pe, ps[:, 2 + c % BANKS, :], u_hi[:, s, P * c:P * c + P],
                                           u_lo[:, s, P * c:P * c + P], a_hi[:, s, :], a_lo[:, s, :],
                                           t == 0, t == G - 1)
                    ins.then_inc(up_done.sem, 1)

            def down(n, s):
                pe.wait_ge(gelu_made.sem, gelu_made.after(n - 2))
                pe.wait_ge(d_lo_made.sem, d_lo_made.after(n))
                for k in range(KD):
                    ins = three_passes(pe, ps[:, s, :], d_hi[:, s, k, :], d_lo[:, s, k, :], h_hi[:, k, :],
                                       h_lo[:, k, :], k == 0, k == KD - 1)
                ins.then_inc(down_done.sem, 1)

            def turn(i, first=False):
                for q in range(SLOTS):
                    if not early(SLOTS * i + q):
                        down(SLOTS * i + q, q % 2)
                    if q >= G or not first:
                        up(2 * i + q // G - 1, 1 - q // G, q % G)

            down_done.open(pe)
            up_done.open(pe)
            turn(0, first=True)
            with pe.Fori(1, TURNS - EARLY_TURNS) as i:
                turn(i)
            for i in range(TURNS - EARLY_TURNS, TURNS):
                turn(i)
            for j in range(G):
                up(2 * TURNS - 1, 1, j)

        @block.vector
        def _(dve):
            def sum_up(g, j):
                for c in (2 * j, 2 * j + 1):
                    dve.wait_ge(up_done.sem, up_done.after(UP * g + c))
                    dve.tensor_tensor(acc[:, c, :], acc[:, c, :], ps[:, 2 + c % BANKS, :],
                                      ALU.add).then_inc(added.sem, 1)

            def turn(i, first=False):
                for q in range(SLOTS):
                    n = SLOTS * i + q
                    if q % G == 0:
                        dve.wait_ge(g_in[q // G], 16 * (i + 1))
                        dve.wait_ge(up_done.sem, up_done.after(UP * (2 * i + q // G - 1) - 1))
                    if early(n):
                        dve.wait_ge(early_in[q % 2], 16 * ((n - FROM) // 2 + 1))
                    else:
                        dve.wait_ge(gelu_made.sem, gelu_made.after(n))
                    dve.tensor_tensor(a[:, q % 2, :].rearrange("p (t k) -> p t k", t=BLOCKS), gates[:, q // G, :, q % G, :],
                                      gelu[:, q % 2, :].rearrange("p (t k) -> p t k", t=BLOCKS),
                                      ALU.mult).then_inc(a_made.sem, 1)
                    dve.wait_ge(a_hi_made.sem, a_hi_made.after(n))
                    dve.tensor_tensor(a_lo[:, q, :], a[:, q % 2, :], a_hi[:, q, :].bitcast(F32),
                                      ALU.subtract).then_inc(a_lo_made.sem, 1)
                    if q >= G or not first:
                        sum_up(2 * i + q // G - 1, q % G)

            a_made.open(dve)
            added.open(dve)
            turn(0, first=True)
            with dve.Fori(1, TURNS - EARLY_TURNS) as i:
                turn(i)
            for i in range(TURNS - EARLY_TURNS, TURNS):
                turn(i)
            for j in range(G):
                sum_up(2 * TURNS - 1, j)


def build(nc, dram, out):
    with ExitStack() as ctx:
        def sb(name, shape, dt=F32):
            return ctx.enter_context(nc.sbuf_tensor(name, shape, dt))

        xT = sb("xT", [P, KD, TOK])
        ident = sb("ident", [P, P])
        ones = sb("ones", [P, P])
        halves = sb("halves", [P, P])
        h_hi = sb("h_hi", [P, KD, TOK], F32R)
        h_lo = sb("h_lo", [P, KD, TOK], F32R)
        cols = sb("cols", [P, 4, NT, HEADS])
        rows_dram = nc.dram_tensor("rows_dram", [HEADS, 3, TOK], F32, kind="Internal").ap()
        gates_dram = nc.dram_tensor("gates_dram", [NCH, KEYS, KEYS, TOK // NCH], F32, kind="Internal").ap()
        gates_stored = ctx.enter_context(nc.semaphore("gates_stored"))
        early_dram = nc.dram_tensor("early_dram", [2 * HEADS + 4, P, TOK], F32, kind="Internal").ap()

        with nc.sbuf_tensor("o_b", [P, HEADS, TOK], F32) as o_b:
            with ExitStack() as weights:
                w_b = Weights(weights, nc, "mb", dram["w_b"], [KD] * 4)
                with nc.sbuf_tensor("h_full", [P, KD, TOK], F32) as h_full:
                    norm_and_split(nc, "n1", xT, dram["norm_mix"], ones, h_full, h_hi, h_lo,
                                   x_dram=dram["xT"], load=[(ident[:], dram["ident"]), (ones[:], dram["ones"]),
                                         (halves[:], dram["halves"])])
                    decay_rows(nc, h_full, dram["w_ab"], dram["dt_bias"], dram["a_log"], ident, dram["resets"],
                               rows_dram, cols, w_b)
                mixer_b(nc, h_hi, h_lo, w_b, dram["conv"], dram["b_norm"], rows_dram, cols, ident, ones,
                        dram["masks"], o_b)
            with nc.sbuf_tensor("o_a", [P, A_W // P, TOK], F32) as o_a:
                mixer_a(nc, h_hi, h_lo, dram["w_a"], dram["bias"], dram["a_gains"], ident, halves, o_a)
                with (nc.sbuf_tensor("mixed_hi", [P, KD, TOK], F32R) as mixed_hi,
                      nc.sbuf_tensor("mixed_lo", [P, KD, TOK], F32R) as mixed_lo):
                    merge(nc, "mg", dram["w_merge"], [KD, KD, A_W // P, KD], h_hi, h_lo, o_a, o_b,
                          dram["b_merge"], mixed_hi, mixed_lo)
                    project_out(nc, dram["w_out"], mixed_hi, mixed_lo, xT)
        first_early = dram["down"].shape[0] - early_dram.shape[0]
        raw = ExpertTiles(ctx, nc, dram["down"], dram["up"])
        a_parts = sb("a_parts", [P, 2, SLOTS, TOK], F32R)
        odd = a_parts[:].bitcast(F32).rearrange("p n s (c t) -> p (n s c) t", t=gates_dram.shape[3])
        with nc.sbuf_tensor("sel", [P, 3, NT, HEADS, TOP], F32) as sel:
            with ExitStack() as weights:
                w_query = Weights(weights, nc, "ce", dram["w_query"], [KD, KD])
                w_down = Weights(weights, nc, "ce_down",
                                 lambda d, m: dram["down"][bass.ds(2 * d + (first_early + m), 1), :, :, :], [KD, KD])
                with nc.sbuf_tensor("hf_full", [P, KD, TOK], F32) as h_full:
                    norm_and_split(nc, "n2", xT, dram["norm_ffn"], ones, h_full, h_hi, h_lo, ahead=[w_query, w_down])
                choose_experts(nc, w_query, w_down, dram["keys"], dram["iota16"], h_hi, h_lo, sel, early_dram)
            spread_gates(nc, sel, ident, dram["iota128"], gates_dram, odd, gates_stored, raw)
        experts(nc, raw, gates_dram, gates_stored, early_dram, h_hi, h_lo, a_parts, xT, out)


A_W, B_W = 512, 1024
OFF_B = 3 * A_W
OFF_AB = OFF_B + 3 * B_W
OFF_G = OFF_AB + 16
OFF_M = OFF_G + B_W


def layout(inputs):
    import numpy as np

    def tiles(w):
        k = w.shape[0] // P
        return np.ascontiguousarray(w.reshape(k, P, w.shape[1] // P, P).transpose(2, 1, 0, 3))

    a = {k: np.asarray(v) for k, v in inputs.items()}
    w_in = a["w_in"][0]
    qkv = [tiles(w_in[:, OFF_B + i * B_W:OFF_B + (i + 1) * B_W]) for i in range(3)]
    gate = tiles(w_in[:, OFF_G:OFF_G + B_W])
    out = {
        "xT": a["x"][0].T.reshape(KD, P, TOK).transpose(1, 0, 2),
        "ident": np.eye(P, dtype=np.float32),
        "ones": np.ones((P, P), np.float32),
        "norm_mix": a["norm_mix_w"][0].reshape(KD, P).T,
        "w_ab": w_in[:, OFF_AB:OFF_AB + 16].reshape(KD, P, 16).transpose(1, 0, 2),
        "dt_bias": a["b_dt_bias"][0][:, None],
        "a_log": a["b_a_log"][0][:, None],
        "resets": np.tile((np.arange(TOK) % CH != 0).astype(np.float32), (HEADS, 1)),
        "w_b": np.concatenate(qkv + [gate], 2),
        "conv": a["b_conv_w"][0].reshape(CONV, 3, HEADS, P).transpose(3, 2, 1, 0),
        "b_norm": a["b_norm_w"][0][:, None],
    }
    i, j = np.arange(CH)[:, None], np.arange(CH)[None, :]
    levels = [((i // (2 * s) == j // (2 * s)) & (i // s > j // s)).astype(np.float32) for s in (1, 2, 4, 8, 16, 32)]
    levels.append(np.where(j >= i, 0.0, NEG).astype(np.float32))
    rel = a["a_rel_bias"][0]
    reach = TOK - P
    longer = np.pad(rel, ((0, 0), (0, TOK - rel.shape[1] + P)), mode="edge")
    rev = longer[:, ::-1]
    last = longer.shape[1] - 1
    out["bias"] = np.stack([rev[:, last - (r + reach + P):last - (r + reach + P) + TOK] for r in range(P)], 1) \
        .reshape(HEADS // 2, 2, P, TOK).transpose(0, 2, 1, 3)
    out["a_gains"] = np.stack([np.tile(a["a_q_norm_w"][0], 2), np.tile(a["a_k_norm_w"][0], 2)], 1)
    out["halves"] = np.kron(np.eye(2, dtype=np.float32), np.ones((64, 64), np.float32))
    out["w_a"] = np.concatenate([tiles(w_in[:, A_W * n:A_W * n + A_W]) for n in range(3)], 2)
    merge_w = [tiles(w_in[:, OFF_M + D * n:OFF_M + D * n + D]) for n in range(2)]
    out["w_merge"] = np.concatenate(merge_w + [tiles(a["w_proj_a"][0]), tiles(a["w_proj_b"][0])], 2)
    out["b_merge"] = a["b_merge"][0].reshape(2, KD, P).transpose(2, 0, 1)
    pair = lambda w: np.concatenate([w[0::2], w[1::2]], 2)
    out["w_out"] = pair(tiles(a["w_out"][0]))
    out["norm_ffn"] = a["norm_ffn_w"][0].reshape(KD, P).T
    out["w_query"] = pair(tiles(a["peer_w_query"][0]))
    out["keys"] = np.stack([a["peer_keys_1"][0], a["peer_keys_2"][0]], 0).transpose(1, 3, 0, 2)
    out["iota16"] = np.tile(np.arange(TOP, dtype=np.float32), (P, 1))
    out["iota128"] = np.tile(np.arange(KEYS, dtype=np.float32), (P, 1))
    out["down"] = a["peer_down"][0].reshape(KEYS, KEYS, KD, P).transpose(1, 3, 2, 0)
    out["up"] = a["peer_up"][0].reshape(KEYS, KEYS, D).transpose(1, 0, 2)
    levels.append(np.eye(CH, dtype=np.float32))
    out["masks"] = np.tile(np.stack(levels, 1), (2, 1, 1))
    return {k: np.ascontiguousarray(v) for k, v in out.items()}


def kernel(**inputs):
    import numpy as np
    import concourse.bacc as bacc
    from concourse.bass_utils import run_bass_kernel_spmd

    arrays = layout(inputs)
    nc = bacc.Bacc("TRN2", target_bir_lowering=False, num_devices=1)
    dram = {k: nc.dram_tensor(f"in_{k}", v.shape, mybir.dt.from_np(v.dtype), kind="ExternalInput").ap()
            for k, v in arrays.items()}
    out = nc.dram_tensor("out_y", [P, KD, TOK], F32, kind="ExternalOutput").ap()
    build(nc, dram, out)
    r = run_bass_kernel_spmd(nc, [{f"in_{k}": v for k, v in arrays.items()}], core_ids=[0])
    y = r.results[0]["out_y"]
    return np.ascontiguousarray(y.transpose(1, 0, 2).reshape(D, TOK).T)[None]
```
